# Optimizing a Trainium2 kernel written in Bass

```python
import jax
import jax.numpy as jnp
from jax import lax
import numpy as np

D_MODEL = 1024
BATCH = 1
SEQ = 256
DEPTH = 2

GRID_W = 64
RMS_EPS = 1e-6

NA_HEADS = 8
NA_HEAD_DIM = 64
NA_WIDTH = NA_HEADS * NA_HEAD_DIM
NA_KR = 8
NA_KC = 16
NA_QC = 16
NA_KCB = 2 * NA_QC
NA_NCB = GRID_W // NA_QC

FN_GROUPS = 8
FN_GROUP_DIM = 64
FN_WIDTH = FN_GROUPS * FN_GROUP_DIM

EVEN_IN = 3 * NA_WIDTH + FN_WIDTH
EVEN_MIX = NA_WIDTH + FN_WIDTH

ML_HEADS = 8
ML_QK_DIM = 64
ML_V_DIM = 128
ML_QK_WIDTH = ML_HEADS * ML_QK_DIM
ML_WIDTH = ML_HEADS * ML_V_DIM
ML_CHUNK = 64
ODD_IN = 2 * ML_QK_WIDTH + 2 * ML_WIDTH + 4 * ML_HEADS

MOE_GROUPS = 4
MOE_EXPERTS_PER_GROUP = 8
MOE_EXPERTS = MOE_GROUPS * MOE_EXPERTS_PER_GROUP
MOE_TOP_K = 2
MOE_FF = 512
MOE_BLOCK = 256

N_EVEN = (DEPTH + 1) // 2
N_ODD = DEPTH // 2

kernel_name = 'hybrid_natten_fnet_mlstm_hmoe_encoder'

def rms_norm(x, gain):
    xf = x.astype(jnp.float32)
    y = xf * lax.rsqrt(jnp.mean(xf * xf, axis=-1, keepdims=True) + RMS_EPS)
    return (y * gain.astype(jnp.float32)).astype(x.dtype)

def neighbourhood_attention(q, k, v, rel_bias):
    B, S, H, dh = q.shape
    rows = S // GRID_W
    kr = min(NA_KR, rows)
    r = jnp.arange(rows)
    row_idx = jnp.clip(r - kr // 2, 0, rows - kr)[:, None] + jnp.arange(kr)[None, :]
    qcol = jnp.arange(GRID_W).reshape(NA_NCB, NA_QC)
    blk_start = jnp.clip(qcol[:, 0] - NA_KC // 2, 0, GRID_W - NA_KCB)
    col_idx = blk_start[:, None] + jnp.arange(NA_KCB)[None, :]
    win_start = jnp.clip(qcol - NA_KC // 2, 0, GRID_W - NA_KC)
    kcol = col_idx[:, None, :]
    col_valid = (kcol >= win_start[..., None]) & (kcol < win_start[..., None] + NA_KC)
    dr = row_idx - r[:, None] + (NA_KR - 1)
    dc = jnp.clip(kcol - qcol[..., None] + (NA_KC - 1), 0, 2 * NA_KC - 2)
    bias = rel_bias.astype(jnp.float32)[:, dr[:, None, None, :, None], dc[None, :, :, None, :]]

    def gather_block(t):
        tg = t.reshape(B, rows, GRID_W, H, dh)
        return jnp.take(jnp.take(tg, row_idx, axis=1), col_idx, axis=3)

    kg = gather_block(k)
    vg = gather_block(v)
    qg = q.reshape(B, rows, NA_NCB, NA_QC, H, dh)
    s = jnp.einsum('brjqhd,brajchd->bhrjqac', qg, kg).astype(jnp.float32) * (dh ** -0.5) + bias[None]
    s = jnp.where(col_valid[:, :, None, :], s, -jnp.inf)
    p = jax.nn.softmax(s.reshape(*s.shape[:-2], kr * NA_KCB), axis=-1).reshape(s.shape)
    o = jnp.einsum('bhrjqac,brajchd->brjqhd', p.astype(v.dtype), vg)
    return o.reshape(B, S, H * dh)

def fourier_mix(u):
    B, S, _ = u.shape
    uf = u.astype(jnp.float32).reshape(B, S, FN_GROUPS, FN_GROUP_DIM)
    z = jnp.fft.fft2(uf, axes=(1, 3), norm='ortho').real
    return z.reshape(B, S, FN_WIDTH).astype(u.dtype)

def even_mixer(xn, w_in, q_gain, k_gain, rel_bias, w_out):
    B, S, _ = xn.shape
    u = xn @ w_in
    q, k, v, ub = jnp.split(u, [NA_WIDTH, 2 * NA_WIDTH, 3 * NA_WIDTH], axis=-1)
    heads = lambda t: t.reshape(B, S, NA_HEADS, NA_HEAD_DIM)
    q = rms_norm(heads(q), q_gain)
    k = rms_norm(heads(k), k_gain)
    a = neighbourhood_attention(q, k, heads(v), rel_bias)
    b = fourier_mix(ub)
    return jnp.concatenate([a, b], axis=-1) @ w_out

def mlstm_chunkwise(q, k, v, log_i, log_f):
    B, H, S, dk = q.shape
    dv = v.shape[-1]
    L = ML_CHUNK
    nc = S // L
    q = q.reshape(B, H, nc, L, dk)
    k = k.reshape(B, H, nc, L, dk)
    v = v.reshape(B, H, nc, L, dv)
    log_i = log_i.reshape(B, H, nc, L)
    b = jnp.cumsum(log_f.reshape(B, H, nc, L), axis=-1)
    g = b[..., -1]
    w_log = g[..., None] - b + log_i
    m_loc = jnp.max(w_log, axis=-1)
    w = jnp.exp(w_log - m_loc[..., None])
    dC = jnp.einsum('bhcl,bhcld,bhcle->bhcde', w, k, v)
    dn = jnp.einsum('bhcl,bhcld->bhcd', w, k)

    def step(carry, xs):
        C, n, m = carry
        g_c, dC_c, dn_c, ml_c = xs
        m_new = jnp.maximum(g_c + m, ml_c)
        a = jnp.exp(g_c + m - m_new)
        c = jnp.exp(ml_c - m_new)
        C_new = a[..., None, None] * C + c[..., None, None] * dC_c
        n_new = a[..., None] * n + c[..., None] * dn_c
        return (C_new, n_new, m_new), (C, n, m)

    init = (jnp.zeros((B, H, dk, dv), jnp.float32), jnp.zeros((B, H, dk), jnp.float32),
            jnp.zeros((B, H), jnp.float32))
    xs = (jnp.moveaxis(g, 2, 0), jnp.moveaxis(dC, 2, 0), jnp.moveaxis(dn, 2, 0), jnp.moveaxis(m_loc, 2, 0))
    _, (C_prev, n_prev, m_prev) = lax.scan(step, init, xs)
    C_prev = jnp.moveaxis(C_prev, 0, 2)
    n_prev = jnp.moveaxis(n_prev, 0, 2)
    m_prev = jnp.moveaxis(m_prev, 0, 2)

    tril = jnp.tril(jnp.ones((L, L), dtype=bool))
    d_log = jnp.where(tril, b[..., :, None] - b[..., None, :] + log_i[..., None, :], -jnp.inf)
    inter_log = b + m_prev[..., None]
    m_out = jnp.maximum(inter_log, jnp.max(d_log, axis=-1))
    d_w = jnp.exp(d_log - m_out[..., None])
    inter_w = jnp.exp(inter_log - m_out)
    s = jnp.einsum('bhcld,bhcsd->bhcls', q, k) * d_w
    num = jnp.einsum('bhcls,bhcse->bhcle', s, v) + inter_w[..., None] * jnp.einsum('bhcld,bhcde->bhcle', q, C_prev)
    den = jnp.sum(s, axis=-1) + inter_w * jnp.einsum('bhcld,bhcd->bhcl', q, n_prev)
    h = num / jnp.maximum(jnp.abs(den), jnp.exp(-m_out))[..., None]
    return h.reshape(B, H, S, dv)

def odd_mixer(xn, w_in, gate_bias, h_gain, w_out):
    B, S, _ = xn.shape
    u = xn @ w_in
    q, k, v, o, gates = jnp.split(
        u, [ML_QK_WIDTH, 2 * ML_QK_WIDTH, 2 * ML_QK_WIDTH + ML_WIDTH, 2 * ML_QK_WIDTH + 2 * ML_WIDTH], axis=-1)
    to_heads = lambda t, d: t.reshape(B, S, ML_HEADS, d).transpose(0, 2, 1, 3).astype(jnp.float32)
    q = to_heads(q, ML_QK_DIM)
    k = to_heads(k, ML_QK_DIM) * (ML_QK_DIM ** -0.5)
    v = to_heads(v, ML_V_DIM)
    gates = (gates.astype(jnp.float32) + gate_bias.astype(jnp.float32)).reshape(B, S, 4, ML_HEADS)
    gates = gates.transpose(2, 0, 3, 1)
    i_fw, f_fw, i_bw, f_bw = gates[0], gates[1], gates[2], gates[3]
    h_fw = mlstm_chunkwise(q, k, v, i_fw, jax.nn.log_sigmoid(f_fw))
    rev = lambda t: jnp.flip(t, axis=2)
    h_bw = rev(mlstm_chunkwise(rev(q), rev(k), rev(v), rev(i_bw), jax.nn.log_sigmoid(rev(f_bw))))
    h = (h_fw + h_bw).transpose(0, 2, 1, 3)
    h = rms_norm(h, h_gain.reshape(ML_HEADS, ML_V_DIM)).reshape(B, S, ML_WIDTH)
    h = h * jax.nn.sigmoid(o.astype(jnp.float32))
    return h.astype(xn.dtype) @ w_out

def hier_route(x2, w_rg, b_rg, w_re, b_re):
    T = x2.shape[0]
    pg = jax.nn.softmax((x2 @ w_rg).astype(jnp.float32) + b_rg.astype(jnp.float32), axis=-1)
    p_top, g_sel = lax.top_k(pg, 1)
    le = ((x2 @ w_re).astype(jnp.float32) + b_re.astype(jnp.float32)).reshape(T, MOE_GROUPS, MOE_EXPERTS_PER_GROUP)
    le_sel = le[jnp.arange(T), g_sel[:, 0]]
    pe = jax.nn.softmax(le_sel, axis=-1)
    v2, i2 = lax.top_k(pe, MOE_TOP_K)
    gate = p_top * v2 / jnp.sum(v2, axis=-1, keepdims=True)
    eid = g_sel * MOE_EXPERTS_PER_GROUP + i2
    return eid.astype(jnp.int32), gate

def expert_mix(x2, eid, gate, w_gate, w_up, w_down):
    T, D = x2.shape
    A = T * MOE_TOP_K
    n_blocks = (A + MOE_EXPERTS * (MOE_BLOCK - 1) + MOE_BLOCK - 1) // MOE_BLOCK
    P = n_blocks * MOE_BLOCK
    flat_e = eid.reshape(-1)
    flat_tok = jnp.broadcast_to(jnp.arange(T, dtype=jnp.int32)[:, None], (T, MOE_TOP_K)).reshape(-1)
    flat_g = gate.reshape(-1)
    order = jnp.argsort(flat_e)
    se, stok, sg = flat_e[order], flat_tok[order], flat_g[order]
    counts = jax.ops.segment_sum(jnp.ones((A,), jnp.int32), flat_e, num_segments=MOE_EXPERTS)
    starts = jnp.cumsum(counts) - counts
    padded = (counts + MOE_BLOCK - 1) // MOE_BLOCK * MOE_BLOCK
    pend = jnp.cumsum(padded)
    pstarts = pend - padded
    dest = pstarts[se] + (jnp.arange(A, dtype=jnp.int32) - starts[se])
    row_tok = jnp.full((P,), T, jnp.int32).at[dest].set(stok)
    row_gate = jnp.zeros((P,), jnp.float32).at[dest].set(sg)
    block_start = jnp.arange(n_blocks, dtype=jnp.int32) * MOE_BLOCK
    block_e = jnp.minimum(jnp.searchsorted(pend, block_start, side='right'), MOE_EXPERTS - 1)
    x_pad = jnp.concatenate([x2, jnp.zeros((1, D), x2.dtype)], axis=0)

    def block_fn(args):
        rows, e = args
        xb = x_pad[rows]
        h = jax.nn.silu(xb @ w_gate[e]) * (xb @ w_up[e])
        return h @ w_down[e]

    y_rows = lax.map(block_fn, (row_tok.reshape(n_blocks, MOE_BLOCK), block_e))
    y = jnp.zeros((T + 1, D), jnp.float32).at[row_tok].add(
        y_rows.reshape(P, D).astype(jnp.float32) * row_gate[:, None])
    return y[:T].astype(x2.dtype)

def hier_moe(xn, w_rg, b_rg, w_re, b_re, w_gate, w_up, w_down):
    B, S, D = xn.shape
    x2 = xn.reshape(B * S, D)
    eid, gate = hier_route(x2, w_rg, b_rg, w_re, b_re)
    return expert_mix(x2, eid, gate, w_gate, w_up, w_down).reshape(B, S, D)

def setup_inputs(seed: int = 0) -> dict:
    key = jax.random.key(seed)
    ks = jax.random.split(key, 21)
    nrm = lambda k, shape, scale: scale * jax.random.normal(k, shape, jnp.float32)
    gate_base = jnp.asarray([0.0, 3.0, 0.0, 3.0], jnp.float32)[None, :, None]
    od_gate_bias = (gate_base + nrm(ks[9], (N_ODD, 4, ML_HEADS), 0.1)).reshape(N_ODD, 4 * ML_HEADS)
    return {
        'x': nrm(ks[0], (BATCH, SEQ, D_MODEL), 1.0),
        'ev_norm': 1.0 + nrm(ks[1], (N_EVEN, D_MODEL), 0.05),
        'ev_w_in': nrm(ks[2], (N_EVEN, D_MODEL, EVEN_IN), D_MODEL ** -0.5),
        'ev_q_gain': 1.0 + nrm(ks[3], (N_EVEN, NA_HEAD_DIM), 0.05),
        'ev_k_gain': 1.0 + nrm(ks[4], (N_EVEN, NA_HEAD_DIM), 0.05),
        'ev_rel_bias': nrm(ks[5], (N_EVEN, NA_HEADS, 2 * NA_KR - 1, 2 * NA_KC - 1), 0.1),
        'ev_w_out': nrm(ks[6], (N_EVEN, EVEN_MIX, D_MODEL), EVEN_MIX ** -0.5),
        'od_norm': 1.0 + nrm(ks[7], (N_ODD, D_MODEL), 0.05),
        'od_w_in': nrm(ks[8], (N_ODD, D_MODEL, ODD_IN), D_MODEL ** -0.5),
        'od_gate_bias': od_gate_bias,
        'od_h_gain': 1.0 + nrm(ks[10], (N_ODD, ML_WIDTH), 0.05),
        'od_w_out': nrm(ks[11], (N_ODD, ML_WIDTH, D_MODEL), ML_WIDTH ** -0.5),
        'moe_norm': 1.0 + nrm(ks[12], (DEPTH, D_MODEL), 0.05),
        'moe_w_rg': nrm(ks[13], (DEPTH, D_MODEL, MOE_GROUPS), D_MODEL ** -0.5),
        'moe_b_rg': nrm(ks[14], (DEPTH, MOE_GROUPS), 0.01),
        'moe_w_re': nrm(ks[15], (DEPTH, D_MODEL, MOE_EXPERTS), D_MODEL ** -0.5),
        'moe_b_re': nrm(ks[16], (DEPTH, MOE_EXPERTS), 0.01),
        'moe_w_gate': nrm(ks[17], (DEPTH, MOE_EXPERTS, D_MODEL, MOE_FF), D_MODEL ** -0.5),
        'moe_w_up': nrm(ks[18], (DEPTH, MOE_EXPERTS, D_MODEL, MOE_FF), D_MODEL ** -0.5),
        'moe_w_down': nrm(ks[19], (DEPTH, MOE_EXPERTS, MOE_FF, D_MODEL), MOE_FF ** -0.5),
    }

def reference(x, ev_norm, ev_w_in, ev_q_gain, ev_k_gain, ev_rel_bias, ev_w_out,
              od_norm, od_w_in, od_gate_bias, od_h_gain, od_w_out,
              moe_norm, moe_w_rg, moe_b_rg, moe_w_re, moe_b_re, moe_w_gate, moe_w_up, moe_w_down):
    for layer in range(DEPTH):
        i = layer // 2
        if layer % 2 == 0:
            x = x + even_mixer(rms_norm(x, ev_norm[i]), ev_w_in[i], ev_q_gain[i], ev_k_gain[i],
                               ev_rel_bias[i], ev_w_out[i])
        else:
            x = x + odd_mixer(rms_norm(x, od_norm[i]), od_w_in[i], od_gate_bias[i], od_h_gain[i], od_w_out[i])
        x = x + hier_moe(rms_norm(x, moe_norm[layer]), moe_w_rg[layer], moe_b_rg[layer], moe_w_re[layer],
                         moe_b_re[layer], moe_w_gate[layer], moe_w_up[layer], moe_w_down[layer])
    return x


_drawn_inputs = setup_inputs


def setup_inputs(seed=0):
    import zlib

    import numpy as np

    out = dict(_drawn_inputs(seed))
    spreads = {}
    factors = {}
    for name, (base, spread) in spreads.items():
        noise = np.random.default_rng([zlib.crc32(name.encode()), seed]).standard_normal(out[name].shape)
        drawn = base * np.exp(spread * noise) if base else spread * noise
        out[name] = jnp.asarray(drawn.astype(out[name].dtype))
    for name, factor in factors.items():
        out[name] = (out[name] * factor).astype(out[name].dtype)
    return out
```

```python
from contextlib import ExitStack

import numpy as np

import concourse.bass as bass
from concourse import mybir

P = 128
F32 = mybir.dt.float32
I32 = mybir.dt.int32
ALU = mybir.AluOpType
ACT = mybir.ActivationFunctionType
AX = mybir.AxisListType.X
ENG = mybir.EngineType

D = 1024
T = 256
TT = T // P
DC = D // P
EPS = 1e-6
GRID_W = 64

HEADS = 8
HP = HEADS // 2
NA_DH = 64
NA_WIN = 16
REL_R, REL_C = 15, 31
REL_SIZE = REL_R * REL_C
BIAS_ROWS = 6
ML_DV = 128
VE = ML_DV + 1

GROUPS, PER_GROUP, FF = 4, 8, 512
EXPERTS = GROUPS * PER_GROUP
ROUTE = GROUPS + EXPERTS
QUAD = 4
QUADS = EXPERTS // QUAD
CAP = P // QUAD
MAX_ROUNDS = T // CAP
GU_PIECES = D // P
DN_PIECES = FF // P
ITEM = GU_PIECES + DN_PIECES

SLOTS = 6
SLOT = 4096
NEG = -1e30

C_IDENT = 0
C_TRI = C_IDENT + P
C_ONES = C_TRI + P
C_SLOTID = C_ONES + P
C_RANKW = C_SLOTID + T + CAP
C_THR = C_RANKW + EXPERTS
C_COMMON = C_THR + MAX_ROUNDS
C0_REV = 0
C0_SEQ = C0_REV + P
C0_CH = C0_SEQ + TT * 2 * T
C0_MASK = C0_CH + 2 * P
C0_SIZE = C0_MASK + GRID_W
C1_MASK = 0
C1_SEL = C1_MASK + 3 * T
C1_SIZE = C1_SEL + HEADS * P
C_LAYER = max(C0_SIZE, C1_SIZE)


def shape_constants():
    common = np.zeros((P, C_COMMON), np.float32)
    p = np.arange(P)
    common[:, C_IDENT:C_TRI] = np.eye(P)
    common[:, C_TRI:C_ONES] = p[:, None] < p[None, :]
    common[:, C_ONES:C_SLOTID] = 1.0
    common[:, C_SLOTID:C_RANKW] = np.arange(T + CAP)
    common[:, C_RANKW:C_THR] = EXPERTS - np.arange(EXPERTS)
    common[:, C_THR:C_COMMON] = CAP * np.arange(1, MAX_ROUNDS + 1) + 0.5

    l0 = np.zeros((P, C_LAYER), np.float32)
    l0[p, C0_REV + (p // GRID_W) * GRID_W + GRID_W - 1 - p % GRID_W] = 1.0
    t = np.arange(T)
    ang = 2 * np.pi * ((t[:, None] * t[None, :]) % T) / T
    norm = 1.0 / np.sqrt(T * 64)
    seq = np.concatenate([np.cos(ang), np.sin(ang)], axis=1) * norm
    l0[:, C0_SEQ:C0_CH] = seq.reshape(TT, P, 2 * T).transpose(1, 0, 2).reshape(P, -1)
    c = np.arange(64)
    ang = 2 * np.pi * ((c[:, None] * c[None, :]) % 64) / 64
    for j, m in enumerate((np.cos(ang), -np.sin(ang))):
        for g in range(2):
            o = C0_CH + j * P + 64 * g
            l0[64 * g:64 * g + 64, o:o + 64] = m
    qc = GRID_W - 1 - p % GRID_W
    lo = np.clip(qc - NA_WIN // 2, 0, GRID_W - NA_WIN)
    kc = np.arange(GRID_W)
    ok = (kc[None, :] >= lo[:, None]) & (kc[None, :] < lo[:, None] + NA_WIN)
    l0[:, C0_MASK:C0_SIZE] = np.where(ok, 0.0, NEG)

    l1 = np.zeros((P, C_LAYER), np.float32)
    s, tt = p[:, None], t[None, :]
    fw0 = np.where(tt >= s, 0.0, NEG)
    bw1 = np.where(tt <= s + P, 0.0, NEG)
    bw0 = np.where(tt[:, :P] <= s, 0.0, NEG)
    fw1 = np.where(tt[:, :P] >= s, 0.0, NEG)
    l1[:, C1_MASK:C1_SEL] = np.concatenate([fw0, bw1, bw0, fw1], axis=1)
    for h in range(HEADS):
        l1[h, C1_SEL + h * P:C1_SEL + (h + 1) * P] = 1.0
    return common, l0, l1


def build(nc, a, out):
    ctx = ExitStack()
    with ctx:
        def sb(name, width, dt=F32):
            return ctx.enter_context(nc.sbuf_tensor(name, [P, width], dt))

        def sem(name):
            return ctx.enter_context(nc.semaphore(name))

        ring = sb("ring", SLOTS * SLOT)
        x = sb("x", TT * D)
        xn = sb("xn", TT * D)
        xnT = sb("xnT", DC * T)
        sq = sb("sq", TT * D)
        gain = sb("gain", D)
        cst = sb("cst", C_COMMON)
        lcst = sb("lcst", C_LAYER)
        w_route = sb("w_route", 2 * DC * ROUTE)
        b_route = sb("b_route", 2 * ROUTE)
        w_gates = sb("w_gates", DC * 32)
        b_gates = sb("b_gates", 32)
        small = sb("small", 128)
        extra_i = sb("items_i", 8, I32)
        PHASE = 15800
        phase = sb("phase", PHASE)
        psum = ctx.enter_context(nc.psum_tensor("psum", [P, 8, 512], F32))

        def carve(sizes):
            at, views = 0, {}
            for name, n in sizes:
                views[name] = phase[:, at:at + n]
                at += n
            assert at <= PHASE, at
            return views

        x3 = x[:, :].rearrange("p (t d) -> p t d", t=TT)
        xn3 = xn[:, :].rearrange("p (t d) -> p t d", t=TT)
        xnT3 = xnT[:, :].rearrange("p (c t) -> p c t", c=DC)
        ident = cst[:, C_IDENT:C_TRI]
        tri = cst[:, C_TRI:C_ONES]
        ones = cst[:, C_ONES:C_SLOTID]
        slotid = cst[:, C_SLOTID:C_RANKW]
        rankw = cst[:, C_RANKW:C_THR]
        thr = cst[:, C_THR:C_COMMON]

        def slot(n):
            return ring[:, (n % SLOTS) * SLOT:(n % SLOTS + 1) * SLOT]

        def bank(b):
            return psum[:, b, :]

        n_a = 4 + 2
        n_c = 6 + 2
        first = {"A": 0, "B": n_a, "C": n_a + QUADS * ITEM, "D": n_a + QUADS * ITEM + n_c}
        assert ITEM % SLOTS == 0
        landed = {ph: [sem(f"landed_{ph}{s}") for s in range(SLOTS)] for ph in "ABCD"}
        used = {ph: sem(f"used_{ph}") for ph in "ABCD"}

        def dense_source(ph, j):
            w_in, w_out, n_in = ((a["ev_w_in"], a["ev_w_out"], 4) if ph == "A"
                                 else (a["od_w_in"], a["od_w_out"], 6))
            w, b = (w_in, j) if j < n_in else (w_out, j - n_in)
            return w[0, :, b * 512:(b + 1) * 512].rearrange("(c p) n -> p c n", p=P)

        s_load = {n: sem(f"loaded_{n}") for n in
                  ("x", "cst", "lc0", "lc1", "bias", "qkgain", "route", "gates", "hgain")}
        s_gain = sem("gain_loaded")
        s_x = sem("x_ready")
        s_ssq = sem("squares_summed")
        s_ms = sem("mean_square_ready")
        s_rt = sem("root_ready")
        s_xn = sem("xn_ready")
        s_xTp = sem("xnT_in_psum")
        s_xTa = sem("xnT_copied_act")
        s_xTv = sem("xnT_copied_dve")
        dvc = sem("dve_chain")
        s_out = sem("out_stored")
        s_free = sem("slot_seen_free")

        s_biasm = sem("bias_masked")
        s_ua = {ph: sem(f"u_copied_act_{ph}") for ph in "AC"}
        s_uv = {ph: sem(f"u_copied_dve_{ph}") for ph in "AC"}
        s_qsq = sem("qk_squared")
        s_qms = sem("qk_mean_square")
        s_qrt = sem("qk_root")
        s_qn = sem("qk_normed")
        s_qTp = {ph: sem(f"qkT_in_psum_{ph}") for ph in "AC"}
        s_qT = {ph: sem(f"qkT_copied_{ph}") for ph in "AC"}
        s_f1 = sem("seq_dft_done")
        s_f1c = sem("seq_dft_copied")
        s_f2 = sem("ch_dft_done")
        s_f2c = sem("ch_dft_copied")
        s_sc = sem("scores_done")
        s_mx = sem("max_ready")
        s_ex = sem("exp_done")
        s_rl = sem("inv_sum_ready")
        s_pn = sem("probs_normed")
        s_pT = sem("probsT_in_psum")
        s_pTc = sem("probsT_copied")
        s_pv = sem("pv_done")
        s_o = sem("attn_copied")

        def moe_sems(l):
            return {n: sem(f"{n}_{l}") for n in
                    ("logits", "gsub", "gexp", "esub", "eexp", "mask", "rank", "routed", "rounds",
                     "sel", "disp", "dispc_a", "dispc_v", "gtp", "gtc", "neg", "h", "hTp",
                     "hTc", "y_a", "y_v", "comb", "added")}

        ms = [moe_sems(0), moe_sems(1)]

        s_gt = sem("gates_done")
        s_gab = sem("gate_abs_ready")
        s_gex = sem("gate_exp_ready")
        s_gp1 = sem("gate_exp1_ready")
        s_gln = sem("gate_log_ready")
        s_gtk = sem("gates_token_major")
        s_gTp = sem("gatesT_in_psum")
        s_em = sem("neg_m_ready")
        s_eme = sem("exp_neg_m_ready")
        s_aTp = sem("aT_in_psum")
        s_aT = sem("aT_copied")
        s_oex = sem("o_exp_ready")
        s_st = sem("st_done")
        s_bc = sem("m_broadcast")
        s_dl = sem("decay_log_ready")
        s_w = sem("decay_exp_ready")
        s_ws = sem("weighted_scores")
        s_nu = sem("num_done")
        s_rd = sem("inv_den_ready")
        s_hf = sem("h_fw_ready")
        s_hb = sem("h_ready")
        s_hsq = sem("h_squared")
        s_hms = sem("h_mean_square")
        s_hrt = sem("h_root")
        s_hn = sem("h_normed")
        s_hTp = sem("hT_in_psum")
        s_hTa = sem("hT_copied_act")
        s_hTv = sem("hT_copied_dve")

        A = carve([("u", TT * 2048), ("qkT", 8 * T), ("bias", BIAS_ROWS * HEADS * GRID_W), ("P", 2 * TT * T),
                   ("PT", 2 * TT * T), ("mixT", DC * T), ("st", 160)])
        C = carve([("qk", TT * 1024), ("ve", TT * HEADS * VE), ("og", TT * D), ("qkT", 8 * T),
                   ("W", 2 * 3 * T), ("h", TT * D), ("tmp", 2 * TT * P), ("gtok", TT * 32),
                   ("gw", 3 * TT * 16), ("gT", 4 * T), ("F", 2 * T), ("a", 2 * T), ("nM", 2 * T),
                   ("E", 2 * T), ("aT", 64), ("st", 160)])
        M = carve([("L", TT * ROUTE), ("work", 8 * TT * EXPERTS), ("oh", 2 * TT * EXPERTS),
                   ("mask", TT * EXPERTS), ("G", TT * EXPERTS), ("rank", TT * EXPERTS), ("st", 64),
                   ("S", TT * P), ("Gs", TT * P), ("xT", DC * P), ("GT", TT * P), ("eg", FF),
                   ("h", FF), ("hT", FF), ("y", D)])

        u_a = A["u"].rearrange("p (t n) -> p t n", t=TT)
        qkT_a = A["qkT"].rearrange("p (c t) -> p c t", c=8)
        bias_a = A["bias"].rearrange("p (r h k) -> p r h k", r=BIAS_ROWS, h=HEADS)
        P_a = A["P"].rearrange("p (b t k) -> p b t k", b=2, t=TT)
        PT_a = A["PT"].rearrange("p (b n) -> p b n", b=2)
        mixT_a = A["mixT"].rearrange("p (c t) -> p c t", c=DC)
        AB = xn[:, :].rearrange("p (c n) -> p c n", c=4)
        rev = lcst[:, C0_REV:C0_SEQ]
        seqdft = lcst[:, C0_SEQ:C0_CH].rearrange("p (t n) -> p t n", t=TT)
        chdft = lcst[:, C0_CH:C0_MASK].rearrange("p (j n) -> p j n", j=2)
        namask = lcst[:, C0_MASK:C0_SIZE]

        qk_c = C["qk"].rearrange("p (t n) -> p t n", t=TT)
        ve = C["ve"].rearrange("p (t h e) -> p t h e", t=TT, h=HEADS)
        og = C["og"].rearrange("p (t n) -> p t n", t=TT)
        qkT_c = C["qkT"].rearrange("p (c t) -> p c t", c=8)
        W_c = C["W"].rearrange("p (b n) -> p b n", b=2)
        h_c = C["h"].rearrange("p (t n) -> p t n", t=TT)
        tmp_c = C["tmp"].rearrange("p (b t n) -> p b t n", b=2, t=TT)
        gtok = C["gtok"].rearrange("p (t n) -> p t n", t=TT)
        gw = C["gw"].rearrange("p (j t d h) -> p j t d h", j=3, t=TT, d=2)
        gT = C["gT"][0:8, :].rearrange("p (j t) -> p j t", j=4)
        F_c = C["F"][0:8, :].rearrange("p (d t) -> p d t", d=2)
        a_c = C["a"][0:8, :].rearrange("p (d t) -> p d t", d=2)
        nM = C["nM"][0:8, :].rearrange("p (d t) -> p d t", d=2)
        E_c = C["E"][0:8, :].rearrange("p (d t) -> p d t", d=2)
        aT = C["aT"].rearrange("p (k d t h) -> p k d t h", k=2, d=2, t=TT)
        mixT_c = C["qk"].rearrange("p (c t) -> p c t", c=DC)
        mlmask = lcst[:, C1_MASK:C1_SEL]
        sel_c = lcst[0:8, C1_SEL:C1_SIZE].rearrange("p (h n) -> p h n", h=HEADS)

        L3 = M["L"].rearrange("p (t n) -> p t n", t=TT)
        S_m = M["S"].rearrange("p (t e s) -> p t e s", t=TT, e=QUAD)
        Gs_m = M["Gs"].rearrange("p (t e s) -> p t e s", t=TT, e=QUAD)
        xT_m = M["xT"].rearrange("p (c s) -> p c s", c=DC)
        hT_m = M["hT"].rearrange("p (c s) -> p c s", c=FF // P)
        rk3 = M["rank"].rearrange("p (t e) -> p t e", t=TT)
        G3 = M["G"].rearrange("p (t e) -> p t e", t=TT)
        COMB = ((0, 0, 0), (1, 0, 1), (6, 1, 0), (7, 1, 1))

        block = ctx.enter_context(nc.Block())

        @block.sync
        def _(sp):
            sp.dma_start(x3, a["x"][0].rearrange("(t p) d -> p t d", p=P)).then_inc(s_load["x"], 16)

            def slot_free(count, value):
                sp.wait_ge(count, value)
                sp.sem_inc(s_free, 1)

            def expert_piece(ph, l, q, j):
                dst = slot(first[ph] + j).rearrange("p (e n) -> p e n", e=QUAD)
                done = landed[ph][(first[ph] + j) % SLOTS]
                if j < GU_PIECES:
                    for k, name in enumerate(("moe_w_gate", "moe_w_up")):
                        src = a[name][l, bass.ds(q * QUAD, QUAD), j * P:(j + 1) * P, :]
                        sp.dma_start(dst[:, :, k * FF:(k + 1) * FF],
                                     src.rearrange("e p f -> p e f")).then_inc(done, 16)
                else:
                    k = j - GU_PIECES
                    for half in range(2):
                        src = a["moe_w_down"][l, bass.ds(q * QUAD + 2 * half, 2), k * P:(k + 1) * P, :]
                        sp.dma_start(dst[:, 2 * half:2 * half + 2, :],
                                     src.rearrange("e p f -> p e f")).then_inc(done, 16)

            def dense(ph, prev, prev_extra, prev_total):
                n_ph = n_a if ph == "A" else n_c
                for j in range(n_ph):
                    if j >= SLOTS:
                        sp.wait_ge(used[ph], j - SLOTS + 1)
                    elif prev is not None:
                        sp.wait_ge(used[prev], prev_extra + (prev_total - SLOTS + 1 + j))
                    dst = slot(first[ph] + j).rearrange("p (c n) -> p c n", c=DC)
                    sp.dma_start(dst, dense_source(ph, j)).then_inc(
                        landed[ph][(first[ph] + j) % SLOTS], 16)

            def moe(ph, l, prev, n_prev):
                for j in range(SLOTS):
                    sp.wait_ge(used[prev], n_prev - SLOTS + 1 + j)
                    expert_piece(ph, l, 0, j)
                sp.wait_ge(ms[l]["rounds"], 1)
                extra = sp.value_load(extra_i[0:1, l:l + 1], min_val=0, max_val=QUADS * (MAX_ROUNDS - 1))
                with sp.Fori(0, extra + (QUADS - 1)) as i:
                    q = sp.snap(i % QUADS)
                    for j in range(SLOTS, ITEM):
                        slot_free(used[ph], i * ITEM + (j - SLOTS + 1))
                        expert_piece(ph, l, q, j)
                    q = sp.snap((i + 1) % QUADS)
                    for j in range(SLOTS):
                        slot_free(used[ph], i * ITEM + (ITEM + j - SLOTS + 1))
                        expert_piece(ph, l, q, j)
                for j in range(SLOTS, ITEM):
                    slot_free(used[ph], extra * ITEM + ((QUADS - 1) * ITEM + j - SLOTS + 1))
                    expert_piece(ph, l, QUADS - 1, j)
                return extra * ITEM, QUADS * ITEM

            dense("A", None, 0, 0)
            total = moe("B", 0, "A", n_a)
            dense("C", "B", *total)
            moe("D", 1, "C", n_c)
            sp.wait_ge(s_x, 4)
            sp.dma_start(out[0].rearrange("(t p) d -> p t d", p=P), x3).then_inc(s_out, 16)
            sp.wait_ge(s_out, 16)

        @block.gpsimd
        def _(pool):
            def bcast(row, n):
                return row.rearrange("(o n) -> o n", o=1).broadcast_to([P, n])

            pool.dma_start(gain[:, :], bcast(a["ev_norm"][0], D)).then_inc(s_gain, 16)
            for r in range(2):
                for k in range(BIAS_ROWS):
                    base = (k + 5 - r) * REL_C + (REL_C // 2 - (GRID_W - 1))
                    src = bass.AP(tensor=a["ev_rel_bias"].tensor, offset=base,
                                  ap=[[1, GRID_W], [REL_SIZE, HEADS], [1, GRID_W]])
                    pool.dma_start(bias_a[GRID_W * r:GRID_W * (r + 1), k], src).then_inc(s_load["bias"], 16)
            route = w_route[:, :].rearrange("p (l c n) -> p l c n", l=2, c=DC)
            for l in range(2):
                pool.dma_start(route[:, l, :, 0:GROUPS],
                               a["moe_w_rg"][l].rearrange("(c p) n -> p c n", p=P)).then_inc(s_load["route"], 16)
                pool.dma_start(route[:, l, :, GROUPS:ROUTE],
                               a["moe_w_re"][l].rearrange("(c p) n -> p c n", p=P)).then_inc(s_load["route"], 16)
                pool.dma_start(b_route[:, l * ROUTE:l * ROUTE + GROUPS],
                               bcast(a["moe_b_rg"][l], GROUPS)).then_inc(s_load["route"], 16)
                pool.dma_start(b_route[:, l * ROUTE + GROUPS:(l + 1) * ROUTE],
                               bcast(a["moe_b_re"][l], EXPERTS)).then_inc(s_load["route"], 16)
            pool.dma_start(w_gates[:, :].rearrange("p (c n) -> p c n", c=DC),
                           a["od_w_in"][0, :, 3072:3104].rearrange("(c p) n -> p c n", p=P)).then_inc(s_load["gates"], 16)
            pool.dma_start(b_gates[:, :], bcast(a["od_gate_bias"][0], 32)).then_inc(s_load["gates"], 16)

            pool.wait_ge(s_load["bias"], 16 * 2 * BIAS_ROWS)
            pool.wait_ge(s_load["lc0"], 16)
            every = A["bias"].rearrange("p (n k) -> p n k", k=GRID_W)
            pool.tensor_tensor(every, every, namask.unsqueeze(1).broadcast_to([P, BIAS_ROWS * HEADS, GRID_W]),
                               ALU.add).then_inc(s_biasm, 1)
            pool.wait_ge(s_xn, 2)
            pool.dma_start(gain[:, :], bcast(a["moe_norm"][0], D)).then_inc(s_gain, 16)
            for h in range(HEADS):
                pool.wait_ge(s_rl, h + 1)
                for t in range(TT):
                    pool.tensor_scalar(P_a[:, h % 2, t], P_a[:, h % 2, t],
                                       A["st"][:, 48 + 2 * h + t:49 + 2 * h + t], None, ALU.mult).then_inc(s_pn, 1)
            pool.wait_ge(s_xn, 4)
            pool.dma_start(gain[:, :], bcast(a["od_norm"][0], D)).then_inc(s_gain, 16)
            pool.wait_ge(used["A"], n_a)
            pool.dma_start(lcst[:, :], a["c_layer1"]).then_inc(s_load["lc1"], 16)
            pool.wait_ge(s_xn, 6)
            pool.dma_start(gain[:, :], bcast(a["od_h_gain"][0], D)).then_inc(s_gain, 16)
            pool.wait_ge(s_hn, 1)
            pool.dma_start(gain[:, :], bcast(a["moe_norm"][1], D)).then_inc(s_gain, 16)

        @block.scalar
        def _(act):
            act.dma_start(cst[:, :], a["c_common"]).then_inc(s_load["cst"], 16)
            act.dma_start(small[0:64, 0:1], a["ev_q_gain"].rearrange("o d -> d o")).then_inc(s_load["qkgain"], 16)
            act.dma_start(small[64:128, 0:1], a["ev_q_gain"].rearrange("o d -> d o")).then_inc(s_load["qkgain"], 16)
            act.dma_start(small[0:64, 1:2], a["ev_k_gain"].rearrange("o d -> d o")).then_inc(s_load["qkgain"], 16)
            act.dma_start(small[64:128, 1:2], a["ev_k_gain"].rearrange("o d -> d o")).then_inc(s_load["qkgain"], 16)
            act.dma_start(lcst[:, :], a["c_layer0"]).then_inc(s_load["lc0"], 16)

            def norm(n):
                if n == 0:
                    act.wait_ge(s_load["x"], 16)
                else:
                    act.wait_ge(s_x, n)
                for t in range(TT):
                    nc.scalar.activation(sq[:, t * D:(t + 1) * D], x3[:, t], ACT.Square,
                                         accum_out=small[:, 8 + t:9 + t]).then_inc(s_ssq, 1)
                act.wait_ge(s_ms, n + 1)
                nc.scalar.activation(small[:, 12:14], small[:, 10:12], ACT.Sqrt).then_inc(s_rt, 1)
                for p in (0, 2):
                    act.wait_ge(s_xTp, 4 * n + p + 1)
                    nc.scalar.copy(xnT[:, p * 512:(p + 1) * 512], bank(p)).then_inc(s_xTa, 1)

            def moe(ph, l):
                s = ms[l]
                norm(2 * l + 1)
                act.wait_ge(s["gsub"], 1)
                nc.scalar.activation(M["st"][:, 0:8], M["st"][:, 0:8], ACT.Exp).then_inc(s["gexp"], 1)
                act.wait_ge(s["esub"], 1)
                nc.scalar.activation(M["st"][:, 20:22], M["st"][:, 20:22], ACT.Exp).then_inc(s["eexp"], 1)
                act.wait_ge(s["rounds"], 1)
                extra = act.value_load(extra_i[0:1, l:l + 1], min_val=0, max_val=QUADS * (MAX_ROUNDS - 1))
                with act.Fori(0, extra + QUADS) as i:
                    n = act.snap(i + 1)
                    act.wait_ge(s["disp"], n)
                    nc.scalar.copy(M["xT"][:, 0:512], bank(4)).then_inc(s["dispc_a"], 1)
                    act.wait_ge(s["gtp"], n)
                    nc.scalar.copy(M["GT"], bank(6)[:, 0:T]).then_inc(s["gtc"], 1)
                    act.wait_ge(used[ph], i * ITEM + GU_PIECES)
                    nc.scalar.activation(M["eg"], bank(0), ACT.Exp, scale=-1.0).then_inc(s["neg"], 1)
                    act.wait_ge(s["hTp"], n)
                    nc.scalar.copy(M["hT"], bank(7)).then_inc(s["hTc"], 1)
                    act.wait_ge(used[ph], i * ITEM + ITEM)
                    nc.scalar.copy(M["y"][:, 0:512], bank(2)).then_inc(s["y_a"], 1)

            norm(0)
            for b in range(4):
                act.wait_ge(used["A"], b + 1)
                nc.scalar.copy(u_a[:, 0, b * 512:(b + 1) * 512], bank(2 * b)).then_inc(s_ua["A"], 1)
                if b == 1:
                    act.wait_ge(s_ua["A"], 2)
                    act.wait_ge(s_uv["A"], 2)
                    nc.scalar.activation(sq[:, :].rearrange("p (t n) -> p t n", t=TT), u_a[:, :, 0:1024],
                                         ACT.Square).then_inc(s_qsq, 1)
            act.wait_ge(s_qms, 1)
            nc.scalar.activation(A["st"][:, 0:32], A["st"][:, 0:32], ACT.Sqrt).then_inc(s_qrt, 1)
            for c in range(4):
                act.wait_ge(s_f1, c + 1)
                nc.scalar.copy(AB[:, c], bank(4 + c)).then_inc(s_f1c, 1)
            for c in range(4):
                act.wait_ge(s_f2, c + 1)
                nc.scalar.copy(mixT_a[:, 4 + c], bank(4 + c)[:, 0:T]).then_inc(s_f2c, 1)
            for h in range(HEADS):
                act.wait_ge(s_mx, h + 1)
                if h >= 2:
                    act.wait_ge(s_pT, h - 1)
                for t in range(TT):
                    nc.scalar.activation(P_a[:, h % 2, t], bank(h % 2)[:, t * T:(t + 1) * T], ACT.Exp,
                                         bias=A["st"][:, 80 + 2 * h + t:81 + 2 * h + t],
                                         accum_out=A["st"][:, 100 + 2 * h + t:101 + 2 * h + t]).then_inc(s_ex, 1)
                if h >= 1:
                    g = h - 1
                    act.wait_ge(s_pT, g + 1)
                    if g >= 2:
                        act.wait_ge(s_pv, g - 1)
                    nc.scalar.copy(PT_a[:, g % 2], bank(2 + g % 2)).then_inc(s_pTc, 1)
            g = HEADS - 1
            act.wait_ge(s_pT, g + 1)
            act.wait_ge(s_pv, g - 1)
            nc.scalar.copy(PT_a[:, g % 2], bank(2 + g % 2)).then_inc(s_pTc, 1)

            moe("B", 0)

            norm(2)
            act.wait_ge(s_gab, 1)
            nc.scalar.activation(gw[:, 1], gw[:, 0], ACT.Exp, scale=-1.0).then_inc(s_gex, 1)
            act.wait_ge(s_gp1, 1)
            nc.scalar.activation(gw[:, 1], gw[:, 1], ACT.Ln).then_inc(s_gln, 1)
            for b in range(6):
                act.wait_ge(used["C"], b + 1)
                src = bank(2 * (b % 4))
                if b < 2:
                    nc.scalar.copy(qk_c[:, 0, b * 512:(b + 1) * 512], src).then_inc(s_ua["C"], 1)
                elif b < 4:
                    nc.scalar.copy(ve[:, 0, 4 * (b - 2):4 * (b - 1), 0:ML_DV],
                                   src.rearrange("p (h e) -> p h e", h=4)).then_inc(s_ua["C"], 1)
                else:
                    for t in range(TT):
                        nc.scalar.activation(og[:, t, (b - 4) * 512:(b - 3) * 512],
                                             bank(2 * (b % 4) + t), ACT.Exp, scale=-1.0).then_inc(
                                                 s_ua["C"] if t == 0 else s_oex, 1)
                if b == 3:
                    act.wait_ge(s_em, 1)
                    nc.scalar.activation(E_c, F_c, ACT.Exp).then_inc(s_eme, 1)
            for h in range(HEADS + 1):
                if h < HEADS:
                    act.wait_ge(s_dl, h + 1)
                    nc.scalar.activation(W_c[:, h % 2], W_c[:, h % 2], ACT.Exp).then_inc(s_w, 1)
                if h >= 1:
                    g = h - 1
                    act.wait_ge(s_rd, g + 1)
                    if g >= 2:
                        act.wait_ge(s_hb, g - 1)
                    for t in range(TT):
                        nc.scalar.activation(tmp_c[:, g % 2, t], bank(4 + 2 * (g % 2))[:, t * VE:t * VE + ML_DV],
                                             ACT.Copy, scale=C["st"][:, 4 * g + t:4 * g + t + 1]).then_inc(s_hf, 1)
            act.wait_ge(s_hb, HEADS)
            nc.scalar.activation(sq[:, :], C["h"], ACT.Square).then_inc(s_hsq, 1)
            act.wait_ge(s_hms, 1)
            nc.scalar.activation(C["st"][:, 64:80], C["st"][:, 64:80], ACT.Sqrt).then_inc(s_hrt, 1)
            for p in (0, 2):
                act.wait_ge(s_hTp, p + 1)
                nc.scalar.copy(mixT_c[:, 2 * p:2 * p + 2, :], bank(p).rearrange("p (c t) -> p c t", c=2)).then_inc(s_hTa, 1)

            moe("D", 1)

        @block.vector
        def _(dve):
            V = nc.vector
            chain = [0]

            def link(ins):
                chain[0] += 1
                ins.then_inc(dvc, 1)
                dve.wait_ge(dvc, chain[0])

            def norm(n):
                dve.wait_ge(s_ssq, 2 * (n + 1))
                V.tensor_scalar(small[:, 10:12], small[:, 8:10], 1.0 / D, EPS, ALU.mult, ALU.add).then_inc(s_ms, 1)
                dve.wait_ge(s_rt, n + 1)
                link(V.reciprocal(small[:, 14:16], small[:, 12:14]))
                dve.wait_ge(s_gain, 16 * (n + 1 if n < 3 else 5))
                for t in range(TT):
                    V.scalar_tensor_tensor(xn3[:, t], x3[:, t], small[:, 14 + t:15 + t], gain[:, :],
                                           ALU.mult, ALU.mult).then_inc(s_xn, 1)
                for p in (1, 3):
                    dve.wait_ge(s_xTp, 4 * n + p + 1)
                    V.tensor_copy(xnT[:, p * 512:(p + 1) * 512], bank(p)).then_inc(s_xTv, 1)

            def out_proj(ph, b0):
                for nb in range(2):
                    dve.wait_ge(used[ph], b0 + nb + 1)
                    for t in range(TT):
                        dst = x3[:, t, nb * 512:(nb + 1) * 512]
                        link(V.tensor_tensor(dst, dst, bank(2 * nb + t), ALU.add))
                dve.sem_inc(s_x, 1)

            def moe(ph, l):
                s = ms[l]
                st = M["st"]
                norm(2 * l + 1)
                dve.wait_ge(s["logits"], 1)
                bb = b_route[:, l * ROUTE:(l + 1) * ROUTE].unsqueeze(1).broadcast_to([P, TT, ROUTE])
                dve.wait_ge(s_load["route"], 128)
                link(V.tensor_tensor(L3, bank(0)[:, 0:TT * ROUTE].rearrange("p (t n) -> p t n", t=TT), bb, ALU.add))
                lg = L3[:, :, 0:GROUPS]
                gm = st[:, 8:10]
                link(V.reduce_max(gm, lg, AX))
                gmb = gm.unsqueeze(2).broadcast_to([P, TT, GROUPS])
                ge = st[:, 0:8].rearrange("p (t g) -> p t g", t=TT)
                V.tensor_tensor(ge, lg, gmb, ALU.subtract).then_inc(s["gsub"], 1)
                w = [M["work"][:, j * 64:(j + 1) * 64] for j in range(8)]
                g1 = w[0][:, 0:8].rearrange("p (t g) -> p t g", t=TT)
                g2 = w[1][:, 0:8].rearrange("p (t g) -> p t g", t=TT)
                order4 = rankw[:, 0:GROUPS].unsqueeze(1).broadcast_to([P, TT, GROUPS])
                link(V.tensor_tensor(g1, lg, gmb, ALU.is_equal))
                link(V.tensor_tensor(g2, g1, order4, ALU.mult))
                link(V.reduce_max(st[:, 10:12], g2, AX))
                link(V.tensor_tensor(g1, g2, st[:, 10:12].unsqueeze(2).broadcast_to([P, TT, GROUPS]), ALU.is_equal))
                link(V.tensor_scalar(g2, g1, -NEG, NEG, ALU.mult, ALU.add))
                w4 = [v.rearrange("p (t g e) -> p t g e", t=TT, g=GROUPS) for v in w]
                w3 = [v.rearrange("p (t e) -> p t e", t=TT) for v in w]
                for t in range(TT):
                    le = L3[:, t, GROUPS:ROUTE].rearrange("p (g e) -> p g e", g=GROUPS)
                    link(V.tensor_tensor(w4[2][:, t], le, g2[:, t].unsqueeze(2).broadcast_to([P, GROUPS, PER_GROUP]), ALU.add))
                order = rankw.unsqueeze(1).broadcast_to([P, TT, EXPERTS])
                oh = [M["oh"][:, j * 64:(j + 1) * 64].rearrange("p (t e) -> p t e", t=TT) for j in range(2)]

                def top(src, vmax, j):
                    link(V.reduce_max(vmax, src, AX))
                    link(V.tensor_tensor(w3[3], src, vmax.unsqueeze(2).broadcast_to([P, TT, EXPERTS]), ALU.is_equal))
                    link(V.tensor_tensor(w3[4], w3[3], order, ALU.mult))
                    link(V.reduce_max(st[:, 12:14], w3[4], AX))
                    link(V.tensor_tensor(oh[j], w3[4], st[:, 12:14].unsqueeze(2).broadcast_to([P, TT, EXPERTS]), ALU.is_equal))

                top(w3[2], st[:, 16:18], 0)
                link(V.scalar_tensor_tensor(w3[5], oh[0], NEG, w3[2], ALU.mult, ALU.add))
                top(w3[5], st[:, 18:20], 1)
                V.tensor_tensor(st[:, 20:22], st[:, 18:20], st[:, 16:18], ALU.subtract).then_inc(s["esub"], 1)
                m3 = M["mask"].rearrange("p (t e) -> p t e", t=TT)
                V.tensor_tensor(m3, oh[0], oh[1], ALU.add).then_inc(s["mask"], 1)
                dve.wait_ge(s["gexp"], 1)
                link(V.reduce_sum(st[:, 22:24], ge, AX))
                dve.wait_ge(s["eexp"], 1)
                link(V.tensor_scalar(st[:, 24:26], st[:, 20:22], 1.0, None, ALU.add))
                link(V.tensor_tensor(st[:, 24:26], st[:, 24:26], st[:, 22:24], ALU.mult))
                link(V.reciprocal(st[:, 26:28], st[:, 24:26]))
                link(V.tensor_tensor(st[:, 28:30], st[:, 26:28], st[:, 20:22], ALU.mult))
                link(V.tensor_tensor(w3[6], oh[0], st[:, 26:28].unsqueeze(2).broadcast_to([P, TT, EXPERTS]), ALU.mult))
                link(V.tensor_tensor(w3[7], oh[1], st[:, 28:30].unsqueeze(2).broadcast_to([P, TT, EXPERTS]), ALU.mult))
                link(V.tensor_tensor(G3, w3[6], w3[7], ALU.add))
                dve.wait_ge(s["rank"], 1)
                link(V.tensor_scalar(w3[6], m3, 1e4, -1e4, ALU.mult, ALU.add))
                link(V.tensor_tensor(rk3, bank(1)[:, 0:64].rearrange("p (t e) -> p t e", t=TT), w3[6], ALU.add))
                link(V.reduce_max(st[:, 30:31], bank(1)[:, 64:96], AX))
                link(V.tensor_tensor(st[:, 32:40], thr, st[:, 30:31].broadcast_to([P, MAX_ROUNDS]), ALU.is_lt))
                link(V.reduce_sum(st[:, 31:32], st[:, 32:40], AX))
                V.tensor_scalar(extra_i[:, l:l + 1], st[:, 31:32], float(QUADS), None,
                                ALU.mult).then_inc(s["rounds"], 1)
                dve.wait_ge(s["rounds"], 1)
                extra = dve.value_load(extra_i[0:1, l:l + 1], min_val=0, max_val=QUADS * (MAX_ROUNDS - 1))

                def select(q4, first_slot, count):
                    sid = slotid[:, bass.ds(first_slot, CAP)].unsqueeze(1).broadcast_to([P, QUAD, CAP])
                    for t in range(TT):
                        V.tensor_tensor(S_m[:, t], rk3[:, t, bass.ds(q4, QUAD)].unsqueeze(2).broadcast_to([P, QUAD, CAP]),
                                        sid, ALU.is_equal).then_inc(s["sel"], 1)
                    dve.wait_ge(s["sel"], count)
                    for t in range(TT):
                        V.tensor_tensor(Gs_m[:, t], S_m[:, t],
                                        G3[:, t, bass.ds(q4, QUAD)].unsqueeze(2).broadcast_to([P, QUAD, CAP]),
                                        ALU.mult).then_inc(s["sel"], 1)

                select(0, 0, 2)
                dve.sem_inc(s["added"], 4)
                base = chain[0]
                with dve.Fori(0, extra + QUADS) as i:
                    n = dve.snap(i + 1)
                    dve.wait_ge(s["disp"], n)
                    V.tensor_copy(M["xT"][:, 512:1024], bank(5)).then_inc(s["dispc_v"], 1)
                    dve.wait_ge(s["neg"], n)
                    V.tensor_scalar(M["eg"], M["eg"], 1.0, None, ALU.add).then_inc(s["h"], 1)
                    dve.wait_ge(s["h"], i * 4 + 1)
                    V.reciprocal(M["eg"], M["eg"]).then_inc(s["h"], 1)
                    dve.wait_ge(s["h"], i * 4 + 2)
                    V.tensor_tensor(M["h"], bank(0), M["eg"], ALU.mult).then_inc(s["h"], 1)
                    dve.wait_ge(s["h"], i * 4 + 3)
                    V.tensor_tensor(M["h"], bank(1), M["h"], ALU.mult).then_inc(s["h"], 1)
                    dve.wait_ge(s["gtp"], n)
                    q4 = dve.snap((n % QUADS) * QUAD)
                    fs = dve.snap((n // QUADS) * CAP)
                    select(q4, fs, i * 4 + 6)
                    dve.wait_ge(used[ph], i * ITEM + ITEM)
                    V.tensor_copy(M["y"][:, 512:1024], bank(3)).then_inc(s["y_v"], 1)
                    for k, (b, t, nb) in enumerate(COMB):
                        dve.wait_ge(s["comb"], i * 4 + (k + 1))
                        dst = x3[:, t, nb * 512:(nb + 1) * 512]
                        V.tensor_tensor(dst, dst, bank(b), ALU.add).then_inc(s["added"], 1)
                assert chain[0] == base
                dve.wait_ge(s["added"], extra * 4 + (QUADS * 4 + 4))
                dve.sem_inc(s_x, 1)

            norm(0)
            st = A["st"]
            for b in range(4):
                dve.wait_ge(used["A"], b + 1)
                V.tensor_copy(u_a[:, 1, b * 512:(b + 1) * 512], bank(2 * b + 1)).then_inc(s_uv["A"], 1)
                if b == 2:
                    dve.wait_ge(s_qsq, 1)
                    link(V.reduce_sum(st[:, 32:64], sq[:, :].rearrange("p (g d) -> p g d", d=NA_DH), AX))
                    V.tensor_scalar(st[:, 0:32], st[:, 32:64], 1.0 / NA_DH, EPS, ALU.mult, ALU.add).then_inc(s_qms, 1)
            dve.wait_ge(s_qrt, 1)
            link(V.reciprocal(st[:, 32:64], st[:, 0:32]))
            dve.wait_ge(s_ua["A"], 2)
            for t in range(TT):
                qk = u_a[:, t, 0:1024].rearrange("p (g d) -> p g d", d=NA_DH)
                rs = st[:, 32 + 16 * t:48 + 16 * t].unsqueeze(2).broadcast_to([P, 16, NA_DH])
                V.tensor_tensor(qk, qk, rs, ALU.mult).then_inc(s_qn, 1)
            dve.wait_ge(s_load["qkgain"], 64)
            for p in range(4):
                dve.wait_ge(s_qTp["A"], p + 1)
                V.tensor_scalar(qkT_a[:, 2 * p:2 * p + 2, :], bank(p).rearrange("p (c t) -> p c t", c=2),
                                small[:, p // 2:p // 2 + 1], NA_DH ** -0.5 if p < 2 else 1.0,
                                ALU.mult, ALU.mult).then_inc(s_qT["A"], 1)
            for h in range(HEADS + 1):
                if h < HEADS:
                    dve.wait_ge(s_sc, h + 1)
                    link(V.reduce_max(st[:, 116 + 2 * h:118 + 2 * h], bank(h % 2).rearrange("p (t k) -> p t k", t=TT), AX))
                    V.tensor_scalar(st[:, 80 + 2 * h:82 + 2 * h], st[:, 116 + 2 * h:118 + 2 * h], -1.0, None, ALU.mult).then_inc(s_mx, 1)
                if h >= 1:
                    g = h - 1
                    dve.wait_ge(s_ex, 2 * (g + 1))
                    V.reciprocal(st[:, 48 + 2 * g:50 + 2 * g], st[:, 100 + 2 * g:102 + 2 * g]).then_inc(s_rl, 1)
                    if g >= 3 and g % 2 == 1:
                        hp = (g - 3) // 2
                        dve.wait_ge(s_pv, g - 1)
                        V.tensor_copy(mixT_a[:, hp], bank(6 + hp % 2)[:, 0:T]).then_inc(s_o, 1)
            dve.wait_ge(s_pv, HEADS)
            V.tensor_copy(mixT_a[:, HP - 1], bank(6 + (HP - 1) % 2)[:, 0:T]).then_inc(s_o, 1)
            out_proj("A", 4)

            moe("B", 0)

            norm(2)
            st = C["st"]
            dve.wait_ge(s_gt, 1)
            dve.wait_ge(s_load["gates"], 32)
            link(V.tensor_tensor(gtok, bank(7)[:, 0:TT * 32].rearrange("p (t n) -> p t n", t=TT),
                                 b_gates[:, :].unsqueeze(1).broadcast_to([P, TT, 32]), ALU.add))
            f4 = gtok.rearrange("p t (d k h) -> p t d k h", d=2, k=2)
            for t in range(TT):
                f = f4[:, t, :, 1, :]
                V.scalar_tensor_tensor(gw[:, 0, t], f, -1.0, f, ALU.mult, ALU.max).then_inc(dvc, 1)
                V.tensor_scalar(gw[:, 2, t], f, 0.0, None, ALU.min).then_inc(dvc, 1)
            chain[0] += 4
            dve.wait_ge(dvc, chain[0])
            dve.sem_inc(s_gab, 1)
            dve.wait_ge(s_gex, 1)
            V.tensor_scalar(gw[:, 1], gw[:, 1], 1.0, None, ALU.add).then_inc(s_gp1, 1)
            dve.wait_ge(s_gln, 1)
            for t in range(TT):
                V.tensor_tensor(f4[:, t, :, 1, :], gw[:, 2, t], gw[:, 1, t], ALU.subtract).then_inc(s_gtk, 1)
            V.memset(ve[:, :, :, ML_DV:VE], 1.0).then_inc(s_gtk, 1)
            dve.wait_ge(s_gTp, 2)
            V.tensor_copy(gT[:, 0:2], bank(6)[0:8, :].rearrange("p (j t) -> p j t", j=2)).then_inc(dvc, 1)
            link(V.tensor_copy(gT[:, 2:4], bank(7)[0:8, :].rearrange("p (j t) -> p j t", j=2)))
            chain[0] += 1
            dve.wait_ge(dvc, chain[0])
            one8 = ones[0:8, 0:1].broadcast_to([8, T])

            def way(ap, d):
                return ap[:, d, :] if d == 0 else ap[:, d, ::-1]

            gTi = gT.rearrange("p (d k) t -> p d k t", k=2)
            for d in range(2):
                lf = gTi[:, d, 1, :] if d == 0 else gTi[:, d, 1, ::-1]
                V.tensor_tensor_scan(way(F_c, d), one8, lf, 0.0, ALU.mult, ALU.add).then_inc(dvc, 1)
            chain[0] += 2
            dve.wait_ge(dvc, chain[0])
            link(V.tensor_tensor(a_c, gTi[:, :, 0, :], F_c, ALU.subtract))
            for d in range(2):
                V.tensor_tensor_scan(way(nM, d), one8, way(a_c, d), 0.0, ALU.mult, ALU.max).then_inc(dvc, 1)
            chain[0] += 2
            dve.wait_ge(dvc, chain[0])
            link(V.tensor_scalar(nM, nM, -1.0, None, ALU.mult))
            V.tensor_tensor(F_c, nM, F_c, ALU.subtract).then_inc(s_em, 1)

            dve.wait_ge(s_gtk, 3)
            for b in range(6):
                dve.wait_ge(used["C"], b + 1)
                src = bank(2 * (b % 4) + 1)
                if b < 2:
                    V.tensor_copy(qk_c[:, 1, b * 512:(b + 1) * 512], src).then_inc(s_uv["C"], 1)
                elif b < 4:
                    V.tensor_copy(ve[:, 1, 4 * (b - 2):4 * (b - 1), 0:ML_DV],
                                  src.rearrange("p (h e) -> p h e", h=4)).then_inc(s_uv["C"], 1)
            dve.wait_ge(s_oex, 2)
            dve.wait_ge(s_ua["C"], 6)
            link(V.tensor_scalar(C["og"], C["og"], 1.0, None, ALU.add))
            link(V.reciprocal(C["og"], C["og"]))
            dve.wait_ge(s_gain, 64)
            link(V.tensor_tensor(og, og, gain[:, :].unsqueeze(1).broadcast_to([P, TT, D]), ALU.mult))
            for p in range(4):
                dve.wait_ge(s_qTp["C"], p + 1)
                V.tensor_scalar(qkT_c[:, 2 * p:2 * p + 2, :], bank(p).rearrange("p (c t) -> p c t", c=2),
                                1.0 if p < 2 else 64 ** -0.5, None, ALU.mult).then_inc(s_qT["C"], 1)
            dve.wait_ge(s_aTp, 1)
            link(V.tensor_copy(C["aT"], bank(7)[:, 0:64]))
            SEG = ((0, 0, 0, 0, T), (T, 1, 1, 0, T), (2 * T, 1, 0, 0, P), (2 * T + P, 0, 1, P, P))

            def decay(h):
                dve.wait_ge(s_bc, h + 1)
                if h >= 2:
                    dve.wait_ge(s_nu, h - 1)
                for o, d, stile, t0, n in SEG:
                    ins = V.scalar_tensor_tensor(W_c[:, h % 2, o:o + n], bank(2 + h % 2)[:, d * T + t0:d * T + t0 + n],
                                                 aT[:, 0, d, stile, h:h + 1], mlmask[:, o:o + n], ALU.add, ALU.min)
                    ins.then_inc(dvc, 1)
                chain[0] += 4
                dve.wait_ge(dvc, chain[0])
                dve.sem_inc(s_dl, 1)

            def weigh(h):
                dve.wait_ge(s_w, h + 1)
                dve.wait_ge(s_st, h + 1)
                w = W_c[:, h % 2]
                sc = bank(h % 2)
                V.tensor_tensor(w[:, 0:2 * T], w[:, 0:2 * T], sc, ALU.mult).then_inc(s_ws, 1)
                diag = bass.AP(tensor=sc.tensor, offset=sc.offset, ap=[list(sc.ap[0]), [T + P, 2], [1, P]])
                V.tensor_tensor(w[:, 2 * T:3 * T].rearrange("p (j n) -> p j n", j=2),
                                w[:, 2 * T:3 * T].rearrange("p (j n) -> p j n", j=2), diag, ALU.mult).then_inc(s_ws, 1)

            def finish(h):
                dve.wait_ge(s_nu, h + 1)
                b = 4 + 2 * (h % 2)
                rd = st[:, 4 * h:4 * h + 4].rearrange("p (d t) -> p d t", d=2)
                den = psum[:, b:b + 2, ML_DV:2 * VE:VE]
                link(V.scalar_tensor_tensor(rd, den, -1.0, aT[:, 1, :, :, h], ALU.mult, ALU.max))
                link(V.tensor_tensor(rd, den, rd, ALU.max))
                V.reciprocal(st[:, 4 * h:4 * h + 4], st[:, 4 * h:4 * h + 4]).then_inc(s_rd, 1)
                dve.wait_ge(s_hf, 2 * (h + 1))
                for t in range(TT):
                    link(V.scalar_tensor_tensor(h_c[:, t, h * ML_DV:(h + 1) * ML_DV],
                                                bank(b + 1)[:, t * VE:t * VE + ML_DV],
                                                st[:, 4 * h + 2 + t:4 * h + 3 + t], tmp_c[:, h % 2, t],
                                                ALU.mult, ALU.add))
                dve.sem_inc(s_hb, 1)

            decay(0)
            for h in range(HEADS):
                weigh(h)
                if h + 1 < HEADS:
                    decay(h + 1)
                if h >= 1:
                    finish(h - 1)
            finish(HEADS - 1)
            dve.wait_ge(s_hsq, 1)
            link(V.reduce_sum(st[:, 80:96], sq[:, :].rearrange("p (g d) -> p g d", d=ML_DV), AX))
            V.tensor_scalar(st[:, 64:80], st[:, 80:96], 1.0 / ML_DV, EPS, ALU.mult, ALU.add).then_inc(s_hms, 1)
            dve.wait_ge(s_hrt, 1)
            link(V.reciprocal(st[:, 80:96], st[:, 64:80]))
            link(V.tensor_tensor(C["h"].rearrange("p (g d) -> p g d", d=ML_DV),
                                 C["h"].rearrange("p (g d) -> p g d", d=ML_DV),
                                 st[:, 80:96].unsqueeze(2).broadcast_to([P, 16, ML_DV]), ALU.mult))
            V.tensor_tensor(C["h"], C["h"], C["og"], ALU.mult).then_inc(s_hn, 1)
            for p in (1, 3):
                dve.wait_ge(s_hTp, p + 1)
                V.tensor_copy(mixT_c[:, 2 * p:2 * p + 2, :], bank(p).rearrange("p (c t) -> p c t", c=2)).then_inc(s_hTv, 1)
            out_proj("C", 6)

            moe("D", 1)

        @block.tensor
        def _(pe):
            def mm(out_, lhsT, rhs, start=True, stop=True):
                return nc.tensor.matmul(out_, lhsT, rhs, start=start, stop=stop)

            def norm_T(n):
                pe.wait_ge(s_xn, 2 * (n + 1))
                for p in range(4):
                    for c in range(2):
                        for t in range(TT):
                            k = 2 * p + c
                            last = nc.tensor.transpose(bank(p)[:, (2 * c + t) * P:(2 * c + t + 1) * P],
                                                       xn3[:, t, k * P:(k + 1) * P], ident)
                    last.then_inc(s_xTp, 1)
                pe.wait_ge(s_xTa, 2 * (n + 1))
                pe.wait_ge(s_xTv, 2 * (n + 1))

            def dense_block(ph, j, lhs, b0):
                pe.wait_ge(landed[ph][(first[ph] + j) % SLOTS], 16 * (j // SLOTS + 1))
                w = slot(first[ph] + j).rearrange("p (c n) -> p c n", c=DC)
                for t in range(TT):
                    for c in range(DC):
                        last = mm(bank(b0 + t), lhs[:, c, t * P:(t + 1) * P], w[:, c, :], c == 0, c == DC - 1)
                last.then_inc(used[ph], 1)

            def qk_T(ph, src):
                for p in range(4):
                    for c in range(2):
                        for t in range(TT):
                            k = 2 * p + c
                            last = nc.tensor.transpose(bank(p)[:, (2 * c + t) * P:(2 * c + t + 1) * P],
                                                       src[:, t, k * P:(k + 1) * P], ident)
                    last.then_inc(s_qTp[ph], 1)

            def moe(ph, l):
                s = ms[l]
                norm_T(2 * l + 1)
                pe.wait_ge(s_load["route"], 128)
                route = w_route[:, :].rearrange("p (l c n) -> p l c n", l=2, c=DC)
                for t in range(TT):
                    for c in range(DC):
                        last = mm(bank(0)[:, t * ROUTE:(t + 1) * ROUTE], xnT3[:, c, t * P:(t + 1) * P],
                                  route[:, l, c, :], c == 0, c == DC - 1)
                last.then_inc(s["logits"], 1)
                pe.wait_ge(s["mask"], 1)
                m3 = M["mask"].rearrange("p (t e) -> p t e", t=TT)
                mm(bank(1)[:, 0:32], tri, m3[:, 0])
                mm(bank(1)[:, 32:64], ones, m3[:, 0], True, False)
                mm(bank(1)[:, 32:64], tri, m3[:, 1], False, True)
                mm(bank(1)[:, 64:96], ones, m3[:, 0], True, False)
                mm(bank(1)[:, 64:96], ones, m3[:, 1], False, True).then_inc(s["rank"], 1)
                pe.wait_ge(s["rounds"], 1)
                extra = pe.value_load(extra_i[0:1, l:l + 1], min_val=0, max_val=QUADS * (MAX_ROUNDS - 1))
                with pe.Fori(0, extra + QUADS) as i:
                    n = pe.snap(i + 1)
                    n4 = pe.snap(i * 4 + 4)
                    pe.wait_ge(s["sel"], n4)
                    for c in range(DC):
                        for t in range(TT):
                            last = mm(bank(4 + c // 4)[:, (c % 4) * P:(c % 4 + 1) * P],
                                      xn3[:, t, c * P:(c + 1) * P], M["S"][:, t * P:(t + 1) * P],
                                      t == 0, t == TT - 1)
                    last.then_inc(s["disp"], 1)
                    pe.wait_ge(s["added"], i * 4 + 4)
                    for t in range(TT):
                        last = nc.tensor.transpose(bank(6)[:, t * P:(t + 1) * P], M["Gs"][:, t * P:(t + 1) * P], ident)
                    last.then_inc(s["gtp"], 1)
                    pe.wait_ge(s["dispc_a"], n)
                    pe.wait_ge(s["dispc_v"], n)
                    for j in range(ITEM):
                        pe.wait_ge(landed[ph][(first[ph] + j) % SLOTS], i * (ITEM // SLOTS * 32) + 32 * (j // SLOTS + 1))
                        w = slot(first[ph] + j).rearrange("p (e n) -> p e n", e=QUAD)
                        if j == GU_PIECES:
                            pe.wait_ge(s["h"], n4)
                            for k in range(FF // P):
                                last = nc.tensor.transpose(bank(7)[:, k * P:(k + 1) * P], M["h"][:, k * P:(k + 1) * P], ident)
                            last.then_inc(s["hTp"], 1)
                            pe.wait_ge(s["hTc"], n)
                        down = j >= GU_PIECES
                        k = j - GU_PIECES if down else j
                        lhs = hT_m if down else xT_m
                        for half in range(2):
                            for e in range(QUAD):
                                last = mm(psum[e * CAP:(e + 1) * CAP, 2 * down + half, :],
                                          lhs[:, k, e * CAP:(e + 1) * CAP],
                                          w[:, e, half * 512:(half + 1) * 512],
                                          k == 0, k == (DN_PIECES if down else GU_PIECES) - 1)
                        last.then_inc(used[ph], 1)
                    pe.wait_ge(s["gtc"], n)
                    pe.wait_ge(s["y_a"], n)
                    pe.wait_ge(s["y_v"], n)
                    for b, t, nb in COMB:
                        mm(bank(b), M["GT"][:, t * P:(t + 1) * P], M["y"][:, nb * 512:(nb + 1) * 512]).then_inc(s["comb"], 1)

            pe.wait_ge(s_load["cst"], 16)
            norm_T(0)
            for j in range(4):
                dense_block("A", j, xnT3, 2 * j)
            pe.wait_ge(s_load["lc0"], 16)
            pe.wait_ge(s_ua["A"], 4)
            pe.wait_ge(s_uv["A"], 4)
            for c in range(4):
                for t in range(TT):
                    last = mm(bank(4 + c), u_a[:, t, 1536 + c * P:1536 + (c + 1) * P], seqdft[:, t, :], t == 0, t == 1)
                last.then_inc(s_f1, 1)
            pe.wait_ge(s_qn, 2)
            qk_T("A", u_a)
            for c in range(4):
                pe.wait_ge(s_f1c, c + 1)
                mm(bank(4 + c)[:, 0:T], chdft[:, 0, :], AB[:, c, 0:T], True, False)
                mm(bank(4 + c)[:, 0:T], chdft[:, 1, :], AB[:, c, T:2 * T], False, True).then_inc(s_f2, 1)
            pe.wait_ge(s_qT["A"], 4)
            pe.wait_ge(s_biasm, 1)

            def scores(h):
                if h >= 2:
                    pe.wait_ge(s_ex, 2 * (h - 1))
                r = slice(64 * (h % 2), 64 * (h % 2) + 64)
                for t in range(TT):
                    o = bank(h % 2)[:, t * T:(t + 1) * T]
                    mm(o, qkT_a[r, h // 2, t * P:(t + 1) * P], qkT_a[r, 4 + h // 2, :], True, False)
                    last = mm(o, rev, bias_a[:, 2 - 2 * t:6 - 2 * t, h, :], False, True)
                last.then_inc(s_sc, 1)

            scores(0)
            scores(1)
            pe.wait_ge(s_f2c, 4)
            for h in range(HEADS):
                pe.wait_ge(s_pn, 2 * (h + 1))
                if h >= 2:
                    pe.wait_ge(s_pTc, h - 1)
                for kt in range(TT):
                    for qt in range(TT):
                        last = nc.tensor.transpose(bank(2 + h % 2)[:, kt * T + qt * P:kt * T + (qt + 1) * P],
                                                   P_a[:, h % 2, qt, kt * P:(kt + 1) * P], ident)
                last.then_inc(s_pT, 1)
                if h + 2 < HEADS:
                    scores(h + 2)
                pe.wait_ge(s_pTc, h + 1)
                hp = h // 2
                if h % 2 == 0 and hp >= 2:
                    pe.wait_ge(s_o, hp - 1)
                r = slice(64 * (h % 2), 64 * (h % 2) + 64)
                for kt in range(TT):
                    last = mm(psum[r, 6 + hp % 2, 0:T], u_a[:, kt, 1024 + 64 * h:1024 + 64 * (h + 1)],
                              PT_a[:, h % 2, kt * T:(kt + 1) * T], kt == 0, kt == TT - 1)
                last.then_inc(s_pv, 1)
            pe.wait_ge(s_o, HP)
            for nb in range(2):
                dense_block("A", 4 + nb, mixT_a, 2 * nb)

            moe("B", 0)

            norm_T(2)
            pe.wait_ge(s_load["gates"], 32)
            wg = w_gates[:, :].rearrange("p (c n) -> p c n", c=DC)
            for t in range(TT):
                for c in range(DC):
                    last = mm(bank(7)[:, t * 32:(t + 1) * 32], xnT3[:, c, t * P:(t + 1) * P], wg[:, c, :], c == 0, c == DC - 1)
            last.then_inc(s_gt, 1)
            for j in range(3):
                dense_block("C", j, xnT3, 2 * j)
            pe.wait_ge(s_gtk, 3)
            for j in range(4):
                for t in range(TT):
                    last = nc.tensor.transpose(bank(6 + j // 2)[0:8, (j % 2) * T + t * P:(j % 2) * T + (t + 1) * P],
                                               gtok[:, t, 8 * j:8 * j + 8], ident)
                if j % 2:
                    last.then_inc(s_gTp, 1)
            pe.wait_ge(s_em, 1)
            for j in range(3, 6):
                if j >= 4:
                    pe.wait_ge(s_ua["C"], j - 3)
                    pe.wait_ge(s_uv["C"], j - 3)
                dense_block("C", j, xnT3, 2 * (j % 4))
            pe.wait_ge(s_ua["C"], 6)
            pe.wait_ge(s_oex, 2)
            pe.wait_ge(s_uv["C"], 4)
            qk_T("C", qk_c)
            pe.wait_ge(s_eme, 1)
            for k, src in enumerate((a_c, E_c)):
                for d in range(2):
                    for t in range(TT):
                        o = ((k * 2 + d) * TT + t) * 8
                        last = nc.tensor.transpose(bank(7)[:, o:o + 8], src[:, d, t * P:(t + 1) * P], ident[0:8, 0:8])
            last.then_inc(s_aTp, 1)
            pe.wait_ge(s_qT["C"], 4)
            pe.wait_ge(s_load["lc1"], 16)

            def ml_scores(h):
                if h >= 2:
                    pe.wait_ge(s_ws, 2 * (h - 1))
                r = slice(64 * (h % 2), 64 * (h % 2) + 64)
                for st_ in range(TT):
                    last = mm(bank(h % 2)[:, st_ * T:(st_ + 1) * T], qkT_c[r, 4 + h // 2, st_ * P:(st_ + 1) * P],
                              qkT_c[r, h // 2, :])
                last.then_inc(s_st, 1)
                if h >= 2:
                    pe.wait_ge(s_dl, h - 1)
                mm(bank(2 + h % 2), sel_c[:, h, :], C["nM"][0:8, :]).then_inc(s_bc, 1)

            ml_scores(0)
            ml_scores(1)
            for h in range(HEADS):
                pe.wait_ge(s_ws, 2 * (h + 1))
                if h >= 2:
                    pe.wait_ge(s_hb, h - 1)
                w = W_c[:, h % 2]
                fb, bb = 4 + 2 * (h % 2), 5 + 2 * (h % 2)
                v = [ve[:, t, h, :] for t in range(TT)]
                if h == 0:
                    pe.wait_ge(s_qT["C"], 4)
                mm(bank(fb)[:, 0:VE], w[:, 0:P], v[0])
                mm(bank(fb)[:, VE:2 * VE], w[:, P:T], v[0], True, False)
                mm(bank(fb)[:, VE:2 * VE], w[:, 2 * T + P:3 * T], v[1], False, True)
                mm(bank(bb)[:, 0:VE], w[:, 2 * T:2 * T + P], v[0], True, False)
                mm(bank(bb)[:, 0:VE], w[:, T:T + P], v[1], False, True)
                mm(bank(bb)[:, VE:2 * VE], w[:, T + P:2 * T], v[1]).then_inc(s_nu, 1)
                if h + 2 < HEADS:
                    ml_scores(h + 2)
            pe.wait_ge(s_hn, 1)
            for p in range(4):
                for c in range(2):
                    for t in range(TT):
                        k = 2 * p + c
                        last = nc.tensor.transpose(bank(p)[:, (2 * c + t) * P:(2 * c + t + 1) * P],
                                                   h_c[:, t, k * P:(k + 1) * P], ident)
                last.then_inc(s_hTp, 1)
            pe.wait_ge(s_hTa, 2)
            pe.wait_ge(s_hTv, 2)
            for nb in range(2):
                dense_block("C", 6 + nb, mixT_c, 2 * nb)

            moe("D", 1)


_INS = ['x', 'ev_norm', 'ev_w_in', 'ev_q_gain', 'ev_k_gain', 'ev_rel_bias', 'ev_w_out',
        'od_norm', 'od_w_in', 'od_gate_bias', 'od_h_gain', 'od_w_out',
        'moe_norm', 'moe_w_rg', 'moe_b_rg', 'moe_w_re', 'moe_b_re', 'moe_w_gate', 'moe_w_up', 'moe_w_down']


def kernel(**inputs):
    import numpy as _np
    import concourse.bacc as _bacc
    from concourse import mybir as _mybir
    from concourse.bass_utils import run_bass_kernel_spmd as _run

    nc = _bacc.Bacc("TRN2", target_bir_lowering=False, num_devices=1)
    arrays, args = {}, {}
    given = {name: _np.ascontiguousarray(inputs[name]) for name in _INS}
    given.update(zip(("c_common", "c_layer0", "c_layer1"), shape_constants()))
    for name, arr in given.items():
        arrays[f"in_{name}"] = arr
        args[name] = nc.dram_tensor(f"in_{name}", arr.shape, _mybir.dt.from_np(arr.dtype), kind="ExternalInput").ap()
    out = nc.dram_tensor("out_0", (1, T, D), _mybir.dt.float32, kind="ExternalOutput").ap()
    build(nc, args, out)
    r = _run(nc, [arrays], core_ids=[0])
    return r.results[0]["out_0"]
```

```python
from contextlib import ExitStack

import numpy as np

import concourse.bass as bass
from concourse import mybir

P = 128
F32 = mybir.dt.float32
I32 = mybir.dt.int32
ALU = mybir.AluOpType
ACT = mybir.ActivationFunctionType
AX = mybir.AxisListType.X
ENG = mybir.EngineType

D = 1024
T = 256
TT = T // P
DC = D // P
EPS = 1e-6
GRID_W = 64

HEADS = 8
HP = HEADS // 2
NA_DH = 64
NA_WIN = 16
REL_R, REL_C = 15, 31
REL_SIZE = REL_R * REL_C
BIAS_ROWS = 6
ML_DV = 128
VE = ML_DV + 1

GROUPS, PER_GROUP, FF = 4, 8, 512
EXPERTS = GROUPS * PER_GROUP
ROUTE = GROUPS + EXPERTS
QUAD = 4
QUADS = EXPERTS // QUAD
CAP = P // QUAD
MAX_ROUNDS = T // CAP
GU_PIECES = D // P
DN_PIECES = FF // P
ITEM = GU_PIECES + DN_PIECES

SLOTS = 6
SLOT = 4096
EXTRA = 3
NEG = -1e30

G_EV, G_MOE0, G_OD, G_MOE1, G_HEADS = (DC * j for j in range(5))
G_NORM = (G_EV, G_MOE0, G_OD, G_MOE1)
G_ROWS = 5 * DC

C_IDENT = 0
C_TRI = C_IDENT + P
C_ONES = C_TRI + P
C_SLOTID = C_ONES + P
C_RANKW = C_SLOTID + T + CAP
C_THR = C_RANKW + EXPERTS
C_COMMON = C_THR + MAX_ROUNDS
C0_SEQ = 0
C0_CH = C0_SEQ + TT * 2 * T
C0_MASK = C0_CH + 2 * P
C0_SIZE = C0_MASK + GRID_W
C1_MASK = 0
C1_SEL = C1_MASK + 3 * T
C1_SIZE = C1_SEL + HEADS * P
C_LAYER = max(C0_SIZE, C1_SIZE)


def shape_constants():
    common = np.zeros((P, C_COMMON), np.float32)
    p = np.arange(P)
    common[:, C_IDENT:C_TRI] = np.eye(P)
    common[:, C_TRI:C_ONES] = p[:, None] < p[None, :]
    common[:, C_ONES:C_SLOTID] = 1.0
    common[:, C_SLOTID:C_RANKW] = np.arange(T + CAP)
    common[:, C_RANKW:C_THR] = EXPERTS - np.arange(EXPERTS)
    common[:, C_THR:C_COMMON] = CAP * np.arange(1, MAX_ROUNDS + 1) + 0.5

    l0 = np.zeros((P, C_LAYER), np.float32)
    t = np.arange(T)
    ang = 2 * np.pi * ((t[:, None] * t[None, :]) % T) / T
    norm = 1.0 / np.sqrt(T * 64)
    seq = np.concatenate([np.cos(ang), np.sin(ang)], axis=1) * norm
    l0[:, C0_SEQ:C0_CH] = seq.reshape(TT, P, 2 * T).transpose(1, 0, 2).reshape(P, -1)
    c = np.arange(64)
    ang = 2 * np.pi * ((c[:, None] * c[None, :]) % 64) / 64
    for j, m in enumerate((np.cos(ang), -np.sin(ang))):
        for g in range(2):
            o = C0_CH + j * P + 64 * g
            l0[64 * g:64 * g + 64, o:o + 64] = m
    qc = GRID_W - 1 - p % GRID_W
    lo = np.clip(qc - NA_WIN // 2, 0, GRID_W - NA_WIN)
    kc = np.arange(GRID_W)
    ok = (kc[None, :] >= lo[:, None]) & (kc[None, :] < lo[:, None] + NA_WIN)
    l0[:, C0_MASK:C0_SIZE] = np.where(ok, 0.0, NEG)

    l1 = np.zeros((P, C_LAYER), np.float32)
    s, tt = p[:, None], t[None, :]
    fw0 = np.where(tt >= s, 0.0, NEG)
    bw1 = np.where(tt <= s + P, 0.0, NEG)
    bw0 = np.where(tt[:, :P] <= s, 0.0, NEG)
    fw1 = np.where(tt[:, :P] >= s, 0.0, NEG)
    l1[:, C1_MASK:C1_SEL] = np.concatenate([fw0, bw1, bw0, fw1], axis=1)
    for h in range(HEADS):
        l1[h, C1_SEL + h * P:C1_SEL + (h + 1) * P] = 1.0
    return common, l0, l1


def build(nc, a, out):
    ctx = ExitStack()
    with ctx:
        def sb(name, width, dt=F32):
            return ctx.enter_context(nc.sbuf_tensor(name, [P, width], dt))

        def sem(name):
            return ctx.enter_context(nc.semaphore(name))

        ring = sb("ring", SLOTS * SLOT)
        x = sb("x", TT * D)
        xs = sb("xs", TT * D)
        scratch = sb("scratch", SLOT)
        xnT = scratch[:, 0:DC * T]
        sq = scratch[:, DC * T:SLOT]
        g_rows = sb("g_rows", P)
        g_cols = sb("g_cols", G_ROWS)
        cst = sb("cst", C_COMMON)
        lcst = sb("lcst", C_LAYER)
        w_route = sb("w_route", 2 * DC * ROUTE)
        b_route = sb("b_route", 2 * ROUTE)
        w_gates = sb("w_gates", DC * 32)
        b_gates = sb("b_gates", 32)
        small = sb("small", 128)
        extra_i = sb("items_i", 8, I32)
        PHASE = 5600 + 2 * SLOT + 2500
        phase = sb("phase", PHASE)
        psum = ctx.enter_context(nc.psum_tensor("psum", [P, 8, 512], F32))

        def carve(sizes):
            at, views = 0, {}
            for name, n in sizes:
                views[name] = phase[:, at:at + n]
                at += n
            assert at <= PHASE, at
            return views

        x3 = x[:, :].rearrange("p (t d) -> p t d", t=TT)
        xs3 = xs[:, :].rearrange("p (t d) -> p t d", t=TT)
        xnT3 = xnT[:, :].rearrange("p (c t) -> p c t", c=DC)
        ident = cst[:, C_IDENT:C_TRI]
        tri = cst[:, C_TRI:C_ONES]
        ones = cst[:, C_ONES:C_SLOTID]
        slotid = cst[:, C_SLOTID:C_RANKW]
        rankw = cst[:, C_RANKW:C_THR]
        thr = cst[:, C_THR:C_COMMON]

        def slot(n):
            return ring[:, (n % SLOTS) * SLOT:(n % SLOTS + 1) * SLOT]

        def bank(b):
            return psum[:, b, :]

        def mbank(b):
            return psum[:, (b + 4) % 8, :]

        n_a = 4 + 2
        n_c = 6 + 2
        first = {"A": 0, "B": n_a, "C": n_a + QUADS * ITEM - EXTRA,
                 "D": n_a + QUADS * ITEM - EXTRA + n_c}
        assert ITEM % SLOTS == 0 and GU_PIECES + 1 >= SLOTS + EXTRA - 2
        ORDER_C = (0, 1, 4, 5, 2, 3)
        BANK_C = (0, 2, 4, 6, 4, 6)

        def ring_turn(i, j):
            if isinstance(i, int) and i == 0:
                return j if j < SLOTS else None if j < SLOTS + EXTRA else j - EXTRA
            return j - EXTRA

        landed = {ph: [sem(f"landed_{ph}{s}") for s in range(SLOTS)] for ph in "ABCD"}
        used = {ph: sem(f"used_{ph}") for ph in "ABCD"}

        landed_x = {ph: [sem(f"landed_{ph}_extra{s}") for s in range(EXTRA)] for ph in "BD"}

        def dense_source(ph, j):
            w_in, w_out, order = ((a["ev_w_in"], a["ev_w_out"], range(4)) if ph == "A"
                                  else (a["od_w_in"], a["od_w_out"], ORDER_C))
            w, b = (w_in, order[j]) if j < len(order) else (w_out, j - len(order))
            return w[0, :, b * 512:(b + 1) * 512].rearrange("(c p) n -> p c n", p=P)

        def piece(ph, i, j):
            turn = ring_turn(i, j)
            if turn is None:
                k = j - SLOTS
                at = scratch[:, :] if k == 2 else phase[:, 5600 + k * SLOT:5600 + (k + 1) * SLOT]
                return at, landed_x[ph][k], 32
            return (slot(first[ph] + turn), landed[ph][(first[ph] + turn) % SLOTS],
                    i * (ITEM // SLOTS * 32) + 32 * (turn // SLOTS + 1))

        s_load = {n: sem(f"loaded_{n}") for n in
                  ("x", "cst", "lc0", "lc1", "bias", "qkgain", "gains", "route", "gates")}
        s_gr = sem("gains_in_psum")
        s_gc = sem("gains_copied")
        s_x = sem("x_ready")
        s_ssq = sem("squares_summed")
        s_ms = sem("mean_square_ready")
        s_rt = sem("root_ready")
        s_rs = sem("inv_rms_ready")
        s_xTp = sem("xnT_in_psum")
        s_xTv = sem("xnT_copied")
        dvc = sem("dve_chain")
        s_out = sem("out_stored")
        s_free = sem("slot_seen_free")

        s_biasm = sem("bias_masked")
        s_ua = {ph: sem(f"u_copied_act_{ph}") for ph in "AC"}
        s_uv = {ph: sem(f"u_copied_dve_{ph}") for ph in "AC"}
        s_qsq = sem("qk_squared")
        s_qms = sem("qk_mean_square")
        s_qrt = sem("qk_root")
        s_qn = sem("qk_normed")
        s_qTp = {ph: sem(f"qkT_in_psum_{ph}") for ph in "AC"}
        s_qT = {ph: sem(f"qkT_copied_{ph}") for ph in "AC"}
        s_f1 = sem("seq_dft_done")
        s_f1c = sem("seq_dft_copied")
        s_f2 = sem("ch_dft_done")
        s_f2c = sem("ch_dft_copied")
        s_sc = sem("scores_done")
        s_mx = sem("max_ready")
        s_ex = sem("exp_done")
        s_rl = sem("inv_sum_ready")
        s_pn = sem("probs_normed")
        s_pT = sem("probsT_in_psum")
        s_pTc = sem("probsT_copied")
        s_pv = sem("pv_done")
        s_o = sem("attn_copied")

        def moe_sems(l):
            return {n: sem(f"{n}_{l}") for n in
                    ("scaled", "logits", "gsub", "gexp", "esub", "eexp", "mask", "rank", "routed", "rounds",
                     "sel", "disp", "dispc_a", "dispc_v", "gtp", "gtc", "silu", "h", "hTp",
                     "hTc", "y_a", "y_v", "comb", "added")}

        ms = [moe_sems(0), moe_sems(1)]

        s_gt = sem("gates_done")
        s_gab = sem("gate_abs_ready")
        s_gex = sem("gate_exp_ready")
        s_gp1 = sem("gate_exp1_ready")
        s_gln = sem("gate_log_ready")
        s_gtk = sem("gates_token_major")
        s_gTp = sem("gatesT_in_psum")
        s_em = sem("neg_m_ready")
        s_eme = sem("exp_neg_m_ready")
        s_gTc = sem("gatesT_copied")
        s_aTp = sem("aT_in_psum")
        s_aT = sem("aT_copied")
        s_og = sem("o_gate_ready")
        s_st = sem("st_done")
        s_bc = sem("m_broadcast")
        s_dl = sem("decay_log_ready")
        s_w = sem("decay_exp_ready")
        s_ws = sem("weighted_scores")
        s_nu = sem("num_done")
        s_rd = sem("inv_den_ready")
        s_hf = sem("h_fw_ready")
        s_hb = sem("h_ready")
        s_hsq = sem("h_squared")
        s_hms = sem("h_mean_square")
        s_hrt = sem("h_root")
        s_hn = sem("h_normed")
        s_hTp = sem("hT_in_psum")
        s_hTa = sem("hT_copied")

        A = carve([("mixT", DC * T), ("u", TT * 2048), ("qkT", 8 * T),
                   ("bias", BIAS_ROWS * HEADS * GRID_W), ("P", 4 * TT * T), ("PT", 2 * TT * T), ("st", 160)])
        C = carve([("qk", TT * 1024), ("ve", TT * HEADS * VE), ("og", TT * D), ("qkT", 8 * T),
                   ("W", 2 * 3 * T), ("h", TT * D), ("tmp", 2 * TT * P), ("gtok", TT * 32),
                   ("gw", 3 * TT * 16), ("gT", 4 * T), ("F", 2 * T), ("a", 2 * T), ("nM", 2 * T),
                   ("E", 2 * T), ("aT", 64), ("st", 160)])
        M = carve([("L", TT * ROUTE), ("work", 8 * TT * EXPERTS), ("oh", 2 * TT * EXPERTS),
                   ("mask", TT * EXPERTS), ("G", TT * EXPERTS), ("rank", TT * EXPERTS), ("st", 64),
                   ("S", TT * P), ("Gs", TT * P), ("xT", DC * P), ("GT", TT * P), ("sg", FF),
                   ("h", FF), ("hT", FF), ("y", D)])
        assert sum(v.shape[1] for v in M.values()) <= 5600

        u_a = A["u"].rearrange("p (t n) -> p t n", t=TT)
        qkT_a = A["qkT"].rearrange("p (c t) -> p c t", c=8)
        bias_a = A["bias"].rearrange("p (r h k) -> p r h k", r=BIAS_ROWS, h=HEADS)
        P_a = A["P"].rearrange("p (b t k) -> p b t k", b=4, t=TT)
        PT_a = A["PT"].rearrange("p (b n) -> p b n", b=2)
        mixT_a = A["mixT"].rearrange("p (c t) -> p c t", c=DC)
        AB = xs[:, :].rearrange("p (c n) -> p c n", c=4)
        seqdft = lcst[:, C0_SEQ:C0_CH].rearrange("p (t n) -> p t n", t=TT)
        chdft = lcst[:, C0_CH:C0_MASK].rearrange("p (j n) -> p j n", j=2)
        namask = lcst[:, C0_MASK:C0_SIZE]

        qk_c = C["qk"].rearrange("p (t n) -> p t n", t=TT)
        ve = C["ve"].rearrange("p (t h e) -> p t h e", t=TT, h=HEADS)
        og = C["og"].rearrange("p (t n) -> p t n", t=TT)
        qkT_c = C["qkT"].rearrange("p (c t) -> p c t", c=8)
        W_c = C["W"].rearrange("p (b n) -> p b n", b=2)
        h_c = C["h"].rearrange("p (t n) -> p t n", t=TT)
        tmp_c = C["tmp"].rearrange("p (b t n) -> p b t n", b=2, t=TT)
        gtok = C["gtok"].rearrange("p (t n) -> p t n", t=TT)
        gw = C["gw"].rearrange("p (j t d h) -> p j t d h", j=3, t=TT, d=2)
        gT = C["gT"][0:8, :].rearrange("p (j t) -> p j t", j=4)
        F_c = C["F"][0:8, :].rearrange("p (d t) -> p d t", d=2)
        a_c = C["a"][0:8, :].rearrange("p (d t) -> p d t", d=2)
        nM = C["nM"][0:8, :].rearrange("p (d t) -> p d t", d=2)
        E_c = C["E"][0:8, :].rearrange("p (d t) -> p d t", d=2)
        aT = C["aT"].rearrange("p (k d t h) -> p k d t h", k=2, d=2, t=TT)
        mixT_c = C["qk"].rearrange("p (c t) -> p c t", c=DC)
        mlmask = lcst[:, C1_MASK:C1_SEL]
        sel_c = lcst[0:8, C1_SEL:C1_SIZE].rearrange("p (h n) -> p h n", h=HEADS)

        L3 = M["L"].rearrange("p (t n) -> p t n", t=TT)
        S_m = M["S"].rearrange("p (t e s) -> p t e s", t=TT, e=QUAD)
        Gs_m = M["Gs"].rearrange("p (t e s) -> p t e s", t=TT, e=QUAD)
        xT_m = M["xT"].rearrange("p (c s) -> p c s", c=DC)
        hT_m = M["hT"].rearrange("p (c s) -> p c s", c=FF // P)
        rk3 = M["rank"].rearrange("p (t e) -> p t e", t=TT)
        G3 = M["G"].rearrange("p (t e) -> p t e", t=TT)
        COMB = ((0, 0, 0), (1, 0, 1), (6, 1, 0), (7, 1, 1))

        block = ctx.enter_context(nc.Block())

        @block.sync
        def _(sp):
            for t in range(TT):
                sp.dma_start(x3[:, t], a["x"][0, t * P:(t + 1) * P, :]).then_inc(s_load["x"], 16)

            def slot_free(count, value):
                sp.wait_ge(count, value)
                sp.sem_inc(s_free, 1)

            def expert_piece(ph, l, i, j, q):
                at, done, _ = piece(ph, i, j)
                dst = at.rearrange("p (e n) -> p e n", e=QUAD)
                if j < GU_PIECES:
                    for k, name in enumerate(("moe_w_gate", "moe_w_up")):
                        src = a[name][l, bass.ds(q * QUAD, QUAD), j * P:(j + 1) * P, :]
                        sp.dma_start(dst[:, :, k * FF:(k + 1) * FF],
                                     src.rearrange("e p f -> p e f")).then_inc(done, 16)
                else:
                    k = j - GU_PIECES
                    for half in range(2):
                        src = a["moe_w_down"][l, bass.ds(q * QUAD + 2 * half, 2), k * P:(k + 1) * P, :]
                        sp.dma_start(dst[:, 2 * half:2 * half + 2, :],
                                     src.rearrange("e p f -> p e f")).then_inc(done, 16)

            def dense(ph, prev, extra):
                for j in range(n_a if ph == "A" else n_c):
                    if j >= SLOTS:
                        sp.wait_ge(used[ph], j - SLOTS + 1)
                    elif prev is not None:
                        sp.wait_ge(used[prev], extra * ITEM + (QUADS * ITEM - SLOTS + 1 + j))
                    dst = slot(first[ph] + j).rearrange("p (c n) -> p c n", c=DC)
                    sp.dma_start(dst, dense_source(ph, j)).then_inc(
                        landed[ph][(first[ph] + j) % SLOTS], 16)

            def moe(ph, l, prev, n_prev):
                for j in range(ITEM):
                    turn = ring_turn(0, j)
                    if turn is None:
                        if j == SLOTS + EXTRA - 1:
                            sp.wait_ge(ms[l]["logits"], 1)
                        elif l == 0:
                            sp.wait_ge(s_o, HP)
                        else:
                            sp.wait_ge(s_hTa, DC)
                    elif turn < SLOTS:
                        sp.wait_ge(used[prev], n_prev - SLOTS + 1 + turn)
                    else:
                        sp.wait_ge(used[ph], turn - SLOTS + 1)
                    expert_piece(ph, l, 0, j, 0)
                sp.wait_ge(ms[l]["rounds"], 1)
                extra = sp.value_load(extra_i[0:1, l:l + 1], min_val=0, max_val=QUADS * (MAX_ROUNDS - 1))
                with sp.Fori(1, extra + QUADS) as i:
                    q = sp.snap(i % QUADS)
                    for j in range(ITEM):
                        slot_free(used[ph], i * ITEM + (j - SLOTS + 1))
                        expert_piece(ph, l, i, j, q)
                return extra

            dense("A", None, 0)
            extra = moe("B", 0, "A", n_a)
            dense("C", "B", extra)
            extra = moe("D", 1, "C", n_c)
            for k, (_, t, nb) in enumerate(COMB):
                slot_free(ms[1]["added"], extra * 4 + (4 * QUADS - 4 + k + 1))
                sp.dma_start(out[0, t * P:(t + 1) * P, nb * 512:(nb + 1) * 512],
                             x3[:, t, nb * 512:(nb + 1) * 512]).then_inc(s_out, 16)
            sp.wait_ge(s_out, 64)

        @block.gpsimd
        def _(pool):
            def bcast(row, n):
                return row.rearrange("(o n) -> o n", o=1).broadcast_to([P, n])

            for r in range(2):
                for k in range(BIAS_ROWS):
                    base = (k + 5 - r) * REL_C + (REL_C // 2 - (GRID_W - 1))
                    src = bass.AP(tensor=a["ev_rel_bias"].tensor, offset=base,
                                  ap=[[1, GRID_W], [REL_SIZE, HEADS], [1, GRID_W]])
                    pool.dma_start(bias_a[GRID_W * r:GRID_W * (r + 1), k], src).then_inc(s_load["bias"], 16)
            pool.wait_ge(s_load["bias"], 16 * 2 * BIAS_ROWS)
            pool.wait_ge(s_load["lc0"], 16)
            every = A["bias"].rearrange("p (n k) -> p n k", k=GRID_W)
            pool.tensor_tensor(every, every, namask.unsqueeze(1).broadcast_to([P, BIAS_ROWS * HEADS, GRID_W]),
                               ALU.add).then_inc(s_biasm, 1)
            route = w_route[:, :].rearrange("p (l c n) -> p l c n", l=2, c=DC)
            for l in range(2):
                pool.dma_start(route[:, l, :, 0:GROUPS],
                               a["moe_w_rg"][l].rearrange("(c p) n -> p c n", p=P)).then_inc(s_load["route"], 16)
                pool.dma_start(route[:, l, :, GROUPS:ROUTE],
                               a["moe_w_re"][l].rearrange("(c p) n -> p c n", p=P)).then_inc(s_load["route"], 16)
                pool.dma_start(b_route[:, l * ROUTE:l * ROUTE + GROUPS],
                               bcast(a["moe_b_rg"][l], GROUPS)).then_inc(s_load["route"], 16)
                pool.dma_start(b_route[:, l * ROUTE + GROUPS:(l + 1) * ROUTE],
                               bcast(a["moe_b_re"][l], EXPERTS)).then_inc(s_load["route"], 16)
            pool.dma_start(w_gates[:, :].rearrange("p (c n) -> p c n", c=DC),
                           a["od_w_in"][0, :, 3072:3104].rearrange("(c p) n -> p c n", p=P)).then_inc(s_load["gates"], 16)
            pool.dma_start(b_gates[:, :], bcast(a["od_gate_bias"][0], 32)).then_inc(s_load["gates"], 16)
            for h in range(HEADS):
                pool.wait_ge(s_rl, h + 1)
                for t in range(TT):
                    pool.tensor_scalar(P_a[:, h % 4, t], P_a[:, h % 4, t],
                                       A["st"][:, 64 + 2 * h + t:65 + 2 * h + t], None, ALU.mult).then_inc(s_pn, 1)
            pool.wait_ge(used["A"], n_a)
            pool.dma_start(lcst[:, :], a["c_layer1"]).then_inc(s_load["lc1"], 16)

        @block.scalar
        def _(act):
            gains = ((G_EV, a["ev_norm"][0]), (G_MOE0, a["moe_norm"][0]), (G_OD, a["od_norm"][0]),
                     (G_MOE1, a["moe_norm"][1]), (G_HEADS, a["od_h_gain"][0]))
            for g, row in gains:
                act.dma_start(g_rows[g:g + DC, :], row.rearrange("(c p) -> c p", p=P)).then_inc(s_load["gains"], 16)
            act.dma_start(cst[:, :], a["c_common"]).then_inc(s_load["cst"], 16)
            for k, name in enumerate(("ev_q_gain", "ev_k_gain")):
                for half in range(2):
                    act.dma_start(small[64 * half:64 * half + 64, k:k + 1],
                                  a[name].rearrange("o d -> d o")).then_inc(s_load["qkgain"], 16)
            act.dma_start(lcst[:, :], a["c_layer0"]).then_inc(s_load["lc0"], 16)

            def norm(n):
                if n == 0:
                    act.wait_ge(s_load["x"], 32)
                else:
                    act.wait_ge(s_x, n)
                for t in range(TT):
                    nc.scalar.activation(sq[:, t * D:(t + 1) * D], x3[:, t], ACT.Square,
                                         accum_out=small[:, 8 + t:9 + t]).then_inc(s_ssq, 1)
                act.wait_ge(s_ms, n + 1)
                nc.scalar.activation(small[:, 12:14], small[:, 10:12], ACT.Sqrt).then_inc(s_rt, 1)
                act.wait_ge(s_rs, n + 1)

            def inv_rms(t):
                return small[:, 14 + t:15 + t]

            def moe(ph, l):
                s = ms[l]
                norm(2 * l + 1)
                for t in range(TT):
                    nc.scalar.activation(xs3[:, t], x3[:, t], ACT.Copy, scale=inv_rms(t)).then_inc(s["scaled"], 1)
                act.wait_ge(s["gsub"], 1)
                nc.scalar.activation(M["st"][:, 0:8], M["st"][:, 0:8], ACT.Exp).then_inc(s["gexp"], 1)
                act.wait_ge(s["esub"], 1)
                nc.scalar.activation(M["st"][:, 20:22], M["st"][:, 20:22], ACT.Exp).then_inc(s["eexp"], 1)

                def item(i):
                    n = i + 1 if isinstance(i, int) else act.snap(i + 1)
                    act.wait_ge(s["disp"], n)
                    for c in range(4):
                        g = G_NORM[2 * l + 1] + c
                        nc.scalar.activation(xT_m[:, c], bank(4)[:, c * P:(c + 1) * P], ACT.Copy,
                                             scale=g_cols[:, g:g + 1]).then_inc(s["dispc_a"], 1)
                    act.wait_ge(s["gtp"], n)
                    nc.scalar.copy(M["GT"], bank(6)[:, 0:T]).then_inc(s["gtc"], 1)
                    act.wait_ge(used[ph], i * ITEM + GU_PIECES)
                    nc.scalar.activation(M["sg"], bank(0), ACT.Silu).then_inc(s["silu"], 1)
                    act.wait_ge(s["hTp"], n)
                    nc.scalar.copy(M["hT"], bank(7)).then_inc(s["hTc"], 1)
                    act.wait_ge(used[ph], i * ITEM + ITEM)
                    nc.scalar.copy(M["y"][:, 0:512], bank(2)).then_inc(s["y_a"], 1)

                item(0)
                act.wait_ge(s["rounds"], 1)
                extra = act.value_load(extra_i[0:1, l:l + 1], min_val=0, max_val=QUADS * (MAX_ROUNDS - 1))
                with act.Fori(1, extra + QUADS) as i:
                    item(i)

            norm(0)
            for b in range(4):
                act.wait_ge(used["A"], b + 1)
                nc.scalar.activation(u_a[:, 0, b * 512:(b + 1) * 512], mbank(2 * b), ACT.Copy,
                                     scale=inv_rms(0)).then_inc(s_ua["A"], 1)
                if b == 1:
                    act.wait_ge(s_ua["A"], 2)
                    act.wait_ge(s_uv["A"], 2)
                    nc.scalar.activation(sq.rearrange("p (t n) -> p t n", t=TT), u_a[:, :, 0:1024],
                                         ACT.Square).then_inc(s_qsq, 1)
                    act.wait_ge(s_qms, 1)
                    nc.scalar.activation(A["st"][:, 0:32], A["st"][:, 0:32], ACT.Sqrt).then_inc(s_qrt, 1)

            def exp_scores(h):
                act.wait_ge(s_mx, h + 1)
                for t in range(TT):
                    nc.scalar.activation(P_a[:, h % 4, t], P_a[:, h % 4, t], ACT.Exp,
                                         bias=A["st"][:, 80 + 2 * h + t:81 + 2 * h + t],
                                         accum_out=A["st"][:, 100 + 2 * h + t:101 + 2 * h + t]).then_inc(s_ex, 1)

            exp_scores(0)
            exp_scores(1)
            for c in range(4):
                act.wait_ge(s_f1, c + 1)
                nc.scalar.copy(AB[:, c], mbank(4 + c)).then_inc(s_f1c, 1)
            exp_scores(2)
            exp_scores(3)
            for c in range(4):
                act.wait_ge(s_f2, c + 1)
                nc.scalar.copy(mixT_a[:, 4 + c], mbank(4 + c)[:, 0:T]).then_inc(s_f2c, 1)
            for h in range(4, HEADS):
                exp_scores(h)

            moe("B", 0)

            norm(2)
            act.wait_ge(s_gab, 1)
            nc.scalar.activation(gw[:, 1], gw[:, 0], ACT.Exp, scale=-1.0).then_inc(s_gex, 1)
            act.wait_ge(s_gp1, 1)
            nc.scalar.activation(gw[:, 1], gw[:, 1], ACT.Ln).then_inc(s_gln, 1)
            for j, b in enumerate(ORDER_C):
                act.wait_ge(used["C"], j + 1)
                src = mbank(BANK_C[j])
                if b < 2:
                    nc.scalar.activation(qk_c[:, 0, b * 512:(b + 1) * 512], src, ACT.Copy,
                                         scale=inv_rms(0)).then_inc(s_ua["C"], 1)
                elif b < 4:
                    nc.scalar.activation(ve[:, 0, 4 * (b - 2):4 * (b - 1), 0:ML_DV],
                                         src.rearrange("p (h e) -> p h e", h=4), ACT.Copy,
                                         scale=inv_rms(0)).then_inc(s_ua["C"], 1)
                else:
                    for t in range(TT):
                        nc.scalar.activation(og[:, t, (b - 4) * 512:(b - 3) * 512],
                                             mbank(BANK_C[j] + t), ACT.Sigmoid, scale=inv_rms(t)).then_inc(s_og, 1)
                if j == 1:
                    act.wait_ge(s_em, 1)
                    nc.scalar.activation(E_c, F_c, ACT.Exp).then_inc(s_eme, 1)

            def decay_exp(h):
                act.wait_ge(s_dl, h + 1)
                nc.scalar.activation(W_c[:, h % 2], W_c[:, h % 2], ACT.Exp).then_inc(s_w, 1)

            def h_squares(h):
                act.wait_ge(s_hb, h + 1)
                for t in range(TT):
                    nc.scalar.activation(sq[:, (2 * h + t) * P:(2 * h + t + 1) * P], h_c[:, t, h * ML_DV:(h + 1) * ML_DV],
                                         ACT.Square, accum_out=C["st"][:, 64 + 8 * t + h:65 + 8 * t + h]).then_inc(s_hsq, 1)

            for h in range(HEADS + 1):
                if h < HEADS:
                    decay_exp(h)
                if h >= 1:
                    g = h - 1
                    act.wait_ge(s_rd, g + 1)
                    if g >= 2:
                        act.wait_ge(s_hb, g - 1)
                    for t in range(TT):
                        nc.scalar.activation(tmp_c[:, g % 2, t], mbank(4 + 2 * (g % 2))[:, t * VE:t * VE + ML_DV],
                                             ACT.Copy, scale=C["st"][:, 4 * g + t:4 * g + t + 1]).then_inc(s_hf, 1)
                if h >= 2:
                    h_squares(h - 2)
            h_squares(HEADS - 1)
            act.wait_ge(s_hms, 1)
            nc.scalar.activation(C["st"][:, 80:96], C["st"][:, 80:96], ACT.Sqrt).then_inc(s_hrt, 1)
            for p in range(4):
                act.wait_ge(s_hTp, p + 1)
                for k in range(2):
                    g = G_HEADS + 2 * p + k
                    nc.scalar.activation(mixT_c[:, 2 * p + k, :], bank(p)[:, k * T:(k + 1) * T], ACT.Copy,
                                         scale=g_cols[:, g:g + 1]).then_inc(s_hTa, 1)

            moe("D", 1)

        @block.vector
        def _(dve):
            V = nc.vector
            chain = [0]

            def join(n):
                chain[0] += n
                dve.wait_ge(dvc, chain[0])

            def link(ins):
                ins.then_inc(dvc, 1)
                join(1)

            def norm(n):
                def copy_bank(p):
                    dve.wait_ge(s_xTp, 4 * n + p + 1)
                    for k in range(2):
                        c = 2 * p + k
                        g = G_NORM[n] + c
                        V.tensor_scalar(xnT3[:, c, :], bank(p)[:, k * T:(k + 1) * T], g_cols[:, g:g + 1],
                                        None, ALU.mult).then_inc(s_xTv, 1)

                copy_bank(0)
                copy_bank(1)
                dve.wait_ge(s_ssq, 2 * (n + 1))
                V.tensor_scalar(small[:, 10:12], small[:, 8:10], 1.0 / D, EPS, ALU.mult, ALU.add).then_inc(s_ms, 1)
                copy_bank(2)
                copy_bank(3)
                dve.wait_ge(s_rt, n + 1)
                V.reciprocal(small[:, 14:16], small[:, 12:14]).then_inc(s_rs, 1)
                dve.wait_ge(s_rs, n + 1)

            def inv_rms(t):
                return small[:, 14 + t:15 + t]

            def out_proj(ph, b0):
                for nb in range(2):
                    dve.wait_ge(used[ph], b0 + nb + 1)
                    for t in range(TT):
                        dst = x3[:, t, nb * 512:(nb + 1) * 512]
                        V.tensor_tensor(dst, dst, bank(4 + 2 * nb + t), ALU.add).then_inc(dvc, 1)
                join(4)
                dve.sem_inc(s_x, 1)

            def moe(ph, l):
                s = ms[l]
                st = M["st"]
                norm(2 * l + 1)
                dve.wait_ge(s_load["route"], 128)
                dve.wait_ge(s["logits"], 1)
                for t in range(TT):
                    V.scalar_tensor_tensor(L3[:, t], bank(4)[:, t * ROUTE:(t + 1) * ROUTE], inv_rms(t),
                                           b_route[:, l * ROUTE:(l + 1) * ROUTE], ALU.mult, ALU.add).then_inc(dvc, 1)
                join(2)
                lg = L3[:, :, 0:GROUPS]
                gm = st[:, 8:10]
                link(V.reduce_max(gm, lg, AX))
                gmb = gm.unsqueeze(2).broadcast_to([P, TT, GROUPS])
                ge = st[:, 0:8].rearrange("p (t g) -> p t g", t=TT)
                V.tensor_tensor(ge, lg, gmb, ALU.subtract).then_inc(s["gsub"], 1)
                w = [M["work"][:, j * 64:(j + 1) * 64] for j in range(8)]
                g1 = w[0][:, 0:8].rearrange("p (t g) -> p t g", t=TT)
                g2 = w[1][:, 0:8].rearrange("p (t g) -> p t g", t=TT)
                order4 = rankw[:, 0:GROUPS].unsqueeze(1).broadcast_to([P, TT, GROUPS])
                link(V.tensor_tensor(g1, lg, gmb, ALU.is_equal))
                link(V.tensor_tensor(g2, g1, order4, ALU.mult))
                link(V.reduce_max(st[:, 10:12], g2, AX))
                link(V.tensor_tensor(g1, g2, st[:, 10:12].unsqueeze(2).broadcast_to([P, TT, GROUPS]), ALU.is_equal))
                link(V.tensor_scalar(g2, g1, -NEG, NEG, ALU.mult, ALU.add))
                w4 = [v.rearrange("p (t g e) -> p t g e", t=TT, g=GROUPS) for v in w]
                w3 = [v.rearrange("p (t e) -> p t e", t=TT) for v in w]
                for t in range(TT):
                    le = L3[:, t, GROUPS:ROUTE].rearrange("p (g e) -> p g e", g=GROUPS)
                    V.tensor_tensor(w4[2][:, t], le, g2[:, t].unsqueeze(2).broadcast_to([P, GROUPS, PER_GROUP]),
                                    ALU.add).then_inc(dvc, 1)
                join(2)
                order = rankw.unsqueeze(1).broadcast_to([P, TT, EXPERTS])
                oh = [M["oh"][:, j * 64:(j + 1) * 64].rearrange("p (t e) -> p t e", t=TT) for j in range(2)]

                def top(src, vmax, j):
                    link(V.reduce_max(vmax, src, AX))
                    link(V.tensor_tensor(w3[3], src, vmax.unsqueeze(2).broadcast_to([P, TT, EXPERTS]), ALU.is_equal))
                    link(V.tensor_tensor(w3[4], w3[3], order, ALU.mult))
                    link(V.reduce_max(st[:, 12:14], w3[4], AX))
                    link(V.tensor_tensor(oh[j], w3[4], st[:, 12:14].unsqueeze(2).broadcast_to([P, TT, EXPERTS]), ALU.is_equal))

                top(w3[2], st[:, 16:18], 0)
                link(V.scalar_tensor_tensor(w3[5], oh[0], NEG, w3[2], ALU.mult, ALU.add))
                top(w3[5], st[:, 18:20], 1)
                m3 = M["mask"].rearrange("p (t e) -> p t e", t=TT)
                V.tensor_tensor(m3, oh[0], oh[1], ALU.add).then_inc(s["mask"], 1)
                V.tensor_tensor(st[:, 20:22], st[:, 18:20], st[:, 16:18], ALU.subtract).then_inc(s["esub"], 1)
                dve.wait_ge(s["mask"], 1)
                link(V.tensor_scalar(w3[6], m3, 1e4, -1e4, ALU.mult, ALU.add))
                dve.wait_ge(s["rank"], 1)
                link(V.tensor_tensor(rk3, bank(5)[:, 0:64].rearrange("p (t e) -> p t e", t=TT), w3[6], ALU.add))

                def select(q4, first_slot):
                    sid = slotid[:, bass.ds(first_slot, CAP)].unsqueeze(1).broadcast_to([P, QUAD, CAP])
                    for t in range(TT):
                        V.tensor_tensor(S_m[:, t], rk3[:, t, bass.ds(q4, QUAD)].unsqueeze(2).broadcast_to([P, QUAD, CAP]),
                                        sid, ALU.is_equal).then_inc(s["sel"], 1)

                def select_gates(q4, count):
                    dve.wait_ge(s["sel"], count)
                    for t in range(TT):
                        V.tensor_tensor(Gs_m[:, t], S_m[:, t],
                                        G3[:, t, bass.ds(q4, QUAD)].unsqueeze(2).broadcast_to([P, QUAD, CAP]),
                                        ALU.mult).then_inc(s["sel"], 1)

                select(0, 0)
                dve.wait_ge(s["gexp"], 1)
                link(V.reduce_sum(st[:, 22:24], ge, AX))
                dve.wait_ge(s["eexp"], 1)
                link(V.tensor_scalar(st[:, 24:26], st[:, 20:22], 1.0, None, ALU.add))
                link(V.tensor_tensor(st[:, 24:26], st[:, 24:26], st[:, 22:24], ALU.mult))
                link(V.reciprocal(st[:, 26:28], st[:, 24:26]))
                link(V.tensor_tensor(st[:, 28:30], st[:, 26:28], st[:, 20:22], ALU.mult))
                V.tensor_tensor(w3[6], oh[0], st[:, 26:28].unsqueeze(2).broadcast_to([P, TT, EXPERTS]), ALU.mult).then_inc(dvc, 1)
                V.tensor_tensor(w3[7], oh[1], st[:, 28:30].unsqueeze(2).broadcast_to([P, TT, EXPERTS]), ALU.mult).then_inc(dvc, 1)
                join(2)
                link(V.tensor_tensor(G3, w3[6], w3[7], ALU.add))
                select_gates(0, 2)
                link(V.reduce_max(st[:, 30:31], bank(5)[:, 64:96], AX))
                link(V.tensor_tensor(st[:, 32:40], thr, st[:, 30:31].broadcast_to([P, MAX_ROUNDS]), ALU.is_lt))
                link(V.reduce_sum(st[:, 31:32], st[:, 32:40], AX))
                V.tensor_scalar(extra_i[:, l:l + 1], st[:, 31:32], float(QUADS), None, ALU.mult).then_inc(s["rounds"], 1)

                def item(i):
                    loop = not isinstance(i, int)
                    n = dve.snap(i + 1) if loop else i + 1
                    dve.wait_ge(s["disp"], n)
                    for c in range(4, DC):
                        g = G_NORM[2 * l + 1] + c
                        V.tensor_scalar(xT_m[:, c], bank(5)[:, (c - 4) * P:(c - 3) * P], g_cols[:, g:g + 1],
                                        None, ALU.mult).then_inc(s["dispc_v"], 1)
                    dve.wait_ge(s["gtp"], n)
                    q4 = dve.snap((n % QUADS) * QUAD) if loop else (n % QUADS) * QUAD
                    fs = dve.snap((n // QUADS) * CAP) if loop else (n // QUADS) * CAP
                    select(q4, fs)
                    select_gates(q4, i * 4 + 6)
                    dve.wait_ge(s["silu"], n)
                    V.tensor_tensor(M["h"], bank(1), M["sg"], ALU.mult).then_inc(s["h"], 1)
                    dve.wait_ge(used[ph], i * ITEM + ITEM)
                    V.tensor_copy(M["y"][:, 512:1024], bank(3)).then_inc(s["y_v"], 1)
                    for k, (b, t, nb) in enumerate(COMB):
                        dve.wait_ge(s["comb"], i * 4 + (k + 1))
                        dst = x3[:, t, nb * 512:(nb + 1) * 512]
                        V.tensor_tensor(dst, dst, bank(b), ALU.add).then_inc(s["added"], 1)

                item(0)
                dve.wait_ge(s["rounds"], 1)
                extra = dve.value_load(extra_i[0:1, l:l + 1], min_val=0, max_val=QUADS * (MAX_ROUNDS - 1))
                with dve.Fori(1, extra + QUADS) as i:
                    item(i)
                dve.wait_ge(s["added"], extra * 4 + QUADS * 4)
                dve.sem_inc(s_x, 1)

            dve.wait_ge(s_gr, 1)
            V.tensor_copy(g_cols[:, :], mbank(3)[:, 0:G_ROWS]).then_inc(s_gc, 1)
            dve.wait_ge(s_gc, 1)
            norm(0)
            st = A["st"]
            for b in range(4):
                dve.wait_ge(used["A"], b + 1)
                V.tensor_scalar(u_a[:, 1, b * 512:(b + 1) * 512], mbank(2 * b + 1), inv_rms(1), None,
                                ALU.mult).then_inc(s_uv["A"], 1)
                if b == 1:
                    dve.wait_ge(s_qsq, 1)
                    link(V.reduce_sum(st[:, 32:64], sq.rearrange("p (g d) -> p g d", d=NA_DH), AX))
                    V.tensor_scalar(st[:, 0:32], st[:, 32:64], 1.0 / NA_DH, EPS, ALU.mult, ALU.add).then_inc(s_qms, 1)
                    dve.wait_ge(s_qrt, 1)
                    link(V.reciprocal(st[:, 32:64], st[:, 0:32]))
                    dve.wait_ge(s_ua["A"], 2)
                    for t in range(TT):
                        qk = u_a[:, t, 0:1024].rearrange("p (g d) -> p g d", d=NA_DH)
                        rs = st[:, 32 + 16 * t:48 + 16 * t].unsqueeze(2).broadcast_to([P, 16, NA_DH])
                        V.tensor_tensor(qk, qk, rs, ALU.mult).then_inc(s_qn, 1)
                    dve.wait_ge(s_load["qkgain"], 64)
                if b == 2:
                    for p in range(4):
                        dve.wait_ge(s_qTp["A"], p + 1)
                        dst = qkT_a[:, 2 * p:2 * p + 2, :].rearrange("p c (r j) -> p (c r) j", j=GRID_W)
                        src = mbank(p).rearrange("p (g j) -> p g j", j=GRID_W)
                        if p < 2:
                            V.tensor_scalar(dst[:, :, ::-1], src, small[:, 0:1], NA_DH ** -0.5,
                                            ALU.mult, ALU.mult).then_inc(s_qT["A"], 1)
                        else:
                            V.tensor_scalar(dst, src, small[:, 1:2], None, ALU.mult).then_inc(s_qT["A"], 1)
            dve.wait_ge(s_biasm, 1)

            def row_max(h):
                dve.wait_ge(s_sc, h + 1)
                if h >= 4:
                    dve.wait_ge(s_pT, h - 3)
                for t in range(TT):
                    V.tensor_tensor(P_a[:, h % 4, t].rearrange("p (r k) -> p r k", k=GRID_W),
                                    mbank(h % 4)[:, t * T:(t + 1) * T].rearrange("p (r k) -> p r k", k=GRID_W),
                                    bias_a[:, 2 - 2 * t:6 - 2 * t, h, :], ALU.add).then_inc(dvc, 1)
                join(2)
                link(V.reduce_max(st[:, 116 + 2 * h:118 + 2 * h], P_a[:, h % 4], AX))
                V.tensor_scalar(st[:, 80 + 2 * h:82 + 2 * h], st[:, 116 + 2 * h:118 + 2 * h], -1.0, None,
                                ALU.mult).then_inc(s_mx, 1)

            def inv_sum(h):
                dve.wait_ge(s_ex, 2 * (h + 1))
                V.reciprocal(st[:, 64 + 2 * h:66 + 2 * h], st[:, 100 + 2 * h:102 + 2 * h]).then_inc(s_rl, 1)

            row_max(0)
            row_max(1)
            inv_sum(0)
            dve.wait_ge(used["A"], 4)
            inv_sum(1)
            row_max(2)
            row_max(3)
            for h in range(HEADS):
                if h + 2 < HEADS and h + 2 <= 3:
                    inv_sum(h + 2)
                dve.wait_ge(s_pT, h + 1)
                if h >= 2:
                    dve.wait_ge(s_pv, h - 1)
                V.tensor_copy(PT_a[:, h % 2].rearrange("p (g j) -> p g j", j=GRID_W)[:, :, ::-1],
                              mbank(4 + h % 2).rearrange("p (g j) -> p g j", j=GRID_W)).then_inc(s_pTc, 1)
                if h >= 2 and h % 2 == 0:
                    hp = h // 2 - 1
                    dve.wait_ge(s_pv, h)
                    V.tensor_copy(mixT_a[:, hp], mbank(6 + hp % 2)[:, 0:T]).then_inc(s_o, 1)
                if h + 4 < HEADS:
                    row_max(h + 4)
                if 4 <= h + 3 < HEADS:
                    inv_sum(h + 3)
            dve.wait_ge(s_pv, HEADS)
            V.tensor_copy(mixT_a[:, HP - 1], mbank(6 + (HP - 1) % 2)[:, 0:T]).then_inc(s_o, 1)
            out_proj("A", 4)

            moe("B", 0)

            norm(2)
            st = C["st"]
            dve.wait_ge(s_gt, 1)
            dve.wait_ge(s_load["gates"], 32)
            for t in range(TT):
                V.scalar_tensor_tensor(gtok[:, t], mbank(7)[:, t * 32:(t + 1) * 32], inv_rms(t), b_gates[:, :],
                                       ALU.mult, ALU.add).then_inc(dvc, 1)
            join(2)
            f4 = gtok.rearrange("p t (d k h) -> p t d k h", d=2, k=2)
            for t in range(TT):
                f = f4[:, t, :, 1, :]
                V.scalar_tensor_tensor(gw[:, 0, t], f, -1.0, f, ALU.mult, ALU.max).then_inc(dvc, 1)
                V.tensor_scalar(gw[:, 2, t], f, 0.0, None, ALU.min).then_inc(dvc, 1)
            join(4)
            dve.sem_inc(s_gab, 1)
            V.memset(ve[:, :, :, ML_DV:VE], 1.0).then_inc(s_gtk, 1)
            dve.wait_ge(s_gex, 1)
            V.tensor_scalar(gw[:, 1], gw[:, 1], 1.0, None, ALU.add).then_inc(s_gp1, 1)
            dve.wait_ge(s_gln, 1)
            for t in range(TT):
                V.tensor_tensor(f4[:, t, :, 1, :], gw[:, 2, t], gw[:, 1, t], ALU.subtract).then_inc(s_gtk, 1)

            def copy_u(j):
                dve.wait_ge(used["C"], j + 1)
                b = ORDER_C[j]
                src = mbank(BANK_C[j] + 1)
                if b < 2:
                    V.tensor_scalar(qk_c[:, 1, b * 512:(b + 1) * 512], src, inv_rms(1), None,
                                    ALU.mult).then_inc(s_uv["C"], 1)
                else:
                    V.tensor_scalar(ve[:, 1, 4 * (b - 2):4 * (b - 1), 0:ML_DV],
                                    src.rearrange("p (h e) -> p h e", h=4), inv_rms(1), None,
                                    ALU.mult).then_inc(s_uv["C"], 1)

            copy_u(0)
            dve.wait_ge(s_gTp, 2)
            for k in range(2):
                V.tensor_copy(gT[:, 2 * k:2 * k + 2], mbank(6 + k)[0:8, :].rearrange("p (j t) -> p j t", j=2)).then_inc(s_gTc, 1)
            dve.wait_ge(s_gTc, 2)
            one8 = ones[0:8, 0:1].broadcast_to([8, T])

            def way(ap, d):
                return ap[:, d, :] if d == 0 else ap[:, d, ::-1]

            gTi = gT.rearrange("p (d k) t -> p d k t", k=2)
            for d in range(2):
                lf = gTi[:, d, 1, :] if d == 0 else gTi[:, d, 1, ::-1]
                V.tensor_tensor_scan(way(F_c, d), one8, lf, 0.0, ALU.mult, ALU.add).then_inc(dvc, 1)
            join(2)
            link(V.tensor_tensor(a_c, gTi[:, :, 0, :], F_c, ALU.subtract))
            for d in range(2):
                V.tensor_tensor_scan(way(nM, d), one8, way(a_c, d), 0.0, ALU.mult, ALU.max).then_inc(dvc, 1)
            join(2)
            link(V.tensor_scalar(nM, nM, -1.0, None, ALU.mult))
            V.tensor_tensor(F_c, nM, F_c, ALU.subtract).then_inc(s_em, 1)
            copy_u(1)
            dve.wait_ge(s_aTp, 1)
            V.tensor_copy(C["aT"], mbank(6)[:, 0:64]).then_inc(s_aT, 1)
            for p in range(4):
                dve.wait_ge(s_qTp["C"], p + 1)
                V.tensor_scalar(qkT_c[:, 2 * p:2 * p + 2, :], mbank(p).rearrange("p (c t) -> p c t", c=2),
                                1.0 if p < 2 else 64 ** -0.5, None, ALU.mult).then_inc(s_qT["C"], 1)
            dve.wait_ge(s_aT, 1)
            copy_u(4)
            SEG = ((0, 0, 0, 0, T), (T, 1, 1, 0, T), (2 * T, 1, 0, 0, P), (2 * T + P, 0, 1, P, P))

            def decay(h):
                dve.wait_ge(s_bc, h + 1)
                if h >= 2:
                    dve.wait_ge(s_nu, h - 1)
                for o, d, stile, t0, n in SEG:
                    ins = V.scalar_tensor_tensor(W_c[:, h % 2, o:o + n], mbank(2 + h % 2)[:, d * T + t0:d * T + t0 + n],
                                                 aT[:, 0, d, stile, h:h + 1], mlmask[:, o:o + n], ALU.add, ALU.min)
                    ins.then_inc(dvc, 1)
                join(4)
                dve.sem_inc(s_dl, 1)

            def weigh(h):
                dve.wait_ge(s_w, h + 1)
                dve.wait_ge(s_st, h + 1)
                w = W_c[:, h % 2]
                sc = mbank(h % 2)
                V.tensor_tensor(w[:, 0:2 * T], w[:, 0:2 * T], sc, ALU.mult).then_inc(s_ws, 1)
                diag = bass.AP(tensor=sc.tensor, offset=sc.offset, ap=[list(sc.ap[0]), [T + P, 2], [1, P]])
                V.tensor_tensor(w[:, 2 * T:3 * T].rearrange("p (j n) -> p j n", j=2),
                                w[:, 2 * T:3 * T].rearrange("p (j n) -> p j n", j=2), diag, ALU.mult).then_inc(s_ws, 1)

            def inv_den(h):
                dve.wait_ge(s_nu, h + 1)
                b = 4 + 2 * (h % 2)
                rd = st[:, 4 * h:4 * h + 4].rearrange("p (d t) -> p d t", d=2)
                den = psum[:, b % 4:b % 4 + 2, ML_DV:2 * VE:VE]
                link(V.scalar_tensor_tensor(rd, den, -1.0, aT[:, 1, :, :, h], ALU.mult, ALU.max))
                link(V.tensor_tensor(rd, den, rd, ALU.max))
                V.reciprocal(st[:, 4 * h:4 * h + 4], st[:, 4 * h:4 * h + 4]).then_inc(s_rd, 1)

            def both_ways(h):
                b = 4 + 2 * (h % 2)
                dve.wait_ge(s_hf, 2 * (h + 1))
                for t in range(TT):
                    V.scalar_tensor_tensor(h_c[:, t, h * ML_DV:(h + 1) * ML_DV],
                                           mbank(b + 1)[:, t * VE:t * VE + ML_DV],
                                           st[:, 4 * h + 2 + t:4 * h + 3 + t], tmp_c[:, h % 2, t],
                                           ALU.mult, ALU.add).then_inc(dvc, 1)
                join(2)
                dve.sem_inc(s_hb, 1)

            decay(0)
            decay(1)
            weigh(0)
            copy_u(5)
            for h in range(HEADS):
                if h + 1 < HEADS:
                    weigh(h + 1)
                inv_den(h)
                if h + 2 < HEADS:
                    decay(h + 2)
                both_ways(h)
            dve.wait_ge(s_hsq, 2 * HEADS)
            V.tensor_scalar(st[:, 80:96], st[:, 64:80], 1.0 / ML_DV, EPS, ALU.mult, ALU.add).then_inc(s_hms, 1)
            dve.wait_ge(s_hrt, 1)
            link(V.reciprocal(st[:, 64:80], st[:, 80:96]))
            for h in range(HEADS):
                for t in range(TT):
                    o = slice(h * ML_DV, (h + 1) * ML_DV)
                    V.scalar_tensor_tensor(h_c[:, t, o], h_c[:, t, o], st[:, 64 + 8 * t + h:65 + 8 * t + h],
                                           og[:, t, o], ALU.mult, ALU.mult).then_inc(s_hn, 1)
            out_proj("C", 6)

            moe("D", 1)

        @block.tensor
        def _(pe):
            def mm(out_, lhsT, rhs, start=True, stop=True):
                return nc.tensor.matmul(out_, lhsT, rhs, start=start, stop=stop)

            def two_chunks_T(to, p, src):
                for c in range(2):
                    for t in range(TT):
                        k = 2 * p + c
                        last = nc.tensor.transpose(to[:, (2 * c + t) * P:(2 * c + t + 1) * P],
                                                   src[:, t, k * P:(k + 1) * P], ident)
                return last

            def x_T(n):
                if n == 0:
                    pe.wait_ge(s_load["x"], 32)
                else:
                    pe.wait_ge(s_x, n)
                for p in range(4):
                    two_chunks_T(bank(p), p, x3).then_inc(s_xTp, 1)

            def dense_block(ph, j, lhs, b0, chunk0=None, chunk_sem=s_xTv):
                pe.wait_ge(landed[ph][(first[ph] + j) % SLOTS], 16 * (j // SLOTS + 1))
                w = slot(first[ph] + j).rearrange("p (c n) -> p c n", c=DC)
                for t in range(TT):
                    for c in range(DC):
                        if t == 0 and chunk0 is not None:
                            pe.wait_ge(chunk_sem, chunk0 + c + 1)
                        last = mm(bank(b0 + t), lhs[:, c, t * P:(t + 1) * P], w[:, c, :], c == 0, c == DC - 1)
                last.then_inc(used[ph], 1)

            def moe(ph, l):
                s = ms[l]
                x_T(2 * l + 1)
                pe.wait_ge(s_load["route"], 128)
                route = w_route[:, :].rearrange("p (l c n) -> p l c n", l=2, c=DC)
                for t in range(TT):
                    for c in range(DC):
                        if t == 0:
                            pe.wait_ge(s_xTv, DC * (2 * l + 1) + c + 1)
                        last = mm(bank(4)[:, t * ROUTE:(t + 1) * ROUTE], xnT3[:, c, t * P:(t + 1) * P],
                                  route[:, l, c, :], c == 0, c == DC - 1)
                last.then_inc(s["logits"], 1)
                pe.wait_ge(s["mask"], 1)
                m3 = M["mask"].rearrange("p (t e) -> p t e", t=TT)
                mm(bank(5)[:, 0:32], tri, m3[:, 0])
                mm(bank(5)[:, 32:64], ones, m3[:, 0], True, False)
                mm(bank(5)[:, 32:64], tri, m3[:, 1], False, True)
                mm(bank(5)[:, 64:96], ones, m3[:, 0], True, False)
                mm(bank(5)[:, 64:96], ones, m3[:, 1], False, True).then_inc(s["rank"], 1)

                def item(i):
                    loop = not isinstance(i, int)
                    n = pe.snap(i + 1) if loop else i + 1
                    pe.wait_ge(s["sel"], i * 4 + 2)
                    if not loop:
                        pe.wait_ge(s["scaled"], 2)
                    for c in range(DC):
                        if c == 4 and not loop:
                            pe.wait_ge(s["rounds"], 1)
                        for t in range(TT):
                            last = mm(bank(4 + c // 4)[:, (c % 4) * P:(c % 4 + 1) * P],
                                      xs3[:, t, c * P:(c + 1) * P], M["S"][:, t * P:(t + 1) * P],
                                      t == 0, t == TT - 1)
                    last.then_inc(s["disp"], 1)
                    pe.wait_ge(s["sel"], i * 4 + 4)
                    if loop:
                        pe.wait_ge(s["added"], i * 4)
                    for t in range(TT):
                        last = nc.tensor.transpose(bank(6)[:, t * P:(t + 1) * P], M["Gs"][:, t * P:(t + 1) * P], ident)
                    last.then_inc(s["gtp"], 1)
                    pe.wait_ge(s["dispc_a"], i * 4 + 4)
                    pe.wait_ge(s["dispc_v"], i * 4 + 4)
                    for j in range(ITEM):
                        at, there, value = piece(ph, i, j)
                        pe.wait_ge(there, value)
                        w = at.rearrange("p (e n) -> p e n", e=QUAD)
                        if j == GU_PIECES:
                            pe.wait_ge(s["h"], n)
                            for k in range(FF // P):
                                last = nc.tensor.transpose(bank(7)[:, k * P:(k + 1) * P], M["h"][:, k * P:(k + 1) * P], ident)
                            last.then_inc(s["hTp"], 1)
                            pe.wait_ge(s["hTc"], n)
                        down = j >= GU_PIECES
                        k = j - GU_PIECES if down else j
                        lhs = hT_m if down else xT_m
                        for half in range(2):
                            for e in range(QUAD):
                                last = mm(psum[e * CAP:(e + 1) * CAP, 2 * down + half, :],
                                          lhs[:, k, e * CAP:(e + 1) * CAP],
                                          w[:, e, half * 512:(half + 1) * 512],
                                          k == 0, k == (DN_PIECES if down else GU_PIECES) - 1)
                        last.then_inc(used[ph], 1)
                    pe.wait_ge(s["gtc"], n)
                    pe.wait_ge(s["y_a"], n)
                    pe.wait_ge(s["y_v"], n)
                    for b, t, nb in COMB:
                        mm(bank(b), M["GT"][:, t * P:(t + 1) * P], M["y"][:, nb * 512:(nb + 1) * 512]).then_inc(s["comb"], 1)

                item(0)
                extra = pe.value_load(extra_i[0:1, l:l + 1], min_val=0, max_val=QUADS * (MAX_ROUNDS - 1))
                with pe.Fori(1, extra + QUADS) as i:
                    item(i)

            pe.wait_ge(s_load["cst"], 16)
            pe.wait_ge(s_load["gains"], 80)
            nc.tensor.transpose(mbank(3)[:, 0:G_ROWS], g_rows[0:G_ROWS, :], ident[0:G_ROWS, 0:G_ROWS]).then_inc(s_gr, 1)
            x_T(0)
            dense_block("A", 0, xnT3, 4, 0)
            dense_block("A", 1, xnT3, 6)
            pe.wait_ge(s_gc, 1)
            pe.wait_ge(s_xTv, DC)
            dense_block("A", 2, xnT3, 0)
            pe.wait_ge(s_qn, 2)
            for p in range(4):
                two_chunks_T(mbank(p), p, u_a).then_inc(s_qTp["A"], 1)
            dense_block("A", 3, xnT3, 2)
            pe.wait_ge(s_qT["A"], 4)

            def scores(h):
                if h >= 4:
                    pe.wait_ge(s_mx, h - 3)
                r = slice(64 * (h % 2), 64 * (h % 2) + 64)
                for t in range(TT):
                    last = mm(mbank(h % 4)[:, t * T:(t + 1) * T], qkT_a[r, h // 2, t * P:(t + 1) * P],
                              qkT_a[r, 4 + h // 2, :])
                last.then_inc(s_sc, 1)

            scores(0)
            scores(1)
            pe.wait_ge(s_load["lc0"], 16)
            pe.wait_ge(s_ua["A"], 4)
            pe.wait_ge(s_uv["A"], 4)
            for c in range(4):
                for t in range(TT):
                    last = mm(mbank(4 + c), u_a[:, t, 1536 + c * P:1536 + (c + 1) * P], seqdft[:, t, :], t == 0, t == 1)
                last.then_inc(s_f1, 1)
            scores(2)
            scores(3)
            for c in range(4):
                pe.wait_ge(s_f1c, c + 1)
                mm(mbank(4 + c)[:, 0:T], chdft[:, 0, :], AB[:, c, 0:T], True, False)
                mm(mbank(4 + c)[:, 0:T], chdft[:, 1, :], AB[:, c, T:2 * T], False, True).then_inc(s_f2, 1)

            def times_v(h):
                pe.wait_ge(s_pTc, h + 1)
                hp = h // 2
                if h % 2 == 0 and hp >= 2:
                    pe.wait_ge(s_o, hp - 1)
                o = 64 * (h % 2)
                for kt in range(TT):
                    last = mm(mbank(6 + hp % 2)[o:o + 64, 0:T], u_a[:, kt, 1024 + 64 * h:1024 + 64 * (h + 1)],
                              PT_a[:, h % 2, kt * T:(kt + 1) * T], kt == 0, kt == TT - 1)
                last.then_inc(s_pv, 1)

            pe.wait_ge(s_f2c, 4)
            for h in range(HEADS):
                pe.wait_ge(s_pn, 2 * (h + 1))
                if h >= 2:
                    pe.wait_ge(s_pTc, h - 1)
                for kt in range(TT):
                    for qt in range(TT):
                        last = nc.tensor.transpose(mbank(4 + h % 2)[:, kt * T + qt * P:kt * T + (qt + 1) * P],
                                                   P_a[:, h % 4, qt, kt * P:(kt + 1) * P], ident)
                last.then_inc(s_pT, 1)
                if h + 4 < HEADS:
                    scores(h + 4)
                if h >= 1:
                    times_v(h - 1)
            times_v(HEADS - 1)
            pe.wait_ge(s_o, HP)
            for nb in range(2):
                dense_block("A", 4 + nb, mixT_a, 4 + 2 * nb)

            moe("B", 0)

            x_T(2)
            pe.wait_ge(s_load["gates"], 32)
            pe.wait_ge(s_xTv, 3 * DC)
            wg = w_gates[:, :].rearrange("p (c n) -> p c n", c=DC)
            for t in range(TT):
                for c in range(DC):
                    last = mm(mbank(7)[:, t * 32:(t + 1) * 32], xnT3[:, c, t * P:(t + 1) * P], wg[:, c, :], c == 0, c == DC - 1)
            last.then_inc(s_gt, 1)
            dense_block("C", 0, xnT3, 4)
            pe.wait_ge(s_gtk, 3)
            for j in range(4):
                for t in range(TT):
                    last = nc.tensor.transpose(mbank(6 + j // 2)[0:8, (j % 2) * T + t * P:(j % 2) * T + (t + 1) * P],
                                               gtok[:, t, 8 * j:8 * j + 8], ident)
                if j % 2:
                    last.then_inc(s_gTp, 1)
            dense_block("C", 1, xnT3, 6)
            pe.wait_ge(s_gTc, 2)
            pe.wait_ge(s_eme, 1)
            for k, src in enumerate((a_c, E_c)):
                for d in range(2):
                    for t in range(TT):
                        o = ((k * 2 + d) * TT + t) * 8
                        last = nc.tensor.transpose(mbank(6)[:, o:o + 8], src[:, d, t * P:(t + 1) * P], ident[0:8, 0:8])
            last.then_inc(s_aTp, 1)
            dense_block("C", 2, xnT3, 0)
            pe.wait_ge(s_aT, 1)
            dense_block("C", 3, xnT3, 2)
            pe.wait_ge(s_ua["C"], 2)
            pe.wait_ge(s_uv["C"], 2)
            for p in range(4):
                two_chunks_T(mbank(p), p, qk_c).then_inc(s_qTp["C"], 1)
            pe.wait_ge(s_og, 2)
            dense_block("C", 4, xnT3, 0)
            pe.wait_ge(s_qT["C"], 4)
            pe.wait_ge(s_load["lc1"], 16)

            def ml_scores(h):
                if h >= 2:
                    pe.wait_ge(s_ws, 2 * (h - 1))
                r = slice(64 * (h % 2), 64 * (h % 2) + 64)
                for st_ in range(TT):
                    last = mm(mbank(h % 2)[:, st_ * T:(st_ + 1) * T], qkT_c[r, 4 + h // 2, st_ * P:(st_ + 1) * P],
                              qkT_c[r, h // 2, :])
                last.then_inc(s_st, 1)
                if h >= 2:
                    pe.wait_ge(s_dl, h - 1)
                mm(mbank(2 + h % 2), sel_c[:, h, :], C["nM"][0:8, :]).then_inc(s_bc, 1)

            ml_scores(0)
            ml_scores(1)
            pe.wait_ge(s_og, 4)
            dense_block("C", 5, xnT3, 2)
            for h in range(HEADS):
                pe.wait_ge(s_ws, 2 * (h + 1))
                if h < 2:
                    pe.wait_ge(s_ua["C"], 3 + h)
                    pe.wait_ge(s_uv["C"], 3 + h)
                else:
                    pe.wait_ge(s_hb, h - 1)
                w = W_c[:, h % 2]
                fb, bb = mbank(4 + 2 * (h % 2)), mbank(5 + 2 * (h % 2))
                v = [ve[:, t, h, :] for t in range(TT)]
                mm(fb[:, 0:VE], w[:, 0:P], v[0])
                mm(fb[:, VE:2 * VE], w[:, P:T], v[0], True, False)
                mm(fb[:, VE:2 * VE], w[:, 2 * T + P:3 * T], v[1], False, True)
                mm(bb[:, 0:VE], w[:, 2 * T:2 * T + P], v[0], True, False)
                mm(bb[:, 0:VE], w[:, T:T + P], v[1], False, True)
                mm(bb[:, VE:2 * VE], w[:, T + P:2 * T], v[1]).then_inc(s_nu, 1)
                if h + 2 < HEADS:
                    ml_scores(h + 2)
            for p in range(4):
                pe.wait_ge(s_hn, 4 * (p + 1))
                two_chunks_T(bank(p), p, h_c).then_inc(s_hTp, 1)
            for nb in range(2):
                dense_block("C", 6 + nb, mixT_c, 4 + 2 * nb, 0 if nb == 0 else None, s_hTa)

            moe("D", 1)


_INS = ['x', 'ev_norm', 'ev_w_in', 'ev_q_gain', 'ev_k_gain', 'ev_rel_bias', 'ev_w_out',
        'od_norm', 'od_w_in', 'od_gate_bias', 'od_h_gain', 'od_w_out',
        'moe_norm', 'moe_w_rg', 'moe_b_rg', 'moe_w_re', 'moe_b_re', 'moe_w_gate', 'moe_w_up', 'moe_w_down']


def kernel(**inputs):
    import numpy as _np
    import concourse.bacc as _bacc
    from concourse import mybir as _mybir
    from concourse.bass_utils import run_bass_kernel_spmd as _run

    nc = _bacc.Bacc("TRN2", target_bir_lowering=False, num_devices=1)
    arrays, args = {}, {}
    given = {name: _np.ascontiguousarray(inputs[name]) for name in _INS}
    given.update(zip(("c_common", "c_layer0", "c_layer1"), shape_constants()))
    for name, arr in given.items():
        arrays[f"in_{name}"] = arr
        args[name] = nc.dram_tensor(f"in_{name}", arr.shape, _mybir.dt.from_np(arr.dtype), kind="ExternalInput").ap()
    out = nc.dram_tensor("out_0", (1, T, D), _mybir.dt.float32, kind="ExternalOutput").ap()
    build(nc, args, out)
    r = _run(nc, [arrays], core_ids=[0])
    return r.results[0]["out_0"]
```

```python
from contextlib import ExitStack

import numpy as np

import concourse.bass as bass
from concourse import mybir

P = 128
F32 = mybir.dt.float32
I32 = mybir.dt.int32
ALU = mybir.AluOpType
ACT = mybir.ActivationFunctionType
AX = mybir.AxisListType.X
ENG = mybir.EngineType

D = 1024
T = 256
TT = T // P
DC = D // P
EPS = 1e-6
GRID_W = 64

HEADS = 8
HP = HEADS // 2
NA_DH = 64
NA_WIN = 16
REL_R, REL_C = 15, 31
REL_SIZE = REL_R * REL_C
BIAS_ROWS = 6
ML_DV = 128
EARLY = 6
VE = ML_DV + 1

GROUPS, PER_GROUP, FF = 4, 8, 512
EXPERTS = GROUPS * PER_GROUP
ROUTE = GROUPS + EXPERTS
QUAD = 4
QUADS = EXPERTS // QUAD
CAP = P // QUAD
MAX_ROUNDS = T // CAP
GU_PIECES = D // P
DN_PIECES = FF // P
ITEM = GU_PIECES + DN_PIECES

SLOTS = 6
WARM = 4
SLOT = 4096
EXTRA = 4
NEG = -1e30

G_EV, G_OD, G_MOE0, G_MOE1, G_HEADS = (DC * j for j in range(5))
G_NORM = (G_EV, G_MOE0, G_OD, G_MOE1)
G_ROWS = 5 * DC

C_IDENT = 0
C_TRI = C_IDENT + P
C_ONES = C_TRI + P
C_SLOTID = C_ONES + P
C_RANKW = C_SLOTID + T + CAP
C_THR = C_RANKW + EXPERTS
C_COMMON = C_THR + MAX_ROUNDS
C0_SEQ = 0
C0_CH = C0_SEQ + TT * 2 * T
C0_MASK = C0_CH + 2 * P
C0_SIZE = C0_MASK + GRID_W
C1_MASK = 0
C1_SEL = C1_MASK + 3 * T
C1_SIZE = C1_SEL + HEADS * P
C_LAYER = max(C0_SIZE, C1_SIZE)


def shape_constants():
    common = np.zeros((P, C_COMMON), np.float32)
    p = np.arange(P)
    common[:, C_IDENT:C_TRI] = np.eye(P)
    common[:, C_TRI:C_ONES] = p[:, None] < p[None, :]
    common[:, C_ONES:C_SLOTID] = 1.0
    common[:, C_SLOTID:C_RANKW] = np.arange(T + CAP)
    common[:, C_RANKW:C_THR] = EXPERTS - np.arange(EXPERTS)
    common[:, C_THR:C_COMMON] = CAP * np.arange(1, MAX_ROUNDS + 1) + 0.5

    l0 = np.zeros((P, C_LAYER), np.float32)
    t = np.arange(T)
    ang = 2 * np.pi * ((t[:, None] * t[None, :]) % T) / T
    norm = 1.0 / np.sqrt(T * 64)
    seq = np.concatenate([np.cos(ang), np.sin(ang)], axis=1) * norm
    l0[:, C0_SEQ:C0_CH] = seq.reshape(TT, P, 2 * T).transpose(1, 0, 2).reshape(P, -1)
    c = np.arange(64)
    ang = 2 * np.pi * ((c[:, None] * c[None, :]) % 64) / 64
    for j, m in enumerate((np.cos(ang), -np.sin(ang))):
        for g in range(2):
            o = C0_CH + j * P + 64 * g
            l0[64 * g:64 * g + 64, o:o + 64] = m
    qc = GRID_W - 1 - p % GRID_W
    lo = np.clip(qc - NA_WIN // 2, 0, GRID_W - NA_WIN)
    kc = np.arange(GRID_W)
    ok = (kc[None, :] >= lo[:, None]) & (kc[None, :] < lo[:, None] + NA_WIN)
    l0[:, C0_MASK:C0_SIZE] = np.where(ok, 0.0, NEG)

    l1 = np.zeros((P, C_LAYER), np.float32)
    s, tt = p[:, None], t[None, :]
    fw0 = np.where(tt >= s, 0.0, NEG)
    bw1 = np.where(tt <= s + P, 0.0, NEG)
    bw0 = np.where(tt[:, :P] <= s, 0.0, NEG)
    fw1 = np.where(tt[:, :P] >= s, 0.0, NEG)
    l1[:, C1_MASK:C1_SEL] = np.concatenate([fw0, bw1, bw0, fw1], axis=1)
    for h in range(HEADS):
        l1[h, C1_SEL + h * P:C1_SEL + (h + 1) * P] = 1.0
    return common, l0, l1


def build(nc, a, out):
    ctx = ExitStack()
    with ctx:
        def sb(name, width, dt=F32):
            return ctx.enter_context(nc.sbuf_tensor(name, [P, width], dt))

        def sem(name):
            return ctx.enter_context(nc.semaphore(name))

        ring = sb("ring", SLOTS * SLOT)
        x = sb("x", TT * D)
        xs = sb("xs", TT * D)
        scratch = sb("scratch", SLOT)
        XNT_MIX, SQ_MIX = scratch[:, 0:DC * T], scratch[:, DC * T:SLOT]
        g_rows = sb("g_rows", P)
        g_cols = sb("g_cols", G_ROWS)
        cst = sb("cst", C_COMMON)
        lcst = sb("lcst", C_LAYER)
        w_route = sb("w_route", 2 * DC * ROUTE)
        b_route = sb("b_route", 2 * ROUTE)
        w_gates = sb("w_gates", DC * 32)
        b_gates = sb("b_gates", 32)
        small = sb("small", 128)
        extra_i = sb("items_i", 8, I32)
        MOE_SIZE = 3840
        PHASE = 16292
        phase = sb("phase", PHASE)
        o = MOE_SIZE + (EXTRA - 2) * SLOT
        XNT_MOE, SQ_MOE = phase[:, o:o + DC * T], phase[:, o + DC * T:o + SLOT]
        psum = ctx.enter_context(nc.psum_tensor("psum", [P, 8, 512], F32))

        def carve(sizes):
            at, views = 0, {}
            for name, n in sizes:
                views[name] = phase[:, at:at + n]
                at += n
            assert at <= PHASE, at
            return views

        x3 = x[:, :].rearrange("p (t d) -> p t d", t=TT)
        xs3 = xs[:, :].rearrange("p (t d) -> p t d", t=TT)

        def xnT_of(n):
            return (XNT_MOE if n % 2 else XNT_MIX).rearrange("p (c t) -> p c t", c=DC)

        xnT3 = xnT_of(0)
        ident = cst[:, C_IDENT:C_TRI]
        tri = cst[:, C_TRI:C_ONES]
        ones = cst[:, C_ONES:C_SLOTID]
        slotid = cst[:, C_SLOTID:C_RANKW]
        rankw = cst[:, C_RANKW:C_THR]
        thr = cst[:, C_THR:C_COMMON]

        def slot(n):
            return ring[:, (n % SLOTS) * SLOT:(n % SLOTS + 1) * SLOT]

        def bank(b):
            return psum[:, b, :]

        def mbank(b):
            return psum[:, (b + 4) % 8, :]

        n_a = 4 + 2
        n_c = 6 + 2
        first = {"A": 0, "B": n_a, "C": n_a + QUADS * ITEM - EXTRA,
                 "D": n_a + QUADS * ITEM - EXTRA + n_c}
        assert ITEM % SLOTS == 0 and SLOTS + EXTRA < ITEM
        ORDER_C = (0, 1, 4, 5, 2, 3)
        BANK_C = (0, 2, 4, 6, 4, 6)

        PLACES_0 = ([*range(SLOTS - 2)] + [-1 - (EXTRA - 1)] + [-1 - k for k in range(EXTRA - 2)]
                    + [SLOTS - 2, SLOTS - 1] + [-1 - (EXTRA - 2)] + [*range(SLOTS, ITEM - EXTRA)])

        def ring_turn(i, j):
            if isinstance(i, int) and i == 0:
                return PLACES_0[j] if PLACES_0[j] >= 0 else None
            return j - EXTRA

        landed = {ph: [sem(f"landed_{ph}{s}") for s in range(SLOTS)] for ph in "AC"}
        landed["B"], landed["D"] = landed["A"], landed["C"]
        used = {ph: sem(f"used_{ph}") for ph in "ABCD"}

        landed_x = {ph: [sem(f"landed_{ph}_extra{s}") for s in range(EXTRA)] for ph in "BD"}

        def dense_source(ph, j):
            w_in, w_out, order = ((a["ev_w_in"], a["ev_w_out"], range(4)) if ph == "A"
                                  else (a["od_w_in"], a["od_w_out"], ORDER_C))
            w, b = (w_in, order[j]) if j < len(order) else (w_out, j - len(order))
            return w[0, :, b * 512:(b + 1) * 512].rearrange("(c p) n -> p c n", p=P)

        def piece(ph, i, j):
            turn = ring_turn(i, j)
            if turn is None:
                k = -1 - PLACES_0[j]
                o = MOE_SIZE + k * SLOT
                at = scratch[:, :] if k == EXTRA - 1 else phase[:, o:o + SLOT]
                return at, landed_x[ph][k], 32
            n = (first[ph] + turn) % SLOTS
            mixer, n_mixer = ("A", n_a) if ph == "B" else ("C", n_c)
            before = sum(16 for k in range(n_mixer) if (first[mixer] + k) % SLOTS == n)
            return (slot(first[ph] + turn), landed[ph][n],
                    i * (ITEM // SLOTS * 32) + 32 * (turn // SLOTS + 1) + before)

        s_load = {n: sem(f"loaded_{n}") for n in
                  ("x", "cst", "lc0", "lc1", "bias", "qkgain", "gains", "route", "gates")}
        s_half = sem("landed_A_first_half")
        s_gr = sem("gains_in_psum")
        s_gc = sem("gains_copied")
        s_x = sem("x_ready")
        s_ssq = sem("squares_summed")
        s_ms = sem("mean_square_ready")
        s_rt = sem("root_ready")
        s_rs = sem("inv_rms_ready")
        s_xTp = sem("xnT_in_psum")
        s_xTv = sem("xnT_copied")
        s_xTa = sem("xnT_copied_act")
        dvc = sem("dve_chain")
        s_out = sem("out_stored")
        s_free = sem("slot_seen_free")

        s_biasm = sem("bias_masked")
        s_ua = {ph: sem(f"u_copied_act_{ph}") for ph in "AC"}
        s_uv = {ph: sem(f"u_copied_dve_{ph}") for ph in "AC"}
        s_qsq = sem("qk_squared")
        s_qms = sem("qk_mean_square")
        s_qrt = sem("qk_root")
        s_qn = sem("qk_normed")
        s_qTp = {ph: sem(f"qkT_in_psum_{ph}") for ph in "AC"}
        s_qT = {ph: sem(f"qkT_copied_{ph}") for ph in "AC"}
        s_f1 = sem("seq_dft_done")
        s_f1c = sem("seq_dft_copied")
        s_f2 = sem("ch_dft_done")
        s_f2c = sem("ch_dft_copied")
        s_sc = sem("scores_done")
        s_mx = sem("max_ready")
        s_ex = sem("exp_done")
        s_rl = sem("inv_sum_ready")
        s_pn = sem("probs_normed_pool")
        s_pna = sem("probs_normed_act")
        s_pT = sem("probsT_in_psum")
        s_pTc = sem("probsT_copied")
        s_pv = sem("pv_done")
        s_o = sem("attn_copied")

        def moe_sems(l):
            return {n: sem(f"{n}_{l}") for n in
                    ("scaled", "logits", "gsub", "gexp", "esub", "eexp", "mask", "rank", "count", "early", "rounds",
                     "sel", "disp", "dispc_a", "dispc_v", "gtp", "gtc", "silu", "h", "hTp",
                     "hTc", "y_a", "y_v", "comb", "added")}

        ms = [moe_sems(0), moe_sems(1)]

        s_gt = sem("gates_done")
        s_gab = sem("gate_abs_ready")
        s_gex = sem("gate_exp_ready")
        s_gp1 = sem("gate_exp1_ready")
        s_gln = sem("gate_log_ready")
        s_gtk = sem("gates_token_major")
        s_gTp = sem("gatesT_in_psum")
        s_em = sem("neg_m_ready")
        s_eme = sem("exp_neg_m_ready")
        s_gTc = sem("gatesT_copied")
        s_aTp = sem("aT_in_psum")
        s_aT = sem("aT_copied")
        s_og = sem("o_gate_ready")
        s_st = sem("st_done")
        s_bc = sem("m_broadcast")
        s_dl = sem("decay_log_ready")
        s_w = sem("decay_exp_ready")
        s_ws = sem("weighted_scores")
        s_nu = sem("num_done")
        s_rd = sem("inv_den_ready")
        s_hf = sem("h_fw_ready")
        s_hb = sem("h_ready")
        s_hsq = sem("h_squared")
        s_hms = sem("h_mean_square")
        s_hrt = sem("h_root")
        s_hn = sem("h_normed")
        s_hTp = sem("hT_in_psum")
        s_hTa = sem("hT_copied")

        A = carve([("mixT", DC * T), ("u", TT * 2048), ("qkT", 8 * T),
                   ("bias", BIAS_ROWS * HEADS * GRID_W), ("P", 4 * TT * T), ("PT", 4 * TT * T), ("st", 160)])
        C = carve([("qk", TT * 1024), ("ve", TT * HEADS * VE), ("og", TT * D), ("qkT", 8 * T),
                   ("W", 2 * 3 * T), ("h", TT * D), ("tmp", 2 * 2 * TT * P), ("gtok", TT * 32),
                   ("gw", 3 * TT * 16), ("gT", 4 * T), ("F", 2 * T), ("a", 2 * T), ("nM", 2 * T),
                   ("E", 2 * T), ("aT", 64), ("st", 160)])
        M = carve([("L", TT * ROUTE), ("oh", 2 * TT * EXPERTS),
                   ("mask", TT * EXPERTS), ("G", TT * EXPERTS), ("rank", TT * EXPERTS), ("st", 64),
                   ("S", TT * P), ("Gs", TT * P), ("xT", DC * P), ("GT", TT * P), ("y", D), ("hT", FF)])
        M["sg"], M["h"] = M["y"][:, 0:FF], M["y"][:, FF:2 * FF]
        M["work"] = M["hT"]
        assert sum(M[k].shape[1] for k in M if k not in ("sg", "h", "work")) <= MOE_SIZE
        assert MOE_SIZE + (EXTRA - 1) * SLOT <= PHASE

        u_a = A["u"].rearrange("p (t n) -> p t n", t=TT)
        qkT_a = A["qkT"].rearrange("p (c t) -> p c t", c=8)
        bias_a = A["bias"].rearrange("p (r h k) -> p r h k", r=BIAS_ROWS, h=HEADS)
        P_a = A["P"].rearrange("p (b t k) -> p b t k", b=4, t=TT)
        PT_a = A["PT"].rearrange("p (b n) -> p b n", b=4)
        mixT_a = A["mixT"].rearrange("p (c t) -> p c t", c=DC)
        AB = xs[:, :].rearrange("p (c n) -> p c n", c=4)
        seqdft = lcst[:, C0_SEQ:C0_CH].rearrange("p (t n) -> p t n", t=TT)
        chdft = lcst[:, C0_CH:C0_MASK].rearrange("p (j n) -> p j n", j=2)
        namask = lcst[:, C0_MASK:C0_SIZE]

        qk_c = C["qk"].rearrange("p (t n) -> p t n", t=TT)
        ve = C["ve"].rearrange("p (t h e) -> p t h e", t=TT, h=HEADS)
        og = C["og"].rearrange("p (t n) -> p t n", t=TT)
        qkT_c = C["qkT"].rearrange("p (c t) -> p c t", c=8)
        W_c = [C["W"][:, 0:3 * T], C["W"][:, 3 * T:6 * T], C["gT"][:, 0:3 * T]]
        h_c = C["h"].rearrange("p (t n) -> p t n", t=TT)
        tmp_c = C["tmp"].rearrange("p (b d t n) -> p b d t n", b=2, d=2, t=TT)
        gtok = C["gtok"].rearrange("p (t n) -> p t n", t=TT)
        gw = C["gw"].rearrange("p (j t d h) -> p j t d h", j=3, t=TT, d=2)
        gT = C["gT"][0:8, :].rearrange("p (j t) -> p j t", j=4)
        F_c = C["F"][0:8, :].rearrange("p (d t) -> p d t", d=2)
        a_c = C["a"][0:8, :].rearrange("p (d t) -> p d t", d=2)
        nM = C["nM"][0:8, :].rearrange("p (d t) -> p d t", d=2)
        E_c = C["E"][0:8, :].rearrange("p (d t) -> p d t", d=2)
        aT = C["aT"].rearrange("p (k d t h) -> p k d t h", k=2, d=2, t=TT)
        mixT_c = C["qk"].rearrange("p (c t) -> p c t", c=DC)

        def h_stats(o, part):
            heads = slice(0, EARLY) if part == 0 else slice(EARLY, HEADS)
            return C["st"][:, o:o + 2 * HEADS].rearrange("p (t h) -> p t h", t=TT)[:, :, heads]

        mlmask = lcst[:, C1_MASK:C1_SEL]
        sel_c = lcst[0:8, C1_SEL:C1_SIZE].rearrange("p (h n) -> p h n", h=HEADS)

        L3 = M["L"].rearrange("p (t n) -> p t n", t=TT)
        S_m = M["S"].rearrange("p (t e s) -> p t e s", t=TT, e=QUAD)
        Gs_m = M["Gs"].rearrange("p (t e s) -> p t e s", t=TT, e=QUAD)
        xT_m = M["xT"].rearrange("p (c s) -> p c s", c=DC)
        hT_m = M["hT"].rearrange("p (c s) -> p c s", c=FF // P)
        rk3 = M["rank"].rearrange("p (t e) -> p t e", t=TT)
        G3 = M["G"].rearrange("p (t e) -> p t e", t=TT)
        COMB = ((0, 0, 0), (1, 0, 1), (6, 1, 0), (7, 1, 1))

        block = ctx.enter_context(nc.Block())

        @block.sync
        def _(sp):
            sp.dma_start(x3[:, 0], a["x"][0, 0:P, :]).then_inc(s_load["x"], 16)
            sp.dma_start(cst[:, :], a["c_common"]).then_inc(s_load["cst"], 16)
            sp.dma_start(x3[:, 1], a["x"][0, P:2 * P, :]).then_inc(s_load["x"], 16)
            rows = a["od_h_gain"].rearrange("l (c p) -> (l c) p", p=P)
            sp.dma_start(g_rows[G_HEADS:G_HEADS + DC, :], rows).then_inc(s_load["gains"], 16)

            def slot_free(count, value):
                sp.wait_ge(count, value)
                sp.sem_inc(s_free, 1)

            def expert_piece(ph, l, i, j, q):
                at, done, _ = piece(ph, i, j)
                dst = at.rearrange("p (e n) -> p e n", e=QUAD)
                if j < GU_PIECES:
                    for k, name in enumerate(("moe_w_gate", "moe_w_up")):
                        src = a[name][l, bass.ds(q * QUAD, QUAD), j * P:(j + 1) * P, :]
                        sp.dma_start(dst[:, :, k * FF:(k + 1) * FF],
                                     src.rearrange("e p f -> p e f")).then_inc(done, 16)
                else:
                    k = j - GU_PIECES
                    for half in range(2):
                        src = a["moe_w_down"][l, bass.ds(q * QUAD + 2 * half, 2), k * P:(k + 1) * P, :]
                        sp.dma_start(dst[:, 2 * half:2 * half + 2, :],
                                     src.rearrange("e p f -> p e f")).then_inc(done, 16)

            def dense(ph, prev, extra):
                for j in range(n_a if ph == "A" else n_c):
                    if j >= SLOTS:
                        sp.wait_ge(used[ph], j - SLOTS + 1)
                    elif prev is not None:
                        sp.wait_ge(used[prev], extra * ITEM + (QUADS * ITEM - SLOTS + 1 + j))
                    dst = slot(first[ph] + j).rearrange("p (c n) -> p c n", c=DC)
                    if ph == "A" and j == 0:
                        half = DC // 2
                        sp.dma_start(dst[:, 0:half], dense_source(ph, j)[:, 0:half]).then_inc(s_half, 16)
                        sp.dma_start(dst[:, half:DC], dense_source(ph, j)[:, half:DC]).then_inc(
                            landed[ph][0], 16)
                        continue
                    sp.dma_start(dst, dense_source(ph, j)).then_inc(
                        landed[ph][(first[ph] + j) % SLOTS], 16)

            def moe(ph, l, prev, n_prev):
                for j in range(ITEM):
                    turn = ring_turn(0, j)
                    if turn is None:
                        if PLACES_0[j] == -1 - (EXTRA - 1):
                            if l == 0:
                                sp.wait_ge(s_qms, 1)
                        elif PLACES_0[j] == -1 - (EXTRA - 2):
                            sp.wait_ge(ms[l]["logits"], 1)
                        elif l == 0:
                            sp.wait_ge(s_o, HP)
                        else:
                            sp.wait_ge(s_hTa, DC)
                    elif turn < SLOTS:
                        sp.wait_ge(used[prev], n_prev - SLOTS + 1 + turn)
                    else:
                        sp.wait_ge(used[ph], turn - SLOTS + 1)
                    expert_piece(ph, l, 0, j, 0)
                held = {PLACES_0[j] % SLOTS: j for j in range(ITEM) if PLACES_0[j] >= 0}
                for j in range(ITEM):
                    n = (SLOTS + SLOTS + j - EXTRA) % SLOTS
                    sp.wait_ge(used[ph], held[n] + 1 if j < SLOTS else ITEM + j - SLOTS + 1)
                    expert_piece(ph, l, 1, j, 1)
                sp.wait_ge(ms[l]["rounds"], 1)
                extra = sp.value_load(extra_i[0:1, l:l + 1], min_val=0, max_val=QUADS * (MAX_ROUNDS - 1))
                with sp.Fori(2, extra + QUADS) as i:
                    q = sp.snap(i % QUADS)
                    for j in range(ITEM):
                        slot_free(used[ph], i * ITEM + (j - SLOTS + 1))
                        expert_piece(ph, l, i, j, q)
                return extra

            dense("A", None, 0)
            extra = moe("B", 0, "A", n_a)
            dense("C", "B", extra)
            extra = moe("D", 1, "C", n_c)
            for k, (_, t, nb) in enumerate(COMB):
                slot_free(ms[1]["added"], extra * 4 + (4 * QUADS - 4 + k + 1))
                sp.dma_start(out[0, t * P:(t + 1) * P, nb * 512:(nb + 1) * 512],
                             x3[:, t, nb * 512:(nb + 1) * 512]).then_inc(s_out, 16)
            sp.wait_ge(s_out, 64)

        @block.gpsimd
        def _(pool):
            def bcast(row, n):
                return row.rearrange("(o n) -> o n", o=1).broadcast_to([P, n])

            pool.wait_ge(s_load["x"], 32)
            for r in range(2):
                for k in range(BIAS_ROWS):
                    base = (k + 5 - r) * REL_C + (REL_C // 2 - (GRID_W - 1))
                    src = bass.AP(tensor=a["ev_rel_bias"].tensor, offset=base,
                                  ap=[[1, GRID_W], [REL_SIZE, HEADS], [1, GRID_W]])
                    pool.dma_start(bias_a[GRID_W * r:GRID_W * (r + 1), k], src).then_inc(s_load["bias"], 16)
            pool.wait_ge(s_load["bias"], 16 * 2 * BIAS_ROWS)
            pool.wait_ge(s_load["lc0"], 16)
            every = A["bias"].rearrange("p (n k) -> p n k", k=GRID_W)
            pool.tensor_tensor(every, every, namask.unsqueeze(1).broadcast_to([P, BIAS_ROWS * HEADS, GRID_W]),
                               ALU.add).then_inc(s_biasm, 1)
            route = w_route[:, :].rearrange("p (l c n) -> p l c n", l=2, c=DC)
            for l in range(2):
                pool.dma_start(route[:, l, :, 0:GROUPS],
                               a["moe_w_rg"][l].rearrange("(c p) n -> p c n", p=P)).then_inc(s_load["route"], 16)
                pool.dma_start(route[:, l, :, GROUPS:ROUTE],
                               a["moe_w_re"][l].rearrange("(c p) n -> p c n", p=P)).then_inc(s_load["route"], 16)
                pool.dma_start(b_route[:, l * ROUTE:l * ROUTE + GROUPS],
                               bcast(a["moe_b_rg"][l], GROUPS)).then_inc(s_load["route"], 16)
                pool.dma_start(b_route[:, l * ROUTE + GROUPS:(l + 1) * ROUTE],
                               bcast(a["moe_b_re"][l], EXPERTS)).then_inc(s_load["route"], 16)
            pool.dma_start(w_gates[:, :].rearrange("p (c n) -> p c n", c=DC),
                           a["od_w_in"][0, :, 3072:3104].rearrange("(c p) n -> p c n", p=P)).then_inc(s_load["gates"], 16)
            pool.dma_start(b_gates[:, :], bcast(a["od_gate_bias"][0], 32)).then_inc(s_load["gates"], 16)
            for h in range(HEADS):
                pool.wait_ge(s_rl, h + 1)
                pool.tensor_scalar(P_a[:, h % 4, 0], P_a[:, h % 4, 0],
                                   A["st"][:, 64 + 2 * h:65 + 2 * h], None, ALU.mult).then_inc(s_pn, 1)
            pool.wait_ge(used["A"], n_a)
            pool.dma_start(lcst[:, :], a["c_layer1"]).then_inc(s_load["lc1"], 16)
            for h in range(HEADS - 1):
                pool.wait_ge(s_hf, 4 * (h + 1))
                pool.tensor_tensor(h_c[:, :, h * ML_DV:(h + 1) * ML_DV], tmp_c[:, h % 2, 0], tmp_c[:, h % 2, 1],
                                   ALU.add).then_inc(s_hb, 1)

        @block.scalar
        def _(act):
            for g, rows in ((G_EV, a["ev_norm"]), (G_OD, a["od_norm"]), (G_MOE0, a["moe_norm"])):
                rows = rows.rearrange("l (c p) -> (l c) p", p=P)
                act.dma_start(g_rows[g:g + rows.shape[0], :], rows).then_inc(s_load["gains"], 16)

            def norm(n):
                if n == 0:
                    act.wait_ge(s_load["x"], 32)
                else:
                    act.wait_ge(s_x, n)
                sq = SQ_MOE if n % 2 else SQ_MIX
                for t in range(TT):
                    nc.scalar.activation(sq[:, t * D:(t + 1) * D], x3[:, t], ACT.Square,
                                         accum_out=small[:, 8 + t:9 + t]).then_inc(s_ssq, 1)
                if n % 2:
                    for p in (2, 3):
                        act.wait_ge(s_xTp, 4 * n + p + 1)
                        for k in range(2):
                            c = 2 * p + k
                            g = G_NORM[n] + c
                            nc.scalar.activation(xnT_of(n)[:, c, :], bank(p)[:, k * T:(k + 1) * T], ACT.Copy,
                                                 scale=g_cols[:, g:g + 1]).then_inc(s_xTa, 1)
                act.wait_ge(s_ms, n + 1)
                nc.scalar.activation(small[:, 12:14], small[:, 10:12], ACT.Sqrt).then_inc(s_rt, 1)
                act.wait_ge(s_rs, n + 1)

            def inv_rms(t):
                return small[:, 14 + t:15 + t]

            def moe(ph, l):
                s = ms[l]
                norm(2 * l + 1)
                for t in range(TT):
                    nc.scalar.activation(xs3[:, t], x3[:, t], ACT.Copy, scale=inv_rms(t)).then_inc(s["scaled"], 1)
                act.wait_ge(s["gsub"], 1)
                nc.scalar.activation(M["st"][:, 0:8], M["st"][:, 0:8], ACT.Exp).then_inc(s["gexp"], 1)
                act.wait_ge(s["esub"], 1)
                nc.scalar.activation(M["st"][:, 20:22], M["st"][:, 20:22], ACT.Exp).then_inc(s["eexp"], 1)

                def item(i):
                    n = i + 1 if isinstance(i, int) else act.snap(i + 1)
                    act.wait_ge(s["disp"], n)
                    for c in range(1, 5) if isinstance(i, int) else range(4):
                        g = G_NORM[2 * l + 1] + c
                        nc.scalar.activation(xT_m[:, c], bank(4)[:, c % 4 * P:(c % 4 + 1) * P], ACT.Copy,
                                             scale=g_cols[:, g:g + 1]).then_inc(s["dispc_a"], 1)
                    act.wait_ge(s["gtp"], n)
                    nc.scalar.copy(M["GT"], bank(6)[:, 0:T]).then_inc(s["gtc"], 1)
                    act.wait_ge(used[ph], i * ITEM + GU_PIECES)
                    nc.scalar.activation(M["sg"], bank(0), ACT.Silu).then_inc(s["silu"], 1)
                    act.wait_ge(s["hTp"], n)
                    nc.scalar.copy(M["hT"], bank(7)).then_inc(s["hTc"], 1)
                    act.wait_ge(used[ph], i * ITEM + ITEM)
                    nc.scalar.copy(M["y"][:, 0:512], bank(2)).then_inc(s["y_a"], 1)

                item(0)
                act.wait_ge(s["rounds"], 1)
                extra = act.value_load(extra_i[0:1, l:l + 1], min_val=0, max_val=QUADS * (MAX_ROUNDS - 1))
                with act.Fori(1, extra + QUADS) as i:
                    item(i)

            norm(0)
            for k, name in enumerate(("ev_q_gain", "ev_k_gain")):
                for half in range(2):
                    act.dma_start(small[64 * half:64 * half + 64, k:k + 1],
                                  a[name].rearrange("o d -> d o")).then_inc(s_load["qkgain"], 16)
            act.dma_start(lcst[:, :], a["c_layer0"]).then_inc(s_load["lc0"], 16)
            for b in range(4):
                act.wait_ge(used["A"], b + 1)
                nc.scalar.activation(u_a[:, 0, b * 512:(b + 1) * 512], mbank(2 * b), ACT.Copy,
                                     scale=inv_rms(0)).then_inc(s_ua["A"], 1)
                if b == 1:
                    act.wait_ge(s_ua["A"], 2)
                    act.wait_ge(s_uv["A"], 2)
                    nc.scalar.activation(SQ_MIX.rearrange("p (t n) -> p t n", t=TT), u_a[:, :, 0:1024],
                                         ACT.Square).then_inc(s_qsq, 1)
                    act.wait_ge(s_qms, 1)
                    nc.scalar.activation(A["st"][:, 0:32], A["st"][:, 0:32], ACT.Sqrt).then_inc(s_qrt, 1)

            def exp_scores(h):
                act.wait_ge(s_mx, h + 1)
                for t in range(TT):
                    nc.scalar.activation(P_a[:, h % 4, t], P_a[:, h % 4, t], ACT.Exp,
                                         bias=A["st"][:, 80 + 2 * h + t:81 + 2 * h + t],
                                         accum_out=A["st"][:, 100 + 2 * h + t:101 + 2 * h + t]).then_inc(s_ex, 1)

            def norm_probs(h):
                act.wait_ge(s_rl, h + 1)
                nc.scalar.activation(P_a[:, h % 4, 1], P_a[:, h % 4, 1], ACT.Copy,
                                     scale=A["st"][:, 65 + 2 * h:66 + 2 * h]).then_inc(s_pna, 1)

            for h in range(4):
                exp_scores(h)
                if h >= 1:
                    norm_probs(h - 1)
                act.wait_ge(s_f1, h + 1)
                nc.scalar.copy(AB[:, h], mbank(4 + h)).then_inc(s_f1c, 1)
            for c in range(4):
                act.wait_ge(s_f2, c + 1)
                nc.scalar.copy(mixT_a[:, 4 + c], mbank(4 + c)[:, 0:T]).then_inc(s_f2c, 1)
                if c == 0:
                    norm_probs(3)
            for h in range(4, HEADS):
                exp_scores(h)
                if h >= 5:
                    norm_probs(h - 1)
            norm_probs(HEADS - 1)

            moe("B", 0)

            norm(2)
            def copy_u(j):
                act.wait_ge(used["C"], j + 1)
                b = ORDER_C[j]
                src = mbank(BANK_C[j])
                if b < 2:
                    nc.scalar.activation(qk_c[:, 0, b * 512:(b + 1) * 512], src, ACT.Copy,
                                         scale=inv_rms(0)).then_inc(s_ua["C"], 1)
                elif b < 4:
                    nc.scalar.activation(ve[:, 0, 4 * (b - 2):4 * (b - 1), 0:ML_DV],
                                         src.rearrange("p (h e) -> p h e", h=4), ACT.Copy,
                                         scale=inv_rms(0)).then_inc(s_ua["C"], 1)
                else:
                    for t in range(TT):
                        nc.scalar.activation(og[:, t, (b - 4) * 512:(b - 3) * 512],
                                             mbank(BANK_C[j] + t), ACT.Sigmoid, scale=inv_rms(t)).then_inc(s_og, 1)

            copy_u(0)
            act.wait_ge(s_gab, 1)
            nc.scalar.activation(gw[:, 1], gw[:, 0], ACT.Exp, scale=-1.0).then_inc(s_gex, 1)
            act.wait_ge(s_gp1, 1)
            nc.scalar.activation(gw[:, 1], gw[:, 1], ACT.Ln).then_inc(s_gln, 1)
            copy_u(1)

            def decay_exp(h):
                act.wait_ge(s_dl, h + 1)
                nc.scalar.activation(W_c[h % 3], W_c[h % 3], ACT.Exp).then_inc(s_w, 1)

            def h_squares(h):
                act.wait_ge(s_hb, h + 1)
                for t in range(TT):
                    nc.scalar.activation(C["qk"][:, (2 * h + t) * P:(2 * h + t + 1) * P], h_c[:, t, h * ML_DV:(h + 1) * ML_DV],
                                         ACT.Square, accum_out=C["st"][:, 64 + 8 * t + h:65 + 8 * t + h]).then_inc(s_hsq, 1)

            act.wait_ge(s_em, 1)
            nc.scalar.activation(E_c, F_c, ACT.Exp).then_inc(s_eme, 1)
            for j in range(2, 5):
                copy_u(j)
            decay_exp(0)
            decay_exp(1)
            copy_u(5)
            decay_exp(2)

            def h_roots(part):
                act.wait_ge(s_hms, part + 1)
                ms_ = h_stats(80, part)
                nc.scalar.activation(ms_, ms_, ACT.Sqrt).then_inc(s_hrt, 1)

            for h in range(1, HEADS + 1):
                if h == HEADS:
                    h_roots(0)
                if h >= 1:
                    g = h - 1
                    act.wait_ge(s_rd, g + 1)
                    if g >= 2:
                        act.wait_ge(s_hb, g - 1)
                    for d in range(2):
                        for t in range(TT):
                            o = 4 * g + 2 * d + t
                            nc.scalar.activation(tmp_c[:, g % 2, d, t], mbank(4 + 2 * (g % 2) + d)[:, t * VE:t * VE + ML_DV],
                                                 ACT.Copy, scale=C["st"][:, o:o + 1]).then_inc(s_hf, 1)
                if h >= 2:
                    h_squares(h - 2)
                if h + 2 < HEADS:
                    decay_exp(h + 2)
            h_squares(HEADS - 1)
            h_roots(1)
            for p in range(4):
                act.wait_ge(s_hTp, p + 1)
                for k in range(2):
                    g = G_HEADS + 2 * p + k
                    nc.scalar.activation(mixT_c[:, 2 * p + k, :], bank(4 + p)[:, k * T:(k + 1) * T], ACT.Copy,
                                         scale=g_cols[:, g:g + 1]).then_inc(s_hTa, 1)

            moe("D", 1)

        @block.vector
        def _(dve):
            V = nc.vector
            chain = [0]

            def join(n):
                chain[0] += n
                dve.wait_ge(dvc, chain[0])

            def link(ins):
                ins.then_inc(dvc, 1)
                join(1)

            def norm(n):
                def copy_bank(p):
                    dve.wait_ge(s_xTp, 4 * n + p + 1)
                    for k in range(2):
                        c = 2 * p + k
                        g = G_NORM[n] + c
                        V.tensor_scalar(xnT_of(n)[:, c, :], bank(p)[:, k * T:(k + 1) * T], g_cols[:, g:g + 1],
                                        None, ALU.mult).then_inc(s_xTv, 1)

                copy_bank(0)
                copy_bank(1)
                dve.wait_ge(s_ssq, 2 * (n + 1))
                V.tensor_scalar(small[:, 10:12], small[:, 8:10], 1.0 / D, EPS, ALU.mult, ALU.add).then_inc(s_ms, 1)
                if n % 2 == 0:
                    copy_bank(2)
                    copy_bank(3)
                dve.wait_ge(s_rt, n + 1)
                V.reciprocal(small[:, 14:16], small[:, 12:14]).then_inc(s_rs, 1)
                dve.wait_ge(s_rs, n + 1)

            def inv_rms(t):
                return small[:, 14 + t:15 + t]

            def out_proj(ph, done, b0):
                for nb in range(2):
                    dve.wait_ge(used[ph], done + nb + 1)
                    for t in range(TT):
                        dst = x3[:, t, nb * 512:(nb + 1) * 512]
                        V.tensor_tensor(dst, dst, bank(b0 + 2 * nb + t), ALU.add).then_inc(dvc, 1)
                join(4)
                dve.sem_inc(s_x, 1)

            def moe(ph, l):
                s = ms[l]
                st = M["st"]
                norm(2 * l + 1)
                dve.wait_ge(s_load["route"], 128)
                dve.wait_ge(s["logits"], 1)
                for t in range(TT):
                    V.scalar_tensor_tensor(L3[:, t], bank(4 + t)[:, 0:ROUTE], inv_rms(t),
                                           b_route[:, l * ROUTE:(l + 1) * ROUTE], ALU.mult, ALU.add).then_inc(dvc, 1)
                join(2)
                lg = L3[:, :, 0:GROUPS]
                gm = st[:, 8:10]
                link(V.reduce_max(gm, lg, AX))
                gmb = gm.unsqueeze(2).broadcast_to([P, TT, GROUPS])
                ge = st[:, 0:8].rearrange("p (t g) -> p t g", t=TT)
                V.tensor_tensor(ge, lg, gmb, ALU.subtract).then_inc(s["gsub"], 1)
                w = [M["work"][:, j * 64:(j + 1) * 64] for j in range(8)]
                w4 = [v.rearrange("p (t g e) -> p t g e", t=TT, g=GROUPS) for v in w]
                w3 = [v.rearrange("p (t e) -> p t e", t=TT) for v in w]
                g1 = w[0][:, 0:8].rearrange("p (t g) -> p t g", t=TT)
                g2 = w[1][:, 0:8].rearrange("p (t g) -> p t g", t=TT)
                for t in range(TT):
                    V.scalar_tensor_tensor(g1[:, t], lg[:, t], gm[:, t:t + 1], rankw[:, 0:GROUPS],
                                           ALU.is_equal, ALU.mult).then_inc(dvc, 1)
                join(2)
                link(V.reduce_max(st[:, 10:12], g1, AX))
                for t in range(TT):
                    V.tensor_scalar(g2[:, t], g1[:, t], st[:, 10 + t:11 + t], NEG, ALU.is_lt, ALU.mult).then_inc(dvc, 1)
                join(2)
                for t in range(TT):
                    le = L3[:, t, GROUPS:ROUTE].rearrange("p (g e) -> p g e", g=GROUPS)
                    V.tensor_tensor(w4[2][:, t], le, g2[:, t].unsqueeze(2).broadcast_to([P, GROUPS, PER_GROUP]),
                                    ALU.add).then_inc(dvc, 1)
                join(2)
                oh = [M["oh"][:, j * 64:(j + 1) * 64].rearrange("p (t e) -> p t e", t=TT) for j in range(2)]
                m3 = M["mask"].rearrange("p (t e) -> p t e", t=TT)

                def top(src, vmax):
                    link(V.reduce_max(vmax, src, AX))
                    for t in range(TT):
                        V.scalar_tensor_tensor(w3[4][:, t], src[:, t], vmax[:, t:t + 1], rankw,
                                               ALU.is_equal, ALU.mult).then_inc(dvc, 1)
                    join(2)
                    link(V.reduce_max(st[:, 12:14], w3[4], AX))

                def one_hot(j):
                    for t in range(TT):
                        V.tensor_scalar(oh[j][:, t], w3[4][:, t], st[:, 12 + t:13 + t], None,
                                        ALU.is_equal).then_inc(dvc, 1)

                top(w3[2], st[:, 16:18])
                one_hot(0)
                join(2)
                link(V.scalar_tensor_tensor(w3[5], oh[0], NEG, w3[2], ALU.mult, ALU.add))
                top(w3[5], st[:, 18:20])
                for t in range(TT):
                    V.scalar_tensor_tensor(m3[:, t], w3[4][:, t], st[:, 12 + t:13 + t], oh[0][:, t],
                                           ALU.is_equal, ALU.add).then_inc(s["mask"], 1)
                one_hot(1)
                V.tensor_tensor(st[:, 20:22], st[:, 18:20], st[:, 16:18], ALU.subtract).then_inc(s["esub"], 1)
                join(2)
                dve.wait_ge(s["mask"], 2)
                link(V.tensor_scalar(w3[6], m3, 1e4, -1e4, ALU.mult, ALU.add))
                dve.wait_ge(s["rank"], 1)
                link(V.tensor_tensor(rk3, bank(5)[:, 0:64].rearrange("p (t e) -> p t e", t=TT), w3[6], ALU.add))

                def select(q4, first_slot):
                    sid = slotid[:, bass.ds(first_slot, CAP)].unsqueeze(1).broadcast_to([P, QUAD, CAP])
                    for t in range(TT):
                        V.tensor_tensor(S_m[:, t], rk3[:, t, bass.ds(q4, QUAD)].unsqueeze(2).broadcast_to([P, QUAD, CAP]),
                                        sid, ALU.is_equal).then_inc(s["sel"], 1)

                def select_gates(q4, count):
                    dve.wait_ge(s["sel"], count)
                    for t in range(TT):
                        V.tensor_tensor(Gs_m[:, t], S_m[:, t],
                                        G3[:, t, bass.ds(q4, QUAD)].unsqueeze(2).broadcast_to([P, QUAD, CAP]),
                                        ALU.mult).then_inc(s["sel"], 1)

                select(0, 0)
                dve.wait_ge(s["early"], 1)
                V.tensor_scalar(xT_m[:, 0], bank(2)[:, 0:P], g_cols[:, G_NORM[2 * l + 1]:G_NORM[2 * l + 1] + 1],
                                None, ALU.mult).then_inc(s["dispc_v"], 1)
                dve.wait_ge(s["gexp"], 1)
                link(V.reduce_sum(st[:, 22:24], ge, AX))
                dve.wait_ge(s["eexp"], 1)
                link(V.tensor_scalar(st[:, 24:26], st[:, 20:22], 1.0, None, ALU.add))
                link(V.tensor_tensor(st[:, 24:26], st[:, 24:26], st[:, 22:24], ALU.mult))
                link(V.reciprocal(st[:, 26:28], st[:, 24:26]))
                link(V.tensor_tensor(st[:, 28:30], st[:, 26:28], st[:, 20:22], ALU.mult))
                V.tensor_tensor(w3[6], oh[0], st[:, 26:28].unsqueeze(2).broadcast_to([P, TT, EXPERTS]), ALU.mult).then_inc(dvc, 1)
                V.tensor_tensor(w3[7], oh[1], st[:, 28:30].unsqueeze(2).broadcast_to([P, TT, EXPERTS]), ALU.mult).then_inc(dvc, 1)
                join(2)
                link(V.tensor_tensor(G3, w3[6], w3[7], ALU.add))
                select_gates(0, 2)
                dve.wait_ge(s["count"], 1)
                link(V.reduce_max(st[:, 30:31], bank(3)[:, 0:32], AX))
                link(V.tensor_tensor(st[:, 32:40], thr, st[:, 30:31].broadcast_to([P, MAX_ROUNDS]), ALU.is_lt))
                link(V.reduce_sum(st[:, 31:32], st[:, 32:40], AX))
                V.tensor_scalar(extra_i[:, l:l + 1], st[:, 31:32], float(QUADS), None, ALU.mult).then_inc(s["rounds"], 1)

                def item(i):
                    loop = not isinstance(i, int)
                    n = dve.snap(i + 1) if loop else i + 1
                    dve.wait_ge(s["disp"], n)
                    for c in range(4 if loop else 5, DC):
                        g = G_NORM[2 * l + 1] + c
                        V.tensor_scalar(xT_m[:, c], bank(5)[:, (c - 4) * P:(c - 3) * P], g_cols[:, g:g + 1],
                                        None, ALU.mult).then_inc(s["dispc_v"], 1)
                    dve.wait_ge(s["gtp"], n)
                    q4 = dve.snap((n % QUADS) * QUAD) if loop else (n % QUADS) * QUAD
                    fs = dve.snap((n // QUADS) * CAP) if loop else (n // QUADS) * CAP
                    select(q4, fs)
                    select_gates(q4, i * 4 + 6)
                    dve.wait_ge(s["silu"], n)
                    V.tensor_tensor(M["h"], bank(1), M["sg"], ALU.mult).then_inc(s["h"], 1)
                    dve.wait_ge(used[ph], i * ITEM + ITEM)
                    V.tensor_copy(M["y"][:, 512:1024], bank(3)).then_inc(s["y_v"], 1)
                    for k, (b, t, nb) in enumerate(COMB):
                        dve.wait_ge(s["comb"], i * 4 + (k + 1))
                        dst = x3[:, t, nb * 512:(nb + 1) * 512]
                        V.tensor_tensor(dst, dst, bank(b), ALU.add).then_inc(s["added"], 1)

                item(0)
                dve.wait_ge(s["rounds"], 1)
                extra = dve.value_load(extra_i[0:1, l:l + 1], min_val=0, max_val=QUADS * (MAX_ROUNDS - 1))
                with dve.Fori(1, extra + QUADS) as i:
                    item(i)
                dve.wait_ge(s["added"], extra * 4 + QUADS * 4)
                dve.sem_inc(s_x, 1)

            dve.wait_ge(s_gr, 1)
            V.tensor_copy(g_cols[:, :], mbank(3)[:, 0:G_ROWS]).then_inc(s_gc, 1)
            dve.wait_ge(s_gc, 1)
            norm(0)
            st = A["st"]
            for b in range(4):
                dve.wait_ge(used["A"], b + 1)
                V.tensor_scalar(u_a[:, 1, b * 512:(b + 1) * 512], mbank(2 * b + 1), inv_rms(1), None,
                                ALU.mult).then_inc(s_uv["A"], 1)
                if b == 1:
                    dve.wait_ge(s_qsq, 1)
                    link(V.reduce_sum(st[:, 32:64], SQ_MIX.rearrange("p (g d) -> p g d", d=NA_DH), AX))
                    V.tensor_scalar(st[:, 0:32], st[:, 32:64], 1.0 / NA_DH, EPS, ALU.mult, ALU.add).then_inc(s_qms, 1)
                    dve.wait_ge(s_qrt, 1)
                    link(V.reciprocal(st[:, 32:64], st[:, 0:32]))
                    dve.wait_ge(s_ua["A"], 2)
                    for t in range(TT):
                        qk = u_a[:, t, 0:1024].rearrange("p (g d) -> p g d", d=NA_DH)
                        rs = st[:, 32 + 16 * t:48 + 16 * t].unsqueeze(2).broadcast_to([P, 16, NA_DH])
                        V.tensor_tensor(qk, qk, rs, ALU.mult).then_inc(s_qn, 1)
                    dve.wait_ge(s_load["qkgain"], 64)
                if b == 2:
                    for p in range(4):
                        dve.wait_ge(s_qTp["A"], p + 1)
                        dst = qkT_a[:, 2 * p:2 * p + 2, :].rearrange("p c (r j) -> p (c r) j", j=GRID_W)
                        src = mbank(p).rearrange("p (g j) -> p g j", j=GRID_W)
                        if p < 2:
                            V.tensor_scalar(dst[:, :, ::-1], src, small[:, 0:1], NA_DH ** -0.5,
                                            ALU.mult, ALU.mult).then_inc(s_qT["A"], 1)
                        else:
                            V.tensor_scalar(dst, src, small[:, 1:2], None, ALU.mult).then_inc(s_qT["A"], 1)
            dve.wait_ge(s_biasm, 1)

            def row_max(h):
                dve.wait_ge(s_sc, h // 2 + 1)
                if h >= 4:
                    dve.wait_ge(s_pT, h - 3)
                for t in range(TT):
                    V.tensor_tensor(P_a[:, h % 4, t].rearrange("p (r k) -> p r k", k=GRID_W),
                                    mbank(h % 4)[:, t * T:(t + 1) * T].rearrange("p (r k) -> p r k", k=GRID_W),
                                    bias_a[:, 2 - 2 * t:6 - 2 * t, h, :], ALU.add).then_inc(dvc, 1)
                join(2)
                link(V.reduce_max(st[:, 116 + 2 * h:118 + 2 * h], P_a[:, h % 4], AX))
                V.tensor_scalar(st[:, 80 + 2 * h:82 + 2 * h], st[:, 116 + 2 * h:118 + 2 * h], -1.0, None,
                                ALU.mult).then_inc(s_mx, 1)

            def inv_sum(h):
                dve.wait_ge(s_ex, 2 * (h + 1))
                V.reciprocal(st[:, 64 + 2 * h:66 + 2 * h], st[:, 100 + 2 * h:102 + 2 * h]).then_inc(s_rl, 1)

            row_max(0)
            row_max(1)
            inv_sum(0)
            row_max(2)
            inv_sum(1)
            row_max(3)
            inv_sum(2)
            inv_sum(3)

            def copy_o(hp):
                dve.wait_ge(s_pv, hp + 1)
                V.tensor_copy(mixT_a[:, hp], mbank(6 + hp % 2)[:, 0:T]).then_inc(s_o, 1)

            for h in range(HEADS):
                dve.wait_ge(s_pT, h + 1)
                if h >= 4:
                    dve.wait_ge(s_pv, h // 2 - 1)
                V.tensor_copy(PT_a[:, h % 4].rearrange("p (g j) -> p g j", j=GRID_W)[:, :, ::-1],
                              mbank(4 + h % 2).rearrange("p (g j) -> p g j", j=GRID_W)).then_inc(s_pTc, 1)
                if h >= 4 and h % 2 == 0:
                    copy_o(h // 2 - 2)
                if 1 <= h and h + 3 < HEADS:
                    inv_sum(h + 3)
                if h + 4 < HEADS:
                    row_max(h + 4)
            copy_o(HP - 2)
            copy_o(HP - 1)
            out_proj("A", 4, 4)

            moe("B", 0)

            norm(2)
            st = C["st"]
            def copy_u(j):
                dve.wait_ge(used["C"], j + 1)
                b = ORDER_C[j]
                src = mbank(BANK_C[j] + 1)
                if b < 2:
                    V.tensor_scalar(qk_c[:, 1, b * 512:(b + 1) * 512], src, inv_rms(1), None,
                                    ALU.mult).then_inc(s_uv["C"], 1)
                else:
                    V.tensor_scalar(ve[:, 1, 4 * (b - 2):4 * (b - 1), 0:ML_DV],
                                    src.rearrange("p (h e) -> p h e", h=4), inv_rms(1), None,
                                    ALU.mult).then_inc(s_uv["C"], 1)

            copy_u(0)
            dve.wait_ge(s_gt, 1)
            dve.wait_ge(s_load["gates"], 32)
            for t in range(TT):
                V.scalar_tensor_tensor(gtok[:, t], mbank(7)[:, t * 32:(t + 1) * 32], inv_rms(t), b_gates[:, :],
                                       ALU.mult, ALU.add).then_inc(dvc, 1)
            join(2)
            f4 = gtok.rearrange("p t (d k h) -> p t d k h", d=2, k=2)
            for t in range(TT):
                f = f4[:, t, :, 1, :]
                V.scalar_tensor_tensor(gw[:, 0, t], f, -1.0, f, ALU.mult, ALU.max).then_inc(dvc, 1)
                V.tensor_scalar(gw[:, 2, t], f, 0.0, None, ALU.min).then_inc(dvc, 1)
            join(4)
            dve.sem_inc(s_gab, 1)
            V.memset(ve[:, :, :, ML_DV:VE], 1.0).then_inc(s_gtk, 1)
            dve.wait_ge(s_gex, 1)
            V.tensor_scalar(gw[:, 1], gw[:, 1], 1.0, None, ALU.add).then_inc(s_gp1, 1)
            dve.wait_ge(s_gln, 1)
            for t in range(TT):
                V.tensor_tensor(f4[:, t, :, 1, :], gw[:, 2, t], gw[:, 1, t], ALU.subtract).then_inc(s_gtk, 1)

            copy_u(1)
            dve.wait_ge(s_gTp, 2)
            for k in range(2):
                V.tensor_copy(gT[:, 2 * k:2 * k + 2], mbank(6 + k)[0:8, :].rearrange("p (j t) -> p j t", j=2)).then_inc(s_gTc, 1)
            dve.wait_ge(s_gTc, 2)
            one8 = ones[0:8, 0:1].broadcast_to([8, T])

            def way(ap, d):
                return ap[:, d, :] if d == 0 else ap[:, d, ::-1]

            gTi = gT.rearrange("p (d k) t -> p d k t", k=2)
            for d in range(2):
                lf = gTi[:, d, 1, :] if d == 0 else gTi[:, d, 1, ::-1]
                V.tensor_tensor_scan(way(F_c, d), one8, lf, 0.0, ALU.mult, ALU.add).then_inc(dvc, 1)
            join(2)
            link(V.tensor_tensor(a_c, gTi[:, :, 0, :], F_c, ALU.subtract))
            for d in range(2):
                V.tensor_tensor_scan(way(nM, d), one8, way(a_c, d), 0.0, ALU.mult, ALU.max).then_inc(dvc, 1)
            join(2)
            link(V.tensor_scalar(nM, nM, -1.0, None, ALU.mult))
            V.tensor_tensor(F_c, nM, F_c, ALU.subtract).then_inc(s_em, 1)
            dve.wait_ge(s_aTp, 1)
            V.tensor_copy(C["aT"], mbank(6)[:, 0:64]).then_inc(s_aT, 1)
            for p in range(4):
                dve.wait_ge(s_qTp["C"], p + 1)
                V.tensor_scalar(qkT_c[:, 2 * p:2 * p + 2, :], mbank(p).rearrange("p (c t) -> p c t", c=2),
                                1.0 if p < 2 else 64 ** -0.5, None, ALU.mult).then_inc(s_qT["C"], 1)
            dve.wait_ge(s_aT, 1)
            copy_u(4)
            SEG = ((0, 0, 0, 0, T), (T, 1, 1, 0, T), (2 * T, 1, 0, 0, P), (2 * T + P, 0, 1, P, P))

            def decay(h):
                dve.wait_ge(s_bc, h + 1)
                if h >= 3:
                    dve.wait_ge(s_nu, h - 2)
                for o, d, stile, t0, n in SEG:
                    ins = V.scalar_tensor_tensor(W_c[h % 3][:, o:o + n], mbank(2 + h % 2)[:, d * T + t0:d * T + t0 + n],
                                                 aT[:, 0, d, stile, h:h + 1], mlmask[:, o:o + n], ALU.add, ALU.min)
                    ins.then_inc(dvc, 1)
                join(4)
                dve.sem_inc(s_dl, 1)

            def weigh(h):
                dve.wait_ge(s_w, h + 1)
                dve.wait_ge(s_st, h + 1)
                w = W_c[h % 3]
                sc = mbank(h % 2)
                V.tensor_tensor(w[:, 0:2 * T], w[:, 0:2 * T], sc, ALU.mult).then_inc(s_ws, 1)
                diag = bass.AP(tensor=sc.tensor, offset=sc.offset, ap=[list(sc.ap[0]), [T + P, 2], [1, P]])
                V.tensor_tensor(w[:, 2 * T:3 * T].rearrange("p (j n) -> p j n", j=2),
                                w[:, 2 * T:3 * T].rearrange("p (j n) -> p j n", j=2), diag, ALU.mult).then_inc(s_ws, 1)

            def inv_den(h):
                dve.wait_ge(s_nu, h + 1)
                b = 4 + 2 * (h % 2)
                rd = st[:, 4 * h:4 * h + 4].rearrange("p (d t) -> p d t", d=2)
                den = psum[:, b % 4:b % 4 + 2, ML_DV:2 * VE:VE]
                link(V.scalar_tensor_tensor(rd, den, -1.0, aT[:, 1, :, :, h], ALU.mult, ALU.max))
                link(V.tensor_tensor(rd, den, rd, ALU.max))
                V.reciprocal(st[:, 4 * h:4 * h + 4], st[:, 4 * h:4 * h + 4]).then_inc(s_rd, 1)

            def both_ways(h):
                dve.wait_ge(s_hf, 4 * (h + 1))
                dve.wait_ge(s_hb, h)
                V.tensor_tensor(h_c[:, :, h * ML_DV:(h + 1) * ML_DV], tmp_c[:, h % 2, 0], tmp_c[:, h % 2, 1],
                                ALU.add).then_inc(s_hb, 1)

            def h_mean_squares(part):
                dve.wait_ge(s_hsq, 2 * (EARLY if part == 0 else HEADS))
                V.tensor_scalar(h_stats(80, part), h_stats(64, part), 1.0 / ML_DV, EPS,
                                ALU.mult, ALU.add).then_inc(s_hms, 1)

            def h_inv_roots(part):
                dve.wait_ge(s_hrt, part + 1)
                link(V.reciprocal(h_stats(64, part), h_stats(80, part)))

            decay(0)
            decay(1)
            weigh(0)
            weigh(1)
            copy_u(5)
            decay(2)
            for h in range(HEADS):
                if 1 <= h < HEADS - 1:
                    weigh(h + 1)
                inv_den(h)
                if h + 3 < HEADS:
                    decay(h + 3)
                if h == EARLY:
                    h_mean_squares(0)
            both_ways(HEADS - 1)
            for p in range(HP):
                if p == 0:
                    h_inv_roots(0)
                if p == 1:
                    h_mean_squares(1)
                if 2 * p == EARLY:
                    h_inv_roots(1)
                for h in (2 * p, 2 * p + 1):
                    for t in range(TT):
                        o = slice(h * ML_DV, (h + 1) * ML_DV)
                        V.scalar_tensor_tensor(h_c[:, t, o], h_c[:, t, o], st[:, 64 + 8 * t + h:65 + 8 * t + h],
                                               og[:, t, o], ALU.mult, ALU.mult).then_inc(s_hn, 1)
            out_proj("C", 6, 0)

            moe("D", 1)

        @block.tensor
        def _(pe):
            def mm(out_, lhsT, rhs, start=True, stop=True):
                return nc.tensor.matmul(out_, lhsT, rhs, start=start, stop=stop)

            def two_chunks_T(to, p, src):
                for c in range(2):
                    for t in range(TT):
                        k = 2 * p + c
                        last = nc.tensor.transpose(to[:, (2 * c + t) * P:(2 * c + t + 1) * P],
                                                   src[:, t, k * P:(k + 1) * P], ident)
                return last

            def x_T(n):
                if n == 0:
                    pe.wait_ge(s_load["x"], 32)
                else:
                    pe.wait_ge(s_x, n)
                for p in range(4):
                    two_chunks_T(bank(p), p, x3).then_inc(s_xTp, 1)

            def dense_block(ph, j, lhs, b0, chunk0=None, chunk_sem=s_xTv):
                halves = ph == "A" and j == 0
                pe.wait_ge(*((s_half, 16) if halves else
                             (landed[ph][(first[ph] + j) % SLOTS], 16 * (j // SLOTS + 1))))
                w = slot(first[ph] + j).rearrange("p (c n) -> p c n", c=DC)
                for t in range(TT):
                    for c in range(DC):
                        if t == 0 and chunk0 is not None:
                            pe.wait_ge(chunk_sem, chunk0 + c + 1)
                        if halves and t == 0 and c == DC // 2:
                            pe.wait_ge(landed["A"][0], 16)
                        last = mm(bank(b0 + t), lhs[:, c, t * P:(t + 1) * P], w[:, c, :], c == 0, c == DC - 1)
                last.then_inc(used[ph], 1)

            def moe(ph, l):
                s = ms[l]
                x_T(2 * l + 1)
                pe.wait_ge(s_load["route"], 128)
                route = w_route[:, :].rearrange("p (l c n) -> p l c n", l=2, c=DC)
                for c in range(DC):
                    if c < DC // 2:
                        pe.wait_ge(s_xTv, (l + 1) * DC + l * DC // 2 + c + 1)
                    else:
                        pe.wait_ge(s_xTa, l * DC // 2 + c - DC // 2 + 1)
                    for t in range(TT):
                        last = mm(bank(4 + t)[:, 0:ROUTE], xnT_of(1)[:, c, t * P:(t + 1) * P],
                                  route[:, l, c, :], c == 0, c == DC - 1)
                last.then_inc(s["logits"], 1)
                for _ in range(WARM):
                    mm(bank(6), ident, x[:, 0:512])
                pe.wait_ge(s["mask"], 2)
                m3 = M["mask"].rearrange("p (t e) -> p t e", t=TT)
                mm(bank(5)[:, 0:32], tri, m3[:, 0])
                mm(bank(5)[:, 32:64], ones, m3[:, 0], True, False)
                mm(bank(5)[:, 32:64], tri, m3[:, 1], False, True).then_inc(s["rank"], 1)
                mm(bank(3)[:, 0:32], ones, m3[:, 0], True, False)
                mm(bank(3)[:, 0:32], ones, m3[:, 1], False, True).then_inc(s["count"], 1)

                def item(i):
                    loop = not isinstance(i, int)
                    n = pe.snap(i + 1) if loop else i + 1
                    pe.wait_ge(s["sel"], i * 4 + 2)
                    if not loop:
                        pe.wait_ge(s["scaled"], 2)
                    def gather(c, to):
                        for t in range(TT):
                            last = mm(to, xs3[:, t, c * P:(c + 1) * P], M["S"][:, t * P:(t + 1) * P], t == 0, t == TT - 1)
                        return last

                    def multiply(j):
                        at, there, value = piece(ph, i, j)
                        pe.wait_ge(there, value)
                        w = at.rearrange("p (e n) -> p e n", e=QUAD)
                        down = j >= GU_PIECES
                        k = j - GU_PIECES if down else j
                        lhs = hT_m if down else xT_m
                        for half in range(2):
                            for e in range(QUAD):
                                last = mm(psum[e * CAP:(e + 1) * CAP, 2 * down + half, :],
                                          lhs[:, k, e * CAP:(e + 1) * CAP],
                                          w[:, e, half * 512:(half + 1) * 512],
                                          k == 0, k == (DN_PIECES if down else GU_PIECES) - 1)
                        last.then_inc(used[ph], 1)

                    if not loop:
                        gather(0, bank(2)[:, 0:P]).then_inc(s["early"], 1)
                        pe.wait_ge(s["dispc_v"], 1)
                        multiply(0)
                    for c in range(0 if loop else 1, DC):
                        b = 4 + c // 4 if loop or c != 4 else 4
                        last = gather(c, bank(b)[:, (c % 4) * P:(c % 4 + 1) * P])
                    last.then_inc(s["disp"], 1)
                    pe.wait_ge(s["dispc_a"], i * 4 + 4)
                    pe.wait_ge(s["dispc_v"], i * 4 + 4)
                    if loop:
                        pe.wait_ge(s["added"], i * 4)
                    for j in range(0 if loop else 1, ITEM):
                        if j == GU_PIECES // 2:
                            pe.wait_ge(s["sel"], i * 4 + 4)
                            for t in range(TT):
                                last = nc.tensor.transpose(bank(6)[:, t * P:(t + 1) * P], M["Gs"][:, t * P:(t + 1) * P], ident)
                            last.then_inc(s["gtp"], 1)
                        if j == GU_PIECES:
                            pe.wait_ge(s["h"], n)
                            for k in range(FF // P):
                                last = nc.tensor.transpose(bank(7)[:, k * P:(k + 1) * P], M["h"][:, k * P:(k + 1) * P], ident)
                            last.then_inc(s["hTp"], 1)
                            pe.wait_ge(s["hTc"], n)
                        multiply(j)
                    pe.wait_ge(s["gtc"], n)
                    pe.wait_ge(s["y_a"], n)
                    pe.wait_ge(s["y_v"], n)
                    for b, t, nb in COMB:
                        mm(bank(b), M["GT"][:, t * P:(t + 1) * P], M["y"][:, nb * 512:(nb + 1) * 512]).then_inc(s["comb"], 1)

                item(0)
                extra = pe.value_load(extra_i[0:1, l:l + 1], min_val=0, max_val=QUADS * (MAX_ROUNDS - 1))
                with pe.Fori(1, extra + QUADS) as i:
                    item(i)

            pe.wait_ge(s_load["cst"], 16)
            pe.wait_ge(s_load["gains"], 64)
            nc.tensor.transpose(mbank(3)[:, 0:G_ROWS], g_rows[0:G_ROWS, :], ident[0:G_ROWS, 0:G_ROWS]).then_inc(s_gr, 1)
            x_T(0)
            dense_block("A", 0, xnT3, 4, 0)
            dense_block("A", 1, xnT3, 6)
            pe.wait_ge(s_gc, 1)
            pe.wait_ge(s_xTv, DC)
            dense_block("A", 2, xnT3, 0)
            pe.wait_ge(s_qn, 2)
            for p in range(4):
                two_chunks_T(mbank(p), p, u_a).then_inc(s_qTp["A"], 1)
            dense_block("A", 3, xnT3, 2)
            pe.wait_ge(s_qT["A"], 4)

            def scores(hp):
                if hp == 1:
                    pe.wait_ge(s_ua["A"], 4)
                    pe.wait_ge(s_uv["A"], 4)
                if hp >= 2:
                    pe.wait_ge(s_mx, 2 * hp - 2)
                for t in range(TT):
                    for h in (2 * hp, 2 * hp + 1):
                        r = slice(64 * (h % 2), 64 * (h % 2) + 64)
                        last = mm(mbank(h % 4)[:, t * T:(t + 1) * T], qkT_a[r, hp, t * P:(t + 1) * P],
                                  qkT_a[r, 4 + hp, :])
                last.then_inc(s_sc, 1)

            scores(0)
            scores(1)
            pe.wait_ge(s_load["lc0"], 16)
            for c in range(4):
                for t in range(TT):
                    last = mm(mbank(4 + c), u_a[:, t, 1536 + c * P:1536 + (c + 1) * P], seqdft[:, t, :], t == 0, t == 1)
                last.then_inc(s_f1, 1)
            scores(2)
            for c in range(4):
                pe.wait_ge(s_f1c, c + 1)
                mm(mbank(4 + c)[:, 0:T], chdft[:, 0, :], AB[:, c, 0:T], True, False)
                mm(mbank(4 + c)[:, 0:T], chdft[:, 1, :], AB[:, c, T:2 * T], False, True).then_inc(s_f2, 1)

            def times_v(hp):
                pe.wait_ge(s_pTc, 2 * hp + 2)
                if hp >= 2:
                    pe.wait_ge(s_o, hp - 1)
                for kt in range(TT):
                    for h in (2 * hp, 2 * hp + 1):
                        o = 64 * (h % 2)
                        last = mm(mbank(6 + hp % 2)[o:o + 64, 0:T], u_a[:, kt, 1024 + 64 * h:1024 + 64 * (h + 1)],
                                  PT_a[:, h % 4, kt * T:(kt + 1) * T], kt == 0, kt == TT - 1)
                last.then_inc(s_pv, 1)

            for h in range(HEADS):
                pe.wait_ge(s_pn, h + 1)
                pe.wait_ge(s_pna, h + 1)
                if h < 2:
                    pe.wait_ge(s_f2c, h + 1)
                if h >= 2:
                    pe.wait_ge(s_pTc, h - 1)
                for kt in range(TT):
                    for qt in range(TT):
                        last = nc.tensor.transpose(mbank(4 + h % 2)[:, kt * T + qt * P:kt * T + (qt + 1) * P],
                                                   P_a[:, h % 4, qt, kt * P:(kt + 1) * P], ident)
                last.then_inc(s_pT, 1)
                if h == 1:
                    scores(3)
                    pe.wait_ge(s_f2c, 4)
                if h % 2 == 0 and h >= 2:
                    times_v(h // 2 - 1)
            times_v(HP - 1)
            pe.wait_ge(s_o, HP)
            for nb in range(2):
                dense_block("A", 4 + nb, mixT_a, 4 + 2 * nb)

            moe("B", 0)

            x_T(2)
            pe.wait_ge(s_load["gates"], 32)
            wg = w_gates[:, :].rearrange("p (c n) -> p c n", c=DC)
            dense_block("C", 0, xnT3, 4, DC + DC // 2)
            for t in range(TT):
                for c in range(DC):
                    last = mm(mbank(7)[:, t * 32:(t + 1) * 32], xnT3[:, c, t * P:(t + 1) * P], wg[:, c, :], c == 0, c == DC - 1)
            last.then_inc(s_gt, 1)
            dense_block("C", 1, xnT3, 6)
            pe.wait_ge(s_gtk, 3)
            for j in range(4):
                for t in range(TT):
                    last = nc.tensor.transpose(mbank(6 + j // 2)[0:8, (j % 2) * T + t * P:(j % 2) * T + (t + 1) * P],
                                               gtok[:, t, 8 * j:8 * j + 8], ident)
                if j % 2:
                    last.then_inc(s_gTp, 1)
            dense_block("C", 2, xnT3, 0)
            pe.wait_ge(s_gTc, 2)
            pe.wait_ge(s_eme, 1)
            for k, src in enumerate((a_c, E_c)):
                for d in range(2):
                    for t in range(TT):
                        o = ((k * 2 + d) * TT + t) * 8
                        last = nc.tensor.transpose(mbank(6)[:, o:o + 8], src[:, d, t * P:(t + 1) * P], ident[0:8, 0:8])
            last.then_inc(s_aTp, 1)
            pe.wait_ge(s_aT, 1)
            dense_block("C", 3, xnT3, 2)
            pe.wait_ge(s_ua["C"], 2)
            pe.wait_ge(s_uv["C"], 2)
            for p in range(4):
                two_chunks_T(mbank(p), p, qk_c).then_inc(s_qTp["C"], 1)
            pe.wait_ge(s_og, 2)
            dense_block("C", 4, xnT3, 0)
            pe.wait_ge(s_qT["C"], 4)
            pe.wait_ge(s_load["lc1"], 16)

            def ml_scores(h):
                if h >= 2:
                    pe.wait_ge(s_ws, 2 * (h - 1))
                r = slice(64 * (h % 2), 64 * (h % 2) + 64)
                for st_ in range(TT):
                    last = mm(mbank(h % 2)[:, st_ * T:(st_ + 1) * T], qkT_c[r, 4 + h // 2, st_ * P:(st_ + 1) * P],
                              qkT_c[r, h // 2, :])
                last.then_inc(s_st, 1)

            def m_on_all(h):
                if h >= 2:
                    pe.wait_ge(s_dl, h - 1)
                mm(mbank(2 + h % 2), sel_c[:, h, :], C["nM"][0:8, :]).then_inc(s_bc, 1)

            for h in range(2):
                ml_scores(h)
                m_on_all(h)
            pe.wait_ge(s_og, 4)
            dense_block("C", 5, xnT3, 2)
            m_on_all(2)
            for h in range(HEADS):
                pe.wait_ge(s_ws, 2 * (h + 1))
                if h < 2:
                    pe.wait_ge(s_ua["C"], 3 + h)
                    pe.wait_ge(s_uv["C"], 3 + h)
                else:
                    pe.wait_ge(s_hf, 4 * (h - 1))
                w = W_c[h % 3]
                fb, bb = mbank(4 + 2 * (h % 2)), mbank(5 + 2 * (h % 2))
                v = [ve[:, t, h, :] for t in range(TT)]
                mm(fb[:, 0:VE], w[:, 0:P], v[0])
                mm(fb[:, VE:2 * VE], w[:, P:T], v[0], True, False)
                mm(fb[:, VE:2 * VE], w[:, 2 * T + P:3 * T], v[1], False, True)
                mm(bb[:, 0:VE], w[:, 2 * T:2 * T + P], v[0], True, False)
                mm(bb[:, 0:VE], w[:, T:T + P], v[1], False, True)
                mm(bb[:, VE:2 * VE], w[:, T + P:2 * T], v[1]).then_inc(s_nu, 1)
                if h + 2 < HEADS:
                    ml_scores(h + 2)
                if h + 3 < HEADS:
                    m_on_all(h + 3)
            for p in range(4):
                pe.wait_ge(s_hn, 4 * (p + 1))
                two_chunks_T(bank(4 + p), p, h_c).then_inc(s_hTp, 1)
            for nb in range(2):
                dense_block("C", 6 + nb, mixT_c, 2 * nb, 0 if nb == 0 else None, s_hTa)

            moe("D", 1)


_INS = ['x', 'ev_norm', 'ev_w_in', 'ev_q_gain', 'ev_k_gain', 'ev_rel_bias', 'ev_w_out',
        'od_norm', 'od_w_in', 'od_gate_bias', 'od_h_gain', 'od_w_out',
        'moe_norm', 'moe_w_rg', 'moe_b_rg', 'moe_w_re', 'moe_b_re', 'moe_w_gate', 'moe_w_up', 'moe_w_down']


def kernel(**inputs):
    import numpy as _np
    import concourse.bacc as _bacc
    from concourse import mybir as _mybir
    from concourse.bass_utils import run_bass_kernel_spmd as _run

    nc = _bacc.Bacc("TRN2", target_bir_lowering=False, num_devices=1)
    arrays, args = {}, {}
    given = {name: _np.ascontiguousarray(inputs[name]) for name in _INS}
    given.update(zip(("c_common", "c_layer0", "c_layer1"), shape_constants()))
    for name, arr in given.items():
        arrays[f"in_{name}"] = arr
        args[name] = nc.dram_tensor(f"in_{name}", arr.shape, _mybir.dt.from_np(arr.dtype), kind="ExternalInput").ap()
    out = nc.dram_tensor("out_0", (1, T, D), _mybir.dt.float32, kind="ExternalOutput").ap()
    build(nc, args, out)
    r = _run(nc, [arrays], core_ids=[0])
    return r.results[0]["out_0"]
```
